# Optimizing a Trainium2 kernel written in Bass

```python
import math
import jax, jax.numpy as jnp
from jax import lax
import numpy as np
import jax
import jax.numpy as jnp

D_MODEL = 1024
BATCH = 1
SEQ = 512
DEPTH = 1

PLE_DIM = 256
D_RG = D_MODEL // 2
RG_BLOCKS = 8
RG_BLOCK = D_RG // RG_BLOCKS
CONV_WIDTH = 4
RG_C = 8.0
D_HG = D_MODEL // 2
HG_HEAD_DIM = 128
HG_HEADS = D_HG // HG_HEAD_DIM
HG_CHUNK = 64
D_MIX = D_RG + D_HG
D_IN = 2 * D_RG + 4 * D_HG
EPS = 1e-6


def rms_norm(x, w):
    xf = x.astype(jnp.float32)
    y = xf * lax.rsqrt(jnp.mean(xf * xf, axis=-1, keepdims=True) + EPS)
    return (y * w.astype(jnp.float32)).astype(x.dtype)

def causal_depthwise_conv(x, w, b):
    T = x.shape[1]
    xp = jnp.pad(x, ((0, 0), (CONV_WIDTH - 1, 0), (0, 0)))
    y = b
    for j in range(CONV_WIDTH):
        y = y + xp[:, j:j + T] * w[j]
    return y

def rg_lru(x, wa, ba, wx, bx, lam):
    B, T, _ = x.shape
    xf = x.astype(jnp.float32)
    xb = xf.reshape(B, T, RG_BLOCKS, RG_BLOCK)
    r = jax.nn.sigmoid(jnp.einsum('btgi,gij->btgj', xb, wa.astype(jnp.float32)).reshape(B, T, D_RG) + ba)
    i = jax.nn.sigmoid(jnp.einsum('btgi,gij->btgj', xb, wx.astype(jnp.float32)).reshape(B, T, D_RG) + bx)
    log_a = -RG_C * r * jax.nn.softplus(-lam.astype(jnp.float32))
    a = jnp.exp(log_a)
    mult = jnp.sqrt(-jnp.expm1(2.0 * log_a))
    mult = jnp.where(jnp.arange(T)[None, :, None] == 0, 1.0, mult)
    u = mult * (i * xf)

    def combine(left, right):
        a_l, b_l = left
        a_r, b_r = right
        return a_l * a_r, a_r * b_l + b_r

    _, h = lax.associative_scan(combine, (a, u), axis=1)
    return h.astype(x.dtype)

def gla_chunked(q, k, logf, v):
    B, T, H, K = q.shape
    V = v.shape[-1]
    C = HG_CHUNK
    N = T // C

    def chunks(t):
        return t.reshape(B, N, C, H, t.shape[-1]).transpose(0, 3, 1, 2, 4)

    q, k, logf, v = chunks(q), chunks(k), chunks(logf), chunks(v)
    b = jnp.cumsum(logf, axis=3)
    b_last = b[:, :, :, -1:, :]
    qe = q * jnp.exp(b)
    ke = k * jnp.exp(-b)
    scores = jnp.einsum('bhnck,bhnsk->bhncs', qe, ke)
    causal = jnp.tril(jnp.ones((C, C), dtype=bool))
    scores = jnp.where(causal, scores, 0.0)
    o_intra = jnp.einsum('bhncs,bhnsv->bhncv', scores, v)

    kd = k * jnp.exp(b_last - b)
    dS = jnp.einsum('bhnsk,bhnsv->bhnkv', kd, v)
    decay = jnp.exp(b_last[:, :, :, 0, :])

    def step(S, inp):
        d, ds = inp
        return d[..., None] * S + ds, S

    S0 = jnp.zeros((B, H, K, V), jnp.float32)
    _, S_prev = lax.scan(step, S0, (jnp.moveaxis(decay, 2, 0), jnp.moveaxis(dS, 2, 0)))
    o_inter = jnp.einsum('bhnck,nbhkv->bhncv', qe, S_prev)
    o = o_intra + o_inter
    return o.transpose(0, 2, 3, 1, 4).reshape(B, T, H, V)

def hgrn2_branch(q, fz, iv, g, lb, norm_w):
    B, T, _ = q.shape
    qf, fzf, ivf, gf = (t.astype(jnp.float32) for t in (q, fz, iv, g))
    lb = lb.astype(jnp.float32)
    f = lb + (1.0 - lb) * jax.nn.sigmoid(fzf)
    logf = jnp.log(f)
    k = (1.0 - lb) * jax.nn.sigmoid(-fzf)
    qs = jax.nn.silu(qf) * (HG_HEAD_DIM ** -0.5)
    heads = lambda t: t.reshape(B, T, HG_HEADS, HG_HEAD_DIM)
    o = gla_chunked(heads(qs), heads(k), heads(logf), heads(ivf))
    o = o * lax.rsqrt(jnp.mean(o * o, axis=-1, keepdims=True) + EPS) * norm_w.astype(jnp.float32)
    o = o.reshape(B, T, D_HG) * jax.nn.silu(gf)
    return o.astype(q.dtype)

def first_inputs(seed: int = 0) -> dict:
    key = jax.random.key(seed)
    ks = jax.random.split(key, 20)
    f32 = jnp.float32
    nrm = lambda k, shape, scale: scale * jax.random.normal(k, shape, f32)
    u = jax.random.uniform(ks[10], (DEPTH, D_RG), f32, minval=0.9, maxval=0.999)
    s = u ** (1.0 / RG_C)
    rg_lambda = jnp.log(s) - jnp.log1p(-s)
    return {
        "x": jax.random.normal(ks[0], (BATCH, SEQ, D_MODEL), f32),
        "p": jax.random.normal(ks[1], (DEPTH, BATCH, SEQ, PLE_DIM), f32),
        "norm_mix_w": 1.0 + nrm(ks[2], (DEPTH, D_MODEL), 0.1),
        "w_in": nrm(ks[3], (DEPTH, D_MODEL, D_IN), D_MODEL ** -0.5),
        "conv_w": nrm(ks[4], (DEPTH, CONV_WIDTH, D_RG), CONV_WIDTH ** -0.5),
        "conv_b": nrm(ks[5], (DEPTH, D_RG), 0.01),
        "rg_wa": nrm(ks[6], (DEPTH, RG_BLOCKS, RG_BLOCK, RG_BLOCK), RG_BLOCK ** -0.5),
        "rg_ba": nrm(ks[7], (DEPTH, D_RG), 0.1),
        "rg_wx": nrm(ks[8], (DEPTH, RG_BLOCKS, RG_BLOCK, RG_BLOCK), RG_BLOCK ** -0.5),
        "rg_bx": nrm(ks[9], (DEPTH, D_RG), 0.1),
        "rg_lambda": rg_lambda,
        "hg_lb": nrm(ks[11], (DEPTH + 1, D_HG), 0.1),
        "hg_norm_w": 1.0 + nrm(ks[12], (DEPTH, HG_HEAD_DIM), 0.1),
        "w_out": nrm(ks[13], (DEPTH, D_MIX, D_MODEL), D_MIX ** -0.5),
        "ple_norm_w": 1.0 + nrm(ks[14], (DEPTH, D_MODEL), 0.1),
        "w_ple_gate": nrm(ks[15], (DEPTH, D_MODEL, D_MODEL), D_MODEL ** -0.5),
        "b_ple_gate": nrm(ks[16], (DEPTH, D_MODEL), 0.1),
        "w_ple_proj": nrm(ks[17], (DEPTH, PLE_DIM, D_MODEL), PLE_DIM ** -0.5),
        "final_norm_w": 1.0 + nrm(ks[18], (D_MODEL,), 0.1),
    }

def first_block(x, p, norm_mix_w, w_in, conv_w, conv_b, rg_wa, rg_ba, rg_wx, rg_bx,
              rg_lambda, hg_lb, hg_norm_w, w_out, ple_norm_w, w_ple_gate, b_ple_gate,
              w_ple_proj, final_norm_w):
    lb_all = jnp.cumsum(jax.nn.softmax(hg_lb.astype(jnp.float32), axis=0), axis=0)
    split_at = [D_RG, 2 * D_RG, 2 * D_RG + D_HG, 2 * D_RG + 2 * D_HG, 2 * D_RG + 3 * D_HG]
    h = x
    for l in range(DEPTH):
        u = rms_norm(h, norm_mix_w[l])
        proj = u @ w_in[l]
        xa, ga, qb, fb, ib, gb = jnp.split(proj, split_at, axis=-1)
        xa = causal_depthwise_conv(xa, conv_w[l], conv_b[l])
        ya = rg_lru(xa, rg_wa[l], rg_ba[l], rg_wx[l], rg_bx[l], rg_lambda[l]) * jax.nn.silu(ga)
        yb = hgrn2_branch(qb, fb, ib, gb, lb_all[l], hg_norm_w[l])
        h = h + jnp.concatenate([ya, yb], axis=-1) @ w_out[l]
        gate = jax.nn.sigmoid(rms_norm(h, ple_norm_w[l]) @ w_ple_gate[l] + b_ple_gate[l])
        h = h + gate * (p[l] @ w_ple_proj[l])
    return rms_norm(h, final_norm_w)


DEPTH_2 = 4

CTX_LEN = 256
GRID_W = 64
N_MIXERS = 3
N_CONV_LAYERS = (DEPTH_2 + 2) // N_MIXERS
N_RWKV_LAYERS = (DEPTH_2 + 1) // N_MIXERS
N_ATTN_LAYERS = DEPTH_2 // N_MIXERS
CONV_WIDTH_2 = 31
RWKV_HEAD = 64
RWKV_HEADS = D_MODEL // RWKV_HEAD
DECAY_LORA = 64
ICLR_LORA = 64
ATTN_HEAD = 128
ATTN_Q_HEADS = D_MODEL // 64
ATTN_KV_HEADS = ATTN_Q_HEADS // 2
ATTN_GROUP = ATTN_Q_HEADS // ATTN_KV_HEADS
ATTN_QW = ATTN_Q_HEADS * ATTN_HEAD
ATTN_KVW = ATTN_KV_HEADS * ATTN_HEAD
Q_BLOCK = 128
ROPE_THETA = 10000.0
AXIS_DIM = ATTN_HEAD // 2
NORM_EPS = 1e-6
LN_EPS = 1e-5
GN_EPS = 64e-5


def rmsnorm(x, g):
    x32 = x.astype(jnp.float32)
    y = x32 * lax.rsqrt(jnp.mean(x32 * x32, axis=-1, keepdims=True) + NORM_EPS)
    return (y * g.astype(jnp.float32)).astype(x.dtype)

def layernorm(x, g, b):
    x32 = x.astype(jnp.float32)
    mean = jnp.mean(x32, axis=-1, keepdims=True)
    var = jnp.mean(jnp.square(x32 - mean), axis=-1, keepdims=True)
    y = (x32 - mean) * lax.rsqrt(var + LN_EPS)
    return (y * g.astype(jnp.float32) + b.astype(jnp.float32)).astype(x.dtype)

def modulation(cvec, w, b):
    m = jax.nn.silu(cvec) @ w + b
    return jnp.split(m, 3, axis=-1)

def modulate(n, shift, scale):
    return n * (1.0 + scale) + shift

def rope_tables(T):
    rows = T // GRID_W
    row = jnp.repeat(jnp.arange(rows), GRID_W).astype(jnp.float32)
    col = (jnp.arange(rows * GRID_W) % GRID_W).astype(jnp.float32)
    inv = 1.0 / (ROPE_THETA ** (jnp.arange(0, AXIS_DIM, 2, dtype=jnp.float32) / AXIS_DIM))
    ang = jnp.stack([row[:, None] * inv, col[:, None] * inv])
    return jnp.cos(ang), jnp.sin(ang)

def rope_axis(x, cos, sin):
    x1, x2 = jnp.split(x, 2, axis=-1)
    return jnp.concatenate([x1 * cos - x2 * sin, x2 * cos + x1 * sin], axis=-1)

def rope2d(x, cos, sin):
    y = jnp.concatenate([rope_axis(x[..., :AXIS_DIM], cos[0], sin[0]),
                         rope_axis(x[..., AXIS_DIM:], cos[1], sin[1])], axis=-1)
    return y.astype(x.dtype)

def depthwise_conv(y, w, b):
    C = y.shape[-1]
    out = lax.conv_general_dilated(y, w[:, None, :].astype(y.dtype), window_strides=(1,),
                                   padding=((CONV_WIDTH_2 // 2, CONV_WIDTH_2 // 2),),
                                   dimension_numbers=("NWC", "WIO", "NWC"),
                                   feature_group_count=C)
    return out + b

def conv_branch(h, w_in, dw, db, ln_g, ln_b, w_out):
    a, b, gate = jnp.split(h @ w_in, 3, axis=-1)
    y = a * jax.nn.sigmoid(b)
    y = depthwise_conv(y, dw, db)
    y = jax.nn.silu(layernorm(y, ln_g, ln_b))
    return (y * jax.nn.silu(gate)) @ w_out

def centred_shift(h):
    hp = jnp.pad(h, ((0, 0), (1, 1), (0, 0)))
    return 0.5 * (hp[:, :-2] + hp[:, 2:])

def rwkv_features(h, proj, with_out):
    mu, w_r, w_k, w_v, w_g, w0, w1, w2, a0, a1, a2, k_k, k_a = proj
    B, T, _ = h.shape
    heads = lambda t: t.reshape(B, T, RWKV_HEADS, RWKV_HEAD)
    xx = centred_shift(h) - h
    lerp = lambda n: h + xx * mu[n]
    k = lerp(2) @ w_k
    v = heads(lerp(3) @ w_v)
    kk = heads(k * k_k).astype(jnp.float32)
    kk = kk * lax.rsqrt(jnp.sum(kk * kk, axis=-1, keepdims=True) + 1e-12)
    xw, xa = lerp(1), lerp(4)
    dirs = []
    for d in range(2):
        w_log = -jax.nn.softplus(-(w0[d] + jnp.tanh(xw @ w1[d]) @ w2[d])) - 0.5
        dec = jnp.exp(-jnp.exp(w_log.astype(jnp.float32)))
        a = jax.nn.sigmoid(a0[d] + (xa @ a1[d]) @ a2[d])
        dirs.append((heads(dec), heads(k * (1.0 + (a - 1.0) * k_a)), heads(a)))
    r = heads(lerp(0) @ w_r) if with_out else None
    g = (lerp(5) @ w_g) if with_out else None
    return r, g, v, kk, dirs

def wkv_scan(state0, r, dec, k, v, kk, a, reverse):
    emit = r is not None

    def step(S, inp):
        d_t, k_t, v_t, kk_t, a_t = inp[:5]
        sa = jnp.einsum("bhvk,bhk->bhv", S, -kk_t)
        S = (S * d_t[:, :, None, :] + sa[..., None] * (kk_t * a_t)[:, :, None, :]
             + v_t[..., None] * k_t[:, :, None, :])
        out = jnp.einsum("bhvk,bhk->bhv", S, inp[5]) if emit else None
        return S, out

    xs = (dec, k, v, kk, a, r) if emit else (dec, k, v, kk, a)
    return lax.scan(step, state0, xs, reverse=reverse)

def rwkv_readout(o, r, v, k_sum, g, r_k, ln_g, ln_b, w_o):
    o = jnp.moveaxis(o, 0, 1)
    B, T = o.shape[:2]
    mean = jnp.mean(o, axis=-1, keepdims=True)
    var = jnp.mean(jnp.square(o - mean), axis=-1, keepdims=True)
    o = (o - mean) * lax.rsqrt(var + GN_EPS)
    o = o * ln_g.reshape(RWKV_HEADS, RWKV_HEAD) + ln_b.reshape(RWKV_HEADS, RWKV_HEAD)
    bonus = jnp.sum(r * k_sum * r_k, axis=-1, keepdims=True) * v
    y = (o + bonus).astype(g.dtype).reshape(B, T, D_MODEL)
    return (y * jax.nn.silu(g)) @ w_o

def rwkv_mixer(h, hc, mu, w_r, w_k, w_v, w_g, w0, w1, w2, a0, a1, a2, k_k, k_a,
               r_k, ln_g, ln_b, w_o, ctx_out):
    proj = (mu, w_r, w_k, w_v, w_g, w0, w1, w2, a0, a1, a2, k_k, k_a)
    r, g, v, kk, dirs = rwkv_features(h, proj, True)
    rc, gc, vc, kkc, dirs_c = rwkv_features(hc, proj, ctx_out)
    tm = lambda t: None if t is None else jnp.moveaxis(t, 1, 0)
    state0 = jnp.zeros((h.shape[0], RWKV_HEADS, RWKV_HEAD, RWKV_HEAD), jnp.float32)
    o, oc = 0.0, 0.0
    for d, rev in ((0, False), (1, True)):
        dec_c, k_c, a_c = dirs_c[d]
        state_c, o_c_d = wkv_scan(state0, tm(rc), tm(dec_c), tm(k_c), tm(vc), tm(kkc), tm(a_c), rev)
        dec_l, k_l, a_l = dirs[d]
        _, o_d = wkv_scan(state_c, tm(r), tm(dec_l), tm(k_l), tm(v), tm(kk), tm(a_l), rev)
        o = o + o_d
        if ctx_out:
            oc = oc + o_c_d
    y = rwkv_readout(o, r, v, dirs[0][1] + dirs[1][1], g, r_k, ln_g, ln_b, w_o)
    yc = None
    if ctx_out:
        yc = rwkv_readout(oc, rc, vc, dirs_c[0][1] + dirs_c[1][1], gc, r_k, ln_g, ln_b, w_o)
    return y, yc

def split_heads(t, n):
    B, T, _ = t.shape
    return t.reshape(B, T, n, ATTN_HEAD).transpose(0, 2, 1, 3)

def merge_heads(o):
    B, _, _, Q, _ = o.shape
    return o.transpose(0, 3, 1, 2, 4).reshape(B, Q, ATTN_QW)

def gqa_attend(q, k, v):
    s = jnp.einsum("bhgqd,bhkd->bhgqk", q, k) * (ATTN_HEAD ** -0.5)
    return jnp.einsum("bhgqk,bhkd->bhgqd", jax.nn.softmax(s, axis=-1), v)

def blocked_attention(q, k, v):
    B, _, T, _ = q.shape
    nb = T // Q_BLOCK
    qb = q.astype(jnp.float32).reshape(B, ATTN_KV_HEADS, ATTN_GROUP, nb, Q_BLOCK, ATTN_HEAD)
    qb = qb.transpose(3, 0, 1, 2, 4, 5)
    ob = lax.map(lambda qq: gqa_attend(qq, k, v), qb)
    return ob.transpose(1, 0, 4, 2, 3, 5).reshape(B, T, ATTN_QW)

def attn_mixer(h, hc, w_in, q_g, k_g, w_out, cos, sin, ctx_out):
    cuts = [ATTN_QW, ATTN_QW + ATTN_KVW, ATTN_QW + 2 * ATTN_KVW]
    q, k, v, g = jnp.split(h @ w_in, cuts, axis=-1)
    q = rope2d(rmsnorm(split_heads(q, ATTN_Q_HEADS), q_g), cos, sin)
    k = rope2d(rmsnorm(split_heads(k, ATTN_KV_HEADS), k_g), cos, sin)
    v = split_heads(v, ATTN_KV_HEADS)
    if ctx_out:
        qc, kc, vc, gc = jnp.split(hc @ w_in, cuts, axis=-1)
    else:
        kc, vc = jnp.split(hc @ w_in[:, ATTN_QW:ATTN_QW + 2 * ATTN_KVW], 2, axis=-1)
    kc = rmsnorm(split_heads(kc, ATTN_KV_HEADS), k_g).astype(jnp.float32)
    vc = split_heads(vc, ATTN_KV_HEADS).astype(jnp.float32)
    k_all = jnp.concatenate([kc, k.astype(jnp.float32)], axis=2)
    v_all = jnp.concatenate([vc, v.astype(jnp.float32)], axis=2)
    o = blocked_attention(q, k_all, v_all).astype(g.dtype)
    y = (o * jax.nn.silu(g)) @ w_out
    yc = None
    if ctx_out:
        qc = rmsnorm(split_heads(qc, ATTN_Q_HEADS), q_g).astype(jnp.float32)
        B, _, L, _ = qc.shape
        oc = merge_heads(gqa_attend(qc.reshape(B, ATTN_KV_HEADS, ATTN_GROUP, L, ATTN_HEAD), kc, vc))
        yc = (oc.astype(gc.dtype) * jax.nn.silu(gc)) @ w_out
    return y, yc

def second_inputs(seed: int = 0) -> dict:
    key = jax.random.key(seed)
    keys = iter(jax.random.split(key, 48))
    D, NC, NR, NA = D_MODEL, N_CONV_LAYERS, N_RWKV_LAYERS, N_ATTN_LAYERS

    def nrm(shape, s):
        return jax.random.normal(next(keys), shape, jnp.float32) * s

    def unif(shape, lo, hi):
        return jax.random.uniform(next(keys), shape, jnp.float32, lo, hi)

    return {
        "x": nrm((BATCH, SEQ, D), 1.0),
        "c": nrm((BATCH, D), 1.0),
        "ctx": nrm((BATCH, CTX_LEN, D), 1.0),
        "c_ctx": nrm((D,), 1.0),
        "norm_g": 1.0 + nrm((DEPTH_2, D), 0.02),
        "mod_w": nrm((DEPTH_2, D, 3 * D), D ** -0.5),
        "mod_b": nrm((DEPTH_2, 3 * D), 0.02),
        "conv_w_in": nrm((NC, D, 3 * D), D ** -0.5),
        "conv_dw": nrm((NC, CONV_WIDTH_2, D), CONV_WIDTH_2 ** -0.5),
        "conv_db": nrm((NC, D), 0.02),
        "conv_ln_g": 1.0 + nrm((NC, D), 0.02),
        "conv_ln_b": nrm((NC, D), 0.02),
        "conv_w_out": nrm((NC, D, D), D ** -0.5),
        "rwkv_mu": unif((NR, 6, D), 0.0, 1.0),
        "rwkv_w_r": nrm((NR, D, D), D ** -0.5),
        "rwkv_w_k": nrm((NR, D, D), D ** -0.5),
        "rwkv_w_v": nrm((NR, D, D), D ** -0.5),
        "rwkv_w_g": nrm((NR, D, D), D ** -0.5),
        "rwkv_w0": unif((NR, 2, D), -5.0, 0.5),
        "rwkv_w1": nrm((NR, 2, D, DECAY_LORA), D ** -0.5),
        "rwkv_w2": nrm((NR, 2, DECAY_LORA, D), 0.1 * DECAY_LORA ** -0.5),
        "rwkv_a0": nrm((NR, 2, D), 0.1),
        "rwkv_a1": nrm((NR, 2, D, ICLR_LORA), D ** -0.5),
        "rwkv_a2": nrm((NR, 2, ICLR_LORA, D), 0.1 * ICLR_LORA ** -0.5),
        "rwkv_k_k": 0.85 + nrm((NR, D), 0.02),
        "rwkv_k_a": 1.0 + nrm((NR, D), 0.02),
        "rwkv_r_k": nrm((NR, RWKV_HEADS, RWKV_HEAD), 0.1),
        "rwkv_ln_g": 1.0 + nrm((NR, D), 0.02),
        "rwkv_ln_b": nrm((NR, D), 0.02),
        "rwkv_w_o": nrm((NR, D, D), D ** -0.5),
        "attn_w_in": nrm((NA, D, 2 * ATTN_QW + 2 * ATTN_KVW), D ** -0.5),
        "attn_q_g": 1.0 + nrm((NA, ATTN_HEAD), 0.02),
        "attn_k_g": 1.0 + nrm((NA, ATTN_HEAD), 0.02),
        "attn_w_out": nrm((NA, ATTN_QW, D), ATTN_QW ** -0.5),
        "final_g": 1.0 + nrm((D,), 0.02),
    }

def second_block(x, c, ctx, c_ctx, norm_g, mod_w, mod_b,
              conv_w_in, conv_dw, conv_db, conv_ln_g, conv_ln_b, conv_w_out,
              rwkv_mu, rwkv_w_r, rwkv_w_k, rwkv_w_v, rwkv_w_g,
              rwkv_w0, rwkv_w1, rwkv_w2, rwkv_a0, rwkv_a1, rwkv_a2,
              rwkv_k_k, rwkv_k_a, rwkv_r_k, rwkv_ln_g, rwkv_ln_b, rwkv_w_o,
              attn_w_in, attn_q_g, attn_k_g, attn_w_out, final_g):
    cos, sin = rope_tables(x.shape[1])
    xc = ctx
    for i in range(DEPTH_2):
        kind, j = i % N_MIXERS, i // N_MIXERS
        ctx_out = any(l % N_MIXERS != 0 for l in range(i + 1, DEPTH_2))
        ctx_in = ctx_out or kind != 0
        shift, scale, gate = modulation(c, mod_w[i], mod_b[i])
        h = modulate(rmsnorm(x, norm_g[i]), shift[:, None], scale[:, None])
        hc = None
        if ctx_in:
            shift_c, scale_c, gate_c = modulation(c_ctx, mod_w[i], mod_b[i])
            hc = modulate(rmsnorm(xc, norm_g[i]), shift_c, scale_c)
        if kind == 0:
            conv_p = (conv_w_in[j], conv_dw[j], conv_db[j], conv_ln_g[j], conv_ln_b[j], conv_w_out[j])
            y = conv_branch(h, *conv_p)
            yc = conv_branch(hc, *conv_p) if ctx_out else None
        elif kind == 1:
            y, yc = rwkv_mixer(h, hc, rwkv_mu[j], rwkv_w_r[j], rwkv_w_k[j], rwkv_w_v[j], rwkv_w_g[j],
                               rwkv_w0[j], rwkv_w1[j], rwkv_w2[j], rwkv_a0[j], rwkv_a1[j], rwkv_a2[j],
                               rwkv_k_k[j], rwkv_k_a[j], rwkv_r_k[j], rwkv_ln_g[j], rwkv_ln_b[j],
                               rwkv_w_o[j], ctx_out)
        else:
            y, yc = attn_mixer(h, hc, attn_w_in[j], attn_q_g[j], attn_k_g[j], attn_w_out[j],
                               cos, sin, ctx_out)
        x = x + gate[:, None] * y
        if ctx_out:
            xc = xc + gate_c * yc
    return rmsnorm(x, final_g)


def setup_inputs(seed=0):
    out = dict(first_inputs(seed))
    for name, value in second_inputs(seed + 1).items():
        if name != "x":
            out[name + "_2"] = value
    return out


def reference(
    x, p, norm_mix_w, w_in, conv_w, conv_b, rg_wa, rg_ba, rg_wx, rg_bx, rg_lambda, hg_lb,
    hg_norm_w, w_out, ple_norm_w, w_ple_gate, b_ple_gate, w_ple_proj, final_norm_w, c_2, ctx_2,
    c_ctx_2, norm_g_2, mod_w_2, mod_b_2, conv_w_in_2, conv_dw_2, conv_db_2, conv_ln_g_2,
    conv_ln_b_2, conv_w_out_2, rwkv_mu_2, rwkv_w_r_2, rwkv_w_k_2, rwkv_w_v_2, rwkv_w_g_2,
    rwkv_w0_2, rwkv_w1_2, rwkv_w2_2, rwkv_a0_2, rwkv_a1_2, rwkv_a2_2, rwkv_k_k_2, rwkv_k_a_2,
    rwkv_r_k_2, rwkv_ln_g_2, rwkv_ln_b_2, rwkv_w_o_2, attn_w_in_2, attn_q_g_2, attn_k_g_2,
    attn_w_out_2, final_g_2,
):
    x = first_block(
        x, p, norm_mix_w, w_in, conv_w, conv_b, rg_wa, rg_ba, rg_wx, rg_bx, rg_lambda, hg_lb,
        hg_norm_w, w_out, ple_norm_w, w_ple_gate, b_ple_gate, w_ple_proj, final_norm_w,
    )
    return second_block(
        x, c_2, ctx_2, c_ctx_2, norm_g_2, mod_w_2, mod_b_2, conv_w_in_2, conv_dw_2, conv_db_2,
        conv_ln_g_2, conv_ln_b_2, conv_w_out_2, rwkv_mu_2, rwkv_w_r_2, rwkv_w_k_2, rwkv_w_v_2,
        rwkv_w_g_2, rwkv_w0_2, rwkv_w1_2, rwkv_w2_2, rwkv_a0_2, rwkv_a1_2, rwkv_a2_2,
        rwkv_k_k_2, rwkv_k_a_2, rwkv_r_k_2, rwkv_ln_g_2, rwkv_ln_b_2, rwkv_w_o_2, attn_w_in_2,
        attn_q_g_2, attn_k_g_2, attn_w_out_2, final_g_2,
    )


_drawn_inputs = setup_inputs


def setup_inputs(seed=0):
    import zlib

    import numpy as np

    out = dict(_drawn_inputs(seed))
    spreads = {}
    factors = {'conv_b': 2.735,
     'rg_ba': 8.0,
     'rg_bx': 6.442,
     'hg_lb': 8.0,
     'ple_norm_w': 2.824,
     'b_ple_gate': 2.79,
     'norm_g_2': 2.88,
     'conv_db_2': 4.808,
     'conv_ln_g_2': 5.447,
     'conv_ln_b_2': 6.332,
     'rwkv_w1_2': 8.0,
     'rwkv_w2_2': 8.0,
     'rwkv_a0_2': 3.354,
     'rwkv_a1_2': 2.955,
     'rwkv_a2_2': 2.873,
     'rwkv_ln_g_2': 8.0,
     'rwkv_ln_b_2': 8.0,
     'attn_q_g_2': 8.0,
     'attn_k_g_2': 8.0,
     'final_g_2': 2.864}
    for name, (base, spread) in spreads.items():
        noise = np.random.default_rng([zlib.crc32(name.encode()), seed]).standard_normal(out[name].shape)
        drawn = base * np.exp(spread * noise) if base else spread * noise
        out[name] = jnp.asarray(drawn.astype(out[name].dtype))
    for name, factor in factors.items():
        out[name] = (out[name] * factor).astype(out[name].dtype)
    return out
```

```python
from contextlib import ExitStack

import numpy as np
import concourse.bass as bass
from concourse import mybir

P = 128
D = 1024
DT = D // P
TX, TC = 512, 256
TT = TX + TC
CH = 64
NCX, NCC = TX // CH, TC // CH
NSTEP = NCX + NCC
NPAIR = 8
NU = 2 * NSTEP
SLOTS = 4
EPS = 1e-6
LN_EPS = 1e-5
GN_EPS = 64e-5
TAPS = 31
PAD = TAPS // 2
XW, CW = TX + 2 * PAD, TC + 2 * PAD
YW = XW + CW

F32 = mybir.dt.float32
ALU = mybir.AluOpType
ACT = mybir.ActivationFunctionType
AX = mybir.AxisListType


def vector_table():
    sizes = [("norm_mix_w", 8), ("conv_w", 16), ("conv_b", 4), ("rg_ba", 4), ("rg_bx", 4),
             ("rg_lambda", 4), ("hg_lb", 8), ("hg_norm_w", 1), ("ple_norm_w", 8),
             ("b_ple_gate", 8), ("final_norm_w", 8), ("c_2", 8), ("c_ctx_2", 8),
             ("norm_g_2", 32), ("mod_b_2", 96), ("conv_dw_2", 496), ("conv_db_2", 16),
             ("conv_ln_g_2", 16), ("conv_ln_b_2", 16), ("rwkv_mu_2", 48), ("rwkv_w0_2", 16),
             ("rwkv_a0_2", 16), ("rwkv_k_k_2", 8), ("rwkv_k_a_2", 8), ("rwkv_r_k_2", 8),
             ("rwkv_ln_g_2", 8), ("rwkv_ln_b_2", 8), ("attn_q_g_2", 1), ("attn_k_g_2", 1),
             ("final_g_2", 8)]
    table, at = {}, 0
    for name, n in sizes:
        table[name] = (at, n)
        at += n
    return table, at


VT, NVEC = vector_table()

CT, NCONST = {}, 0
for _n, _w in (("ident", 128), ("ones", 128), ("ones64", 128), ("rot", 128),
               ("gla_mask", 128), ("inv_mask", 6 * 128), ("wkv_mask", 2 * 256)):
    CT[_n] = (NCONST, _w)
    NCONST += _w


def constants():
    out = np.zeros((P, NCONST), np.float32)
    i, j = np.arange(P)[:, None], np.arange(P)[None, :]

    def put(name, a):
        out[:, CT[name][0]:CT[name][0] + CT[name][1]] = a

    put("ident", i == j)
    put("ones", np.ones((P, P)))
    put("ones64", i // 64 == j // 64)
    put("rot", np.where((j % 64 < 32) & (i == j + 32), -1.0, 0) + np.where((j % 64 >= 32) & (i == j - 32), 1.0, 0))
    put("gla_mask", (i // CH == j // CH) & (i <= j))
    m = [((i // (2 * b) == j // (2 * b)) & (i // b != j // b)) for b in (1, 2, 4, 8, 16, 32)]
    put("inv_mask", np.concatenate(m, 1))
    s, t = i % 64, j % 64
    w = []
    for strict, incl in ((s < t, s <= t), (s > t, s >= t)):
        w += [np.where(j < 64, strict, incl), np.where(j < 64, incl, strict)]
    put("wkv_mask", np.concatenate(w, 1))
    return out


def rope_tables():
    row = np.repeat(np.arange(TX // 64), 64).astype(np.float32)
    col = (np.arange(TX) % 64).astype(np.float32)
    inv = (1.0 / (np.float32(10000.0) ** (np.arange(0, 64, 2, dtype=np.float32) / np.float32(64)))).astype(np.float32)
    ang = np.concatenate([inv[:, None] * row[None]] * 2 + [inv[:, None] * col[None]] * 2, 0).astype(np.float32)
    return np.concatenate([np.cos(ang), np.sin(ang)], 1).astype(np.float32)


def weight_plan():
    plan, start = [], {}

    def stage(name, body, mod=None):
        start[name] = len(plan)
        for n, b in enumerate(body):
            plan.append(b)
            if mod is not None and n < 24:
                plan.append(("mod_w_2", mod, n))

    stage("in1", [("w_in", 0, m) for m in range(24)], 0)
    stage("rg", [("rg", 0, 0)])
    stage("out1", [("w_out", 0, m) for m in range(8)])
    stage("gate1", [("w_ple_gate", 0, m) for m in range(8)] + [("w_ple_proj", 0, 0), ("w_ple_proj", 0, 1)])
    tri = [("conv_w_in_2", 0, 8 * part + m) for m in range(8) for part in (0, 1, 2)]
    stage("conv0", tri, 1)
    stage("convout0", [("conv_w_out_2", 0, m) for m in range(8)])
    stage("lora", [("lora_w1", 0, 0), ("lora_a1", 0, 0), ("lora_w2", 0, 0), ("lora_a2", 0, 0)])
    stage("rkvg", [(f"rwkv_w_{n}_2", 0, m) for n in "rkvg" for m in range(8)], 2)
    stage("rwkvout", [("rwkv_w_o_2", 0, m) for m in range(8)])
    stage("attn_qk", [("attn_w_in_2", 0, m) for m in range(24)], 3)
    stage("attn_v", [("attn_w_in_2", 0, 24 + m) for m in range(8)])
    stage("attn_g", [("attn_w_in_2", 0, 32 + m) for m in range(16)])
    stage("attnout", [("attn_w_out_2", k, m) for m in range(8) for k in (0, 1)])
    stage("conv1", [("conv_w_in_2", 1, 8 * part + m) for m in range(8) for part in (0, 1, 2)])
    stage("convout1", [("conv_w_out_2", 1, m) for m in range(8)])
    return plan, start


PLAN, START = weight_plan()
NB = len(PLAN)


class Ring:

    def __init__(self, ready, used):
        self.ready, self.used = ready, used
        self.issued = 0
        self.taken = 0

    def supply(self, sp, ring, weights, upto):
        upto = min(upto, NB)
        while self.issued < upto:
            b = self.issued
            n = (upto - b) // SLOTS
            if b % SLOTS == 0 and b >= SLOTS and n > 1:
                with sp.Fori(0, n) as i:
                    for s in range(SLOTS):
                        sp.wait_ge(self.used, i * SLOTS + (b + s - SLOTS + 1))
                        sp.dma_start(ring[:, s, :], weights[bass.ds(i * SLOTS + (b + s), 1), :, :]
                                     .rearrange("a p n -> (a p) n")).then_inc(self.ready[s], 16)
                self.issued += n * SLOTS
                continue
            if b >= SLOTS:
                sp.wait_ge(self.used, b - SLOTS + 1)
            sp.dma_start(ring[:, b % SLOTS, :], weights[b, :, :]).then_inc(self.ready[b % SLOTS], 16)
            self.issued += 1

    def take(self, pe):
        b = self.taken
        pe.wait_ge(self.ready[b % SLOTS], 16 * (b // SLOTS + 1))
        self.taken += 1
        return b % SLOTS


class Chain:

    def __init__(self, sem):
        self.sem, self.n, self.base = sem, 0, 0

    def inc(self, ins):
        self.n += 1
        ins.then_inc(self.sem, 1)

    def wait(self, eng):
        eng.wait_ge(self.sem, self.base + self.n)

    def link(self, eng, ins):
        self.inc(ins)
        self.wait(eng)


def two_blocks(nc, xT, pT, ctxT, vectors, consts, rope, weights, outT):
    ctx = ExitStack()
    names = [0]

    def sem(name):
        names[0] += 1
        return ctx.enter_context(nc.semaphore(f"{name}_{names[0]}"))

    def sb(name, shape):
        return ctx.enter_context(nc.sbuf_tensor(name, shape, F32))

    def ap(t):
        return t[tuple(slice(None) for _ in t.shape)]

    with ctx:
        X = ap(sb("stream", [P, DT, TT]))
        RINGT = ap(sb("ring", [P, SLOTS, DT * P]))
        VEC = ap(sb("vec", [P, NVEC]))
        CON = ap(sb("con", [P, NCONST]))
        MODL = ap(sb("mod", [P, 4, 24, 2]))
        SC = ap(sb("sc", [P, DT, 2]))
        GA = ap(sb("ga", [P, DT, 2]))
        TINY = ap(sb("tiny", [P, 128]))
        room = 212000 // 4 - DT * TT - SLOTS * DT * P - NVEC - NCONST - 192 - 32 - 128
        ARENA = ap(sb("arena", [P, room]))
        PS = ap(ctx.enter_context(nc.psum_tensor("ps", [P, 4096], F32)))
        PMOD = PS[:, 7 * 512:7 * 512 + 48].rearrange("p (m v) -> p m v", v=2)

        rwkv_dram = nc.dram_tensor("rwkv_spill", [DT + 1, 8, P, TT], F32, kind="Internal").ap()
        y_dram = nc.dram_tensor("y_spill", [DT, P, TT], F32, kind="Internal").ap()
        x_dram = nc.dram_tensor("x_spill", [P, DT * TT], F32, kind="Internal").ap()

        ring_ready = [sem(f"ring_ready{s}") for s in range(SLOTS)]
        blocks_done = sem("blocks_done")
        loads = sem("loads")
        stores = sem("stores")
        R = Ring(ring_ready, blocks_done)
        dve_chain = Chain(sem("dve_chain"))
        act_chain = Chain(sem("act_chain"))
        pool_chain = Chain(sem("pool_chain"))

        def V(name, k=0, n=1):
            return VEC[:, VT[name][0] + k:VT[name][0] + k + n]

        def C(name, k=0, n=None):
            a = CT[name][0] + k
            return CON[:, a:a + (CT[name][1] if n is None else n)]

        def carve():
            at = [0]

            def take(*shape):
                n = int(np.prod(shape))
                a = ARENA[:, at[0]:at[0] + n]
                at[0] += n
                assert at[0] <= room, (at[0], room)
                if len(shape) == 1:
                    return a
                names_ = "abcd"[:len(shape)]
                kw = {c: s for c, s in zip(names_, shape)}
                return a.rearrange(f"p ({' '.join(names_)}) -> p {' '.join(names_)}", **kw)
            return take

        def dlink(ins):
            dve_chain.link(nc.vector, ins)

        def alink(ins):
            act_chain.link(nc.scalar, ins)

        def plink(ins):
            pool_chain.link(nc.gpsimd, ins)

        def vtt(o, a, b, op=ALU.mult):
            return nc.vector.tensor_tensor(o, a, b, op)

        def vts(o, a, s1, s2=None, op0=ALU.mult, op1=None):
            if s2 is None:
                return nc.vector.tensor_scalar(o, a, s1, None, op0)
            return nc.vector.tensor_scalar(o, a, s1, s2, op0, op1)

        def stt(o, a, s, b, op0=ALU.mult, op1=ALU.mult):
            return nc.vector.scalar_tensor_tensor(out=o, in0=a, scalar=s, in1=b, op0=op0, op1=op1)

        def act(o, a, f, **kw):
            return nc.scalar.activation(o, a, f, **kw)

        def mm(o, l, r, start=True, stop=True):
            return nc.tensor.matmul(o, l, r, start=start, stop=stop)


        def mod_block(pe, n):
            s = R.take(pe)
            w = RINGT[:, s, :].rearrange("p (k m) -> p k m", k=DT)
            for k in range(DT):
                last = mm(PMOD[:, n, :], w[:, k, :], SC[:, k, :], k == 0, k == DT - 1)
            last.then_inc(blocks_done, 1)

        def mod_finish(layer):
            b = V("mod_b_2", 24 * layer, 24).rearrange("p (m o) -> p m o", o=1).broadcast_to([P, 24, 2])
            dlink(vtt(MODL[:, layer], PMOD, b, ALU.add))

        def mod_gain(layer):
            g = V("norm_g_2", 8 * layer, 8).rearrange("p (m o) -> p m o", o=1).broadcast_to([P, 8, 2])
            dlink(stt(GA, MODL[:, layer, 8:16], 1.0, g, ALU.add, ALU.mult))

        def product(o, l, rhs, width, start, stop):
            last = None
            for a in range(0, width, 512):
                b = min(a + 512, width)
                last = mm(o[:, a:b], l, rhs[:, a:b], start, stop)
            return last

        def tile_product(pe, o, rhs, width):
            s = R.take(pe)
            w = RINGT[:, s, :].rearrange("p (k m) -> p k m", k=DT)
            for k in range(DT):
                last = product(o, w[:, k, :], rhs[k], width, k == 0, k == DT - 1)
            last.then_inc(blocks_done, 1)

        EPSC = {}
        for n, e in enumerate((EPS, LN_EPS, GN_EPS, 1e-12)):
            EPSC[e] = TINY[:, n:n + 1]

        def norm_stats(src, width, ones_name, scale, eps, rstd, sq, psum):
            n = len(src)
            sq_ready, sq_used = sem("sq_ready"), sem("sq_used")
            with nc.Block() as block:
                @block.scalar
                def _(a):
                    for k in range(n):
                        if k >= 2:
                            a.wait_ge(sq_used, k - 1)
                        act(sq[k % 2], src[k], ACT.Square).then_inc(sq_ready, 1)
                    a.wait_ge(sq_used, n)
                    alink(act(rstd, psum[:, 0:width], ACT.Ln, scale=scale, bias=EPSC[eps]))
                    alink(act(rstd, rstd, ACT.Exp, scale=-0.5))

                @block.tensor
                def _(pe):
                    for k in range(n):
                        pe.wait_ge(sq_ready, k + 1)
                        product(psum, C(ones_name), sq[k % 2], width, k == 0, k == n - 1).then_inc(sq_used, 1)

        def layer_input(layer, H, width, sq, rst):
            norm_stats([X[:, k, 0:width] for k in range(DT)], width, "ones", 1.0 / D, EPS, rst[:, 0:width],
                       [sq[:, 0, 0:width], sq[:, 1, 0:width]], PS)
            scaled = sem("scaled")
            halves = [(0, TX, 0), (TX, TT, 1)][:1 if width == TX else 2]
            with nc.Block() as block:
                @block.vector
                def _(v):
                    mod_gain(layer)
                    for k in range(DT):
                        for a, b, c in halves:
                            stt(H[c][:, k, :], X[:, k, a:b], GA[:, k, c:c + 1], rst[:, a:b]).then_inc(scaled, 1)

                @block.scalar
                def _(a_):
                    n = 0
                    for k in range(DT):
                        for a, b, c in halves:
                            n += 1
                            a_.wait_ge(scaled, n)
                            act(H[c][:, k, :], H[c][:, k, :], ACT.Identity, bias=MODL[:, layer, k, c:c + 1])

        SP8N, SP8, LB, OMLB = TINY[:, 8:12], TINY[:, 12:16], TINY[:, 16:20], TINY[:, 20:24]
        with nc.Block() as block:
            @block.sync
            def _(sp):
                sp.dma_start(VEC, vectors).then_inc(loads, 16)
                sp.dma_start(X[:, :, 0:TX], xT.rearrange("(k p) t -> p k t", p=P)).then_inc(loads, 16)
                sp.dma_start(CON, consts).then_inc(loads, 16)
                sp.dma_start(X[:, :, TX:TT], ctxT.rearrange("(k p) t -> p k t", p=P)).then_inc(loads, 16)
                R.supply(sp, RINGT, weights, SLOTS)

            @block.scalar
            def _(a):
                a.wait_ge(loads, 64)
                act(SC[:, :, 0], V("c_2", 0, 8), ACT.Silu)
                alink(act(SC[:, :, 1], V("c_ctx_2", 0, 8), ACT.Silu))

            @block.gpsimd
            def _(g):
                for n, e in enumerate((EPS, LN_EPS, GN_EPS, 1e-12)):
                    nc.gpsimd.memset(TINY[:, n:n + 1], e)
                plink(nc.gpsimd.memset(TINY[:, 4:5], 1.0))

        with nc.Block() as block:
            t0, t1, t2, t3 = (TINY[:, 32 + 4 * n:36 + 4 * n] for n in range(4))
            e_ready, e_asked = sem("e_ready"), sem("e_asked")

            @block.vector
            def _(v):
                lam = V("rg_lambda", 0, 4)
                h0, h1 = V("hg_lb", 0, 4), V("hg_lb", 4, 4)
                dlink(vts(t0, lam, -1.0))
                dlink(vtt(t1, t0, lam, ALU.max))
                dlink(vtt(t2, h0, h1, ALU.max))
                dlink(vtt(TINY[:, 48:52], h0, t2, ALU.subtract))
                vtt(TINY[:, 52:56], h1, t2, ALU.subtract).then_inc(e_asked, 1)
                v.wait_ge(e_ready, 2)
                E_ = TINY[:, 56:60]
                dlink(vts(t2, E_, 2.0, None, ALU.add))
                dlink(nc.vector.reciprocal(t2, t2))
                dlink(vtt(t2, t2, E_))
                dlink(vtt(t3, t2, t2))
                dlink(vts(t1, t3, 1.0 / 19, 1.0 / 17, ALU.mult, ALU.add))
                for q in (15, 13, 11, 9, 7, 5, 3, 1):
                    dlink(vtt(t1, t1, t3))
                    dlink(vts(t1, t1, 1.0 / q, None, ALU.add))
                dlink(stt(t1, t1, 2.0, t2, ALU.mult, ALU.mult))
                dlink(vts(t0, t0, 0.0, None, ALU.max))
                dlink(vtt(t1, t1, t0, ALU.add))
                dlink(vts(SP8N, t1, -8.0))
                dlink(vts(SP8, t1, 8.0))
                a0, a1 = TINY[:, 60:64], TINY[:, 64:68]
                dlink(vtt(t2, a0, a1, ALU.add))
                dlink(nc.vector.reciprocal(t2, t2))
                dlink(vtt(LB, a0, t2))
                dlink(vtt(OMLB, a1, t2))

            @block.scalar
            def _(a):
                a.wait_ge(e_asked, 1)
                act(TINY[:, 56:60], t1, ACT.Exp, scale=-1.0).then_inc(e_ready, 1)
                act(TINY[:, 60:68], TINY[:, 48:56], ACT.Exp).then_inc(e_ready, 1)

        take = carve()
        H = take(DT, TX)
        RAW = take(20, TX)
        VTOK = take(4, 512)
        sq = take(2, TT)
        RST = take(TT)
        XAP = take(4, TX + 4)
        XC, RG, IG, AG, TH = (take(4, TX) for _ in range(5))

        norm_stats([X[:, k, 0:TX] for k in range(DT)], TX, "ones", 1.0 / D, EPS, RST[:, 0:TX],
                   [sq[:, 0, 0:TX], sq[:, 1, 0:TX]], PS)
        with nc.Block() as block:
            @block.vector
            def _(v):
                for k in range(DT):
                    stt(H[:, k, :], X[:, k, 0:TX], V("norm_mix_w", k), RST[:, 0:TX])
                dlink(nc.vector.memset(XAP[:, :, 0:3], 0.0))

        bank_free = sem("bank_free")
        with nc.Block() as block:
            @block.sync
            def _(sp):
                R.supply(sp, RINGT, weights, START["rg"] + SLOTS)

            @block.tensor
            def _(pe):
                for m in range(24):
                    if m >= 2:
                        pe.wait_ge(bank_free, m - 1)
                    bank = PS[:, (m % 2) * 512:(m % 2) * 512 + 512]
                    if 16 <= m < 20:
                        s = R.take(pe)
                        w = RINGT[:, s, :].rearrange("p (k m) -> p k m", k=DT)
                        for t in range(4):
                            for k in range(DT):
                                last = mm(bank[:, t * P:t * P + P], H[:, k, t * P:t * P + P], w[:, k, :], k == 0, k == DT - 1)
                        last.then_inc(blocks_done, 1)
                    else:
                        tile_product(pe, bank, [H[:, k, :] for k in range(DT)], TX)
                    mod_block(pe, m)

            @block.scalar
            def _(a):
                for m in range(24):
                    a.wait_ge(blocks_done, START["in1"] + 2 * m + 1)
                    bank = PS[:, (m % 2) * 512:(m % 2) * 512 + 512]
                    o, i_ = RAW[:, m if m < 16 else m - 4, :], bank
                    if m < 4:
                        o = XAP[:, m, 3:3 + TX]
                    if 16 <= m < 20:
                        o = VTOK.rearrange("p t (h v) -> p t h v", h=4)[:, :, m - 16, :]
                        i_ = bank.rearrange("p (t v) -> p t v", t=4)
                    act(o, i_, ACT.Copy).then_inc(bank_free, 1)

        xc_ready = sem("xc_ready")
        gates_done, rg_done = sem("gates_done"), sem("rg_done")
        Y1 = H
        with nc.Block() as block:
            @block.sync
            def _(sp):
                R.supply(sp, RINGT, weights, START["out1"] + SLOTS)

            @block.vector
            def _(v):
                mod_finish(0)
                for m in range(4):
                    dlink(vts(XC[:, m, :], XAP[:, m, 3:3 + TX], V("conv_w", 12 + m), V("conv_b", m), ALU.mult, ALU.add))
                    for j in range(3):
                        ins = stt(XC[:, m, :], XAP[:, m, j:j + TX], V("conv_w", 4 * j + m), XC[:, m, :], ALU.mult, ALU.add)
                        if j < 2:
                            dlink(ins)
                        else:
                            ins.then_inc(xc_ready, 1)

            @block.tensor
            def _(pe):
                s = R.take(pe)
                for m in range(4):
                    pe.wait_ge(xc_ready, m + 1)
                    for g in range(2):
                        bank = 2 * (m % 2) + g
                        if m >= 2:
                            pe.wait_ge(gates_done, 2 * (m - 2) + g + 1)
                        last = mm(PS[:, bank * 512:bank * 512 + 512], RINGT[:, s, (4 * g + m) * P:(4 * g + m + 1) * P], XC[:, m, :])
                        last.then_inc(rg_done, 1)
                mm(PS[:, 2048:2049], C("ident"), C("ident", 0, 1)).then_inc(blocks_done, 1)

            @block.scalar
            def _(a):
                act(RAW[:, 4:8, :], RAW[:, 4:8, :], ACT.Silu)
                act(RAW[:, 8:12, :], RAW[:, 8:12, :], ACT.Silu)
                act(RAW[:, 16:20, :], RAW[:, 16:20, :], ACT.Silu)
                for m in range(4):
                    for g in range(2):
                        a.wait_ge(rg_done, 2 * m + g + 1)
                        bank = 2 * (m % 2) + g
                        act((RG, IG)[g][:, m, :], PS[:, bank * 512:bank * 512 + 512], ACT.Sigmoid,
                            bias=V(("rg_ba", "rg_bx")[g], m)).then_inc(gates_done, 1)

        tanh_ready, root_asked, root_ready = sem("tanh_ready"), sem("root_asked"), sem("root_ready")
        with nc.Block() as block:
            @block.scalar
            def _(a):
                for m in range(4):
                    act(AG[:, m, :], RG[:, m, :], ACT.Exp, scale=SP8N[:, m:m + 1])
                    act(TH[:, m, :], RG[:, m, :], ACT.Tanh, scale=SP8[:, m:m + 1]).then_inc(tanh_ready, 1)
                for m in range(4):
                    a.wait_ge(root_asked, m + 1)
                    act(TH[:, m, :], TH[:, m, :], ACT.Sqrt).then_inc(root_ready, 1)

            @block.vector
            def _(v):
                for m in range(4):
                    v.wait_ge(tanh_ready, m + 1)
                    dlink(vtt(RG[:, m, :], AG[:, m, :], AG[:, m, :]))
                    stt(TH[:, m, :], RG[:, m, :], 1.0, TH[:, m, :], ALU.add, ALU.mult).then_inc(root_asked, 1)
                    dlink(vtt(IG[:, m, :], IG[:, m, :], XC[:, m, :]))
                for m in range(4):
                    v.wait_ge(root_ready, m + 1)
                    dlink(nc.vector.memset(TH[:, m, 0:1], 1.0))
                    dlink(vtt(IG[:, m, :], IG[:, m, :], TH[:, m, :]))
                    dlink(nc.vector.tensor_tensor_scan(XC[:, m, :], AG[:, m, :], IG[:, m, :], 0.0, ALU.mult, ALU.add))
                    dlink(vtt(Y1[:, m, :], XC[:, m, :], RAW[:, 4 + m, :]))

        SF, BC, EB, ENB, SM = XC, RG, IG, AG, TH
        Q, K = RAW[:, 8:12, :], RAW[:, 12:16, :]
        KT = SF
        ST = RAW[:, 0:8, :].rearrange("p a b -> p (a b)").rearrange("p (h n v) -> p h n v", h=4, n=NCX)
        CMASK = sq[:, 0, 0:TX]
        with nc.Block() as block:
            @block.scalar
            def _(a):
                act(EB, RAW[:, 12:16, :], ACT.Sigmoid)
                alink(act(K, K, ACT.Sigmoid, scale=-1.0))
                for m in range(4):
                    act(SF[:, m, :], EB[:, m, :], ACT.Ln, scale=OMLB[:, m:m + 1], bias=LB[:, m:m + 1])

            @block.vector
            def _(v):
                dlink(nc.vector.memset(CMASK, 1.0))
                dlink(nc.vector.memset(CMASK.rearrange("p (n t) -> p n t", t=CH)[:, :, 0:1], 0.0))
        with nc.Block() as block:
            @block.vector
            def _(v):
                for m in range(4):
                    dlink(nc.vector.tensor_tensor_scan(BC[:, m, :], CMASK, SF[:, m, :], 0.0, ALU.mult, ALU.add))
                for m in range(4):
                    dlink(vts(K[:, m, :], K[:, m, :], OMLB[:, m:m + 1]))
        BL = sq[:, 1, 0:32].rearrange('p (n o) -> p n o', o=1)
        b4 = BC.rearrange("p h (n t) -> p (h n) t", t=CH)
        eb_ready, db_ready, ed_ready = sem("eb_ready"), sem("db_ready"), sem("ed_ready")
        with nc.Block() as block:
            @block.scalar
            def _(a):
                act(EB, BC, ACT.Exp).then_inc(eb_ready, 1)
                act(ENB, BC, ACT.Exp, scale=-1.0).then_inc(eb_ready, 1)
                a.wait_ge(db_ready, 1)
                act(BC, BC, ACT.Exp).then_inc(ed_ready, 1)

            @block.vector
            def _(v):
                v.wait_ge(eb_ready, 2)
                dlink(nc.vector.tensor_copy(BL, b4[:, :, CH - 1:CH]))
                vtt(b4, BL.broadcast_to([P, 32, CH]), b4, ALU.subtract).then_inc(db_ready, 1)
                dlink(stt(Q, Q, float(P) ** -0.5, EB, ALU.mult, ALU.mult))
                dlink(vtt(ENB, ENB, K))
                v.wait_ge(ed_ready, 1)
                dlink(vtt(BC, BC, K))
        QE, KE, KD = Q, ENB, BC
        sc_done, sc_masked, kt_done, kt_read = (sem(n) for n in ("sc_done", "sc_masked", "kt_done", "kt_read"))
        gmask = C("gla_mask").rearrange("p (o t) -> p o t", o=1).broadcast_to([P, 4, P])
        with nc.Block() as block:
            @block.tensor
            def _(pe):
                for h in range(4):
                    for u in range(4):
                        last = mm(PS[:, h * 512 + u * P:h * 512 + u * P + P], KE[:, h, u * P:u * P + P], QE[:, h, u * P:u * P + P])
                    last.then_inc(sc_done, 1)
                    if h >= 2:
                        pe.wait_ge(kt_read, h - 1)
                    for u in range(4):
                        o = 2048 + (h % 2) * 512 + u * P
                        last = nc.tensor.transpose(PS[:, o:o + P], KD[:, h, u * P:u * P + P], C("ident"))
                    last.then_inc(kt_done, 1)

            @block.vector
            def _(v):
                for h in range(4):
                    v.wait_ge(sc_done, h + 1)
                    dlink(vtt(SM[:, h, :].rearrange("p (u t) -> p u t", u=4),
                              PS[:, h * 512:h * 512 + 512].rearrange("p (u t) -> p u t", u=4), gmask))

            @block.scalar
            def _(a):
                for h in range(4):
                    a.wait_ge(kt_done, h + 1)
                    o = 2048 + (h % 2) * 512
                    act(KT[:, h, :], PS[:, o:o + 512], ACT.Copy).then_inc(kt_read, 1)
        ds_done, st_ready, o_done = (sem(n) for n in ("ds_done", "st_ready", "o_done"))
        with nc.Block() as block:
            @block.tensor
            def _(pe):
                for h in range(4):
                    if h >= 1:
                        pe.wait_ge(st_ready, (NCX - 1) * h)
                    for e in range(2):
                        for u in range(4):
                            last = mm(PS[:, 2048 + e * 512 + u * P:2048 + e * 512 + u * P + P],
                                      KT[e * CH:e * CH + CH, h, u * P:u * P + P], VTOK[e * CH:e * CH + CH, u, h * P:h * P + P])
                        last.then_inc(ds_done, 1)
                for h in range(4):
                    pe.wait_ge(st_ready, (NCX - 1) * (h + 1))
                    for u in range(4):
                        o = PS[:, h * 512 + u * P:h * 512 + u * P + P]
                        mm(o, VTOK[:, u, h * P:h * P + P], SM[:, h, u * P:u * P + P], True, False)
                        for e in range(2):
                            n = 2 * u + e
                            last = mm(o[:, e * CH:e * CH + CH], ST[:, h, n, :], QE[:, h, n * CH:n * CH + CH], False, e == 1)
                    last.then_inc(o_done, 1)

            @block.vector
            def _(v):
                for h in range(4):
                    dlink(nc.vector.memset(ST[:, h, 0, :], 0.0))
                    v.wait_ge(ds_done, 2 * h + 2)
                    for n in range(NCX - 1):
                        o = 2048 + (n % 2) * 512 + (n // 2) * P
                        ins = stt(ST[:, h, n + 1, :], ST[:, h, n, :], EB[:, h, n * CH + CH - 1:n * CH + CH], PS[:, o:o + P], ALU.mult, ALU.add)
                        ins.then_inc(st_ready, 1)
                        v.wait_ge(st_ready, h * (NCX - 1) + n + 1)

            @block.scalar
            def _(a):
                for h in range(4):
                    a.wait_ge(o_done, h + 1)
                    act(KE[:, h, :], PS[:, h * 512:h * 512 + 512], ACT.Copy)
        O = KE
        osq, orst = SM, KD
        osq_ready, osum = sem('osq_ready'), sem('osum')
        with nc.Block() as block:
            @block.scalar
            def _(a):
                act(osq, O, ACT.Square).then_inc(osq_ready, 1)
                a.wait_ge(osum, 4)
                alink(act(orst, PS[:, 0:2048].rearrange("p (h t) -> p h t", h=4), ACT.Ln, scale=1.0 / P, bias=EPSC[EPS]))
                act(orst, orst, ACT.Exp, scale=-0.5).then_inc(osq_ready, 1)

            @block.tensor
            def _(pe):
                pe.wait_ge(osq_ready, 1)
                for h in range(4):
                    mm(PS[:, h * 512:h * 512 + 512], C("ones"), osq[:, h, :]).then_inc(osum, 1)

            @block.vector
            def _(v):
                v.wait_ge(osum, 4)
                dlink(stt(O, O, V("hg_norm_w"), RAW[:, 16:20, :], ALU.mult, ALU.mult))
                v.wait_ge(osq_ready, 2)
                dlink(vtt(Y1[:, 4:8, :], O, orst))

        def add_products(stage, rhs, width, gate):
            freed = sem("freed")
            halves = [(0, TX, 0), (TX, TT, 1)][:1 if width == TX else 2]
            with nc.Block() as block:
                @block.sync
                def _(sp):
                    R.supply(sp, RINGT, weights, START[stage] + 8 + SLOTS)

                @block.tensor
                def _(pe):
                    for m in range(DT):
                        if m >= 2:
                            pe.wait_ge(freed, len(halves) * (m - 1))
                        tile_product(pe, PS[:, (m % 2) * 1024:(m % 2) * 1024 + width], rhs, width)

                @block.vector
                def _(v):
                    for m in range(DT):
                        v.wait_ge(blocks_done, START[stage] + m + 1)
                        for a, b, c in halves:
                            p = PS[:, (m % 2) * 1024 + a:(m % 2) * 1024 + b]
                            if gate is None:
                                vtt(X[:, m, a:b], p, X[:, m, a:b], ALU.add).then_inc(freed, 1)
                            else:
                                stt(X[:, m, a:b], p, gate(m, c), X[:, m, a:b], ALU.mult, ALU.add).then_inc(freed, 1)

        add_products("out1", [Y1[:, k, :] for k in range(DT)], TX, None)

        take = carve()
        H = take(DT, TX)
        PE_ = take(2, TX)
        GT = take(DT, TX)
        sq = take(2, TT)
        RST = take(TT)
        norm_stats([X[:, k, 0:TX] for k in range(DT)], TX, "ones", 1.0 / D, EPS, RST[:, 0:TX],
                   [sq[:, 0, 0:TX], sq[:, 1, 0:TX]], PS)
        with nc.Block() as block:
            @block.sync
            def _(sp):
                sp.dma_start(PE_, pT.rearrange("(k p) t -> p k t", p=P)).then_inc(loads, 16)
                sp.wait_ge(loads, 80)

            @block.vector
            def _(v):
                for k in range(DT):
                    stt(H[:, k, :], X[:, k, 0:TX], V("ple_norm_w", k), RST[:, 0:TX])
        g_read, p_done, p_added = sem("g_read"), sem("p_done"), sem("p_added")
        gated = Chain(sem("gated"))
        with nc.Block() as block:
            @block.sync
            def _(sp):
                R.supply(sp, RINGT, weights, START["conv0"] + SLOTS)

            @block.tensor
            def _(pe):
                for m in range(DT):
                    if m >= 2:
                        pe.wait_ge(g_read, m - 1)
                    tile_product(pe, PS[:, (m % 2) * 512:(m % 2) * 512 + 512], [H[:, k, :] for k in range(DT)], TX)
                for half in range(2):
                    s = R.take(pe)
                    for j in range(4):
                        m = 4 * half + j
                        if m >= 2:
                            pe.wait_ge(p_added, m - 1)
                        for k in range(2):
                            last = mm(PS[:, 1024 + (m % 2) * 512:1536 + (m % 2) * 512],
                                      RINGT[:, s, (2 * j + k) * P:(2 * j + k + 1) * P], PE_[:, k, :], k == 0, k == 1)
                        last.then_inc(p_done, 1)
                    mm(PS[:, 2048:2049], C("ident"), C("ident", 0, 1)).then_inc(blocks_done, 1)

            @block.scalar
            def _(a):
                for m in range(DT):
                    a.wait_ge(blocks_done, START["gate1"] + m + 1)
                    act(GT[:, m, :], PS[:, (m % 2) * 512:(m % 2) * 512 + 512], ACT.Sigmoid, bias=V("b_ple_gate", m)).then_inc(g_read, 1)

            @block.vector
            def _(v):
                for m in range(DT):
                    v.wait_ge(g_read, m + 1)
                    v.wait_ge(p_done, m + 1)
                    vtt(GT[:, m, :], PS[:, 1024 + (m % 2) * 512:1536 + (m % 2) * 512], GT[:, m, :]).then_inc(p_added, 1)
                    v.wait_ge(p_added, m + 1)
                    dlink(vtt(X[:, m, 0:TX], X[:, m, 0:TX], GT[:, m, :], ALU.add))
        norm_stats([X[:, k, 0:TX] for k in range(DT)], TX, "ones", 1.0 / D, EPS, RST[:, 0:TX],
                   [sq[:, 0, 0:TX], sq[:, 1, 0:TX]], PS)
        with nc.Block() as block:
            @block.vector
            def _(v):
                for k in range(DT):
                    stt(X[:, k, 0:TX], X[:, k, 0:TX], V("final_norm_w", k), RST[:, 0:TX])

        def conv_layer(layer, j_, width, next_mod):
            take = carve()
            H = take(DT, TT)
            YP = take(DT, YW)
            G = take(DT, TT)
            Z = take(DT, TT)
            sa, sb_ = take(2, TT), take(2, TT)
            sq = take(2, TT)
            RST = take(TT)
            ME = sa[:, 0, :]
            halves = [(0, TX, 0), (TX, TT, 1)][:1 if width == TX else 2]
            yoff = (PAD, XW + PAD)
            layer_input(layer, (H[:, :, 0:TX], H[:, :, TX:TT]), width, sq, RST)
            stage = f"conv{j_}"
            y_ready, a_read, b_read, g_read, s_free = (sem(n) for n in ("y_ready", "a_read", "b_read", "g_read", "s_free"))
            step = 2 if next_mod is not None else 1
            nh = len(halves)
            with nc.Block() as block:
                @block.sync
                def _(sp):
                    R.supply(sp, RINGT, weights, START[f"convout{j_}"] + SLOTS)

                @block.tensor
                def _(pe):
                    for m in range(DT):
                        for part, read in enumerate((a_read, b_read, g_read)):
                            if m >= 1:
                                pe.wait_ge(read, m)
                            tile_product(pe, PS[:, part * 1024:part * 1024 + width], [H[:, k, :] for k in range(DT)], width)
                            if next_mod is not None:
                                mod_block(pe, 3 * m + part)

                @block.scalar
                def _(a):
                    for m in range(DT):
                        base = START[stage] + step * 3 * m + 1
                        if m >= 2:
                            a.wait_ge(s_free, nh * (m - 1))
                        a.wait_ge(blocks_done, base)
                        act(sa[:, m % 2, 0:width], PS[:, 0:width], ACT.Copy).then_inc(a_read, 1)
                        a.wait_ge(blocks_done, base + step)
                        act(sb_[:, m % 2, 0:width], PS[:, 1024:1024 + width], ACT.Sigmoid).then_inc(b_read, 1)
                        a.wait_ge(blocks_done, base + 2 * step)
                        act(G[:, m, 0:width], PS[:, 2048:2048 + width], ACT.Silu).then_inc(g_read, 1)

                @block.gpsimd
                def _(g):
                    plink(nc.gpsimd.memset(YP, 0.0))
                    for m in range(DT):
                        g.wait_ge(a_read, m + 1)
                        g.wait_ge(b_read, m + 1)
                        for (a, b, c) in halves:
                            nc.gpsimd.tensor_tensor(YP[:, m, yoff[c]:yoff[c] + b - a], sa[:, m % 2, a:b], sb_[:, m % 2, a:b], ALU.mult).then_inc(s_free, 1)

                @block.vector
                def _(v):
                    for m in range(DT):
                        v.wait_ge(s_free, nh * (m + 1))
                        pieces = [(0, TX, yoff[0]), (TX, TT, yoff[1])] if nh == 2 else [(0, TX // 2, yoff[0]), (TX // 2, TX, yoff[0] + TX // 2)]
                        for t in range(TAPS):
                            for n, (a, b, y) in enumerate(pieces):
                                src = YP[:, m, y + t - PAD:y + t - PAD + b - a]
                                wt = V("conv_dw_2", (j_ * TAPS + t) * DT + m)
                                if t == 0:
                                    ins = vts(Z[:, m, a:b], src, wt, V("conv_db_2", j_ * DT + m), ALU.mult, ALU.add)
                                else:
                                    if n == 0:
                                        dve_chain.wait(v)
                                    ins = stt(Z[:, m, a:b], src, wt, Z[:, m, a:b], ALU.mult, ALU.add)
                                dve_chain.inc(ins)
                        dve_chain.wait(v)

            z_summed, centred = sem("z_summed"), sem("centred")
            with nc.Block() as block:
                @block.tensor
                def _(pe):
                    for k in range(DT):
                        last = product(PS, C("ones"), Z[:, k, :], width, k == 0, k == DT - 1)
                    last.then_inc(z_summed, 1)

                @block.scalar
                def _(a):
                    a.wait_ge(z_summed, 1)
                    act(ME[:, 0:width], PS[:, 0:width], ACT.Copy, scale=1.0 / D).then_inc(centred, 1)

                @block.vector
                def _(v):
                    if next_mod is not None:
                        mod_finish(next_mod)
                    v.wait_ge(centred, 1)
                    for k in range(DT):
                        dlink(vtt(Z[:, k, 0:width], Z[:, k, 0:width], ME[:, 0:width], ALU.subtract))
            norm_stats([Z[:, k, 0:width] for k in range(DT)], width, "ones", 1.0 / D, LN_EPS, RST[:, 0:width],
                       [sq[:, 0, 0:width], sq[:, 1, 0:width]], PS)
            scaled, silued = sem("scaled"), sem("silued")
            with nc.Block() as block:
                @block.vector
                def _(v):
                    for k in range(DT):
                        vtt(Z[:, k, 0:width], Z[:, k, 0:width], RST[:, 0:width]).then_inc(scaled, 1)
                        if k >= 1:
                            v.wait_ge(silued, k)
                            vtt(Z[:, k - 1, 0:width], Z[:, k - 1, 0:width], G[:, k - 1, 0:width])
                    v.wait_ge(silued, DT)
                    dlink(vtt(Z[:, DT - 1, 0:width], Z[:, DT - 1, 0:width], G[:, DT - 1, 0:width]))

                @block.scalar
                def _(a):
                    for k in range(DT):
                        a.wait_ge(scaled, k + 1)
                        act(Z[:, k, 0:width], Z[:, k, 0:width], ACT.Silu, scale=V("conv_ln_g_2", j_ * DT + k),
                            bias=V("conv_ln_b_2", j_ * DT + k)).then_inc(silued, 1)
            add_products(f"convout{j_}", [Z[:, k, :] for k in range(DT)], width,
                         lambda m, c: MODL[:, layer, 16 + m, c:c + 1])

        conv_layer(0, 0, TT, 1)

        take = carve()
        HP = take(DT, TT + 4)
        XX = take(DT, TT)
        L2 = take(2, DT, TT)
        sq = L2[:, 0, 0:2, :]
        RST = L2[:, 0, 2, :]
        STG = take(4, TT)
        TW, TA = take(TT), take(TT)
        HALF = [(0, TX, 0), (TX, TT, 1)]
        hoff = (1, TX + 3)
        HH = (HP[:, :, 1:1 + TX], HP[:, :, TX + 3:TX + 3 + TC])
        layer_input(1, HH, TT, sq, RST)
        with nc.Block() as block:
            @block.vector
            def _(v):
                for z in (0, TX + 1, TX + 2, TX + TC + 3):
                    dlink(nc.vector.memset(HP[:, :, z:z + 1], 0.0))
                for a, b, c in HALF:
                    n, o = b - a, hoff[c]
                    dlink(vtt(XX[:, :, a:b], HP[:, :, o - 1:o - 1 + n], HP[:, :, o + 1:o + 1 + n], ALU.add))
                    dlink(stt(XX[:, :, a:b], XX[:, :, a:b], 0.5, HP[:, :, o:o + n], ALU.mult, ALU.subtract))

        lerps = [1, 4, 0, 2, 3, 5]
        l_ready = sem("l_ready")
        l_used, ev = sem("l_used"), sem("ev")
        slot_stored = [sem(f"slot_stored{s}") for s in range(4)]
        t_ready = sem("t_ready")
        outs = [("lora", 0), ("lora", 1)]
        outs += [("w", d, m) for m in range(DT) for d in range(2)]
        outs += [("a", d, m) for m in range(DT) for d in range(2)]
        outs += [("rkvg"[q], q, m) for q in range(4) for m in range(DT)]
        prod = sem("prod")
        NO = len(outs)
        with nc.Block() as block:
            @block.sync
            def _(sp):
                R.supply(sp, RINGT, weights, START["rwkvout"] + SLOTS)

            @block.vector
            def _(v):
                for n, mu in enumerate(lerps):
                    if n >= 2:
                        v.wait_ge(l_used, n - 1)
                    for k in range(DT):
                        for a, b, c in HALF:
                            ins = stt(L2[:, n % 2, k, a:b], XX[:, k, a:b], V("rwkv_mu_2", mu * DT + k),
                                      HP[:, k, hoff[c]:hoff[c] + b - a], ALU.mult, ALU.add)
                            ins.then_inc(l_ready, 1)

            @block.tensor
            def _(pe):
                done = 0

                def area(n):
                    return PS[:, (n % 3) * 1024:(n % 3) * 1024 + TT]

                for n in range(2):
                    pe.wait_ge(l_ready, 16 * (n + 1))
                    s = R.take(pe)
                    w = RINGT[:, s, :].rearrange("p (k m) -> p k m", k=DT)
                    for k in range(DT):
                        last = product(area(n), w[:, k, :], L2[:, n, k, :], TT, k == 0, k == DT - 1)
                    last.then_inc(prod, 1)
                    pe.wait_ge(prod, n + 1)
                    pe.nop().then_inc(blocks_done, 1)
                    pe.nop().then_inc(l_used, 1)
                done = 2
                for kind, T_ in (("w", TW), ("a", TA)):
                    s = R.take(pe)
                    for m in range(DT):
                        for d in range(2):
                            pe.wait_ge(ev, done - 1 if done - 1 > 2 else 2)
                            last = product(area(done), RINGT[d * 64:d * 64 + 64, s, m * P:m * P + P], T_[d * 64:d * 64 + 64, :], TT, True, True)
                            last.then_inc(prod, 1)
                            done += 1
                            pe.wait_ge(prod, done)
                    pe.nop().then_inc(blocks_done, 1)
                for q in range(4):
                    pe.wait_ge(l_ready, 16 * (q + 3))
                    for m in range(DT):
                        pe.wait_ge(ev, done - 2)
                        s = R.take(pe)
                        w = RINGT[:, s, :].rearrange("p (k m) -> p k m", k=DT)
                        for k in range(DT):
                            last = product(area(done), w[:, k, :], L2[:, q % 2, k, :], TT, k == 0, k == DT - 1)
                        last.then_inc(prod, 1)
                        done += 1
                        pe.wait_ge(prod, done)
                        pe.nop().then_inc(blocks_done, 1)
                        if q * DT + m < 24:
                            mod_block(pe, q * DT + m)
                    pe.nop().then_inc(l_used, 1)

            @block.scalar
            def _(a):
                for n, o in enumerate(outs):
                    a.wait_ge(prod, n + 1)
                    src = PS[:, (n % 3) * 1024:(n % 3) * 1024 + TT]
                    if o[0] == "lora":
                        act((TW, TA)[o[1]], src, (ACT.Tanh, ACT.Copy)[o[1]]).then_inc(ev, 1)
                        continue
                    sl = (n - 2) % 4
                    if n >= 6:
                        a.wait_ge(slot_stored[sl], 16 * ((n - 2) // 4))
                    kind, q, m = o
                    if kind in "wa":
                        ins = act(STG[:, sl, :], src, ACT.Sigmoid, bias=V({"w": "rwkv_w0_2", "a": "rwkv_a0_2"}[kind], q * DT + m))
                        at = (4 if kind == "w" else 6) + q
                    else:
                        ins = act(STG[:, sl, :], src, ACT.Silu if kind == "g" else ACT.Copy)
                        at = q
                    ins.then_inc(ev, 1)
                    a.wait_ge(ev, n + 1)
                    a.dma_start(rwkv_dram[m, at], STG[:, sl, :]).then_inc(slot_stored[sl], 16)

        with nc.Block() as block:
            @block.sync
            def _(sp):
                for sl in range(4):
                    sp.wait_ge(slot_stored[sl], 16 * ((NO - 2) // 4))
                sp.dma_start(x_dram, X.rearrange("p k t -> p (k t)")).then_inc(stores, 16)
                sp.wait_ge(stores, 16)

            @block.vector
            def _(v):
                mod_finish(2)

        take = carve()
        GM = take(NU, 2, P)
        TINV = take(NU, P)
        BKT = take(NU, 2, CH)
        UV = take(NU, 2, CH)
        AV = take(NU, CH)
        AR = take(NU, 2, CH)
        BK = take(NU, 2, CH)
        VS = take(TT + 2 * CH)
        GS, BON = take(TT), take(TT)
        EBC = take(NU)
        S2, S3 = take(2, CH), take(2, CH)
        RS2 = take(2, CH)
        PC = take(8)
        free_x = X.rearrange("p k t -> p (k t)")
        IN = free_x.rearrange("p (q t) -> p q t", q=8)
        TALL = take(7, TT)
        T = [TALL[:, n, :] for n in range(7)]
        O2 = TALL[:, 3:5, :]
        grp = []
        for _ in range(2):
            grp.append({n: take(4, P) for n in ("ATB", "PQ", "PT", "T1", "NT0", "NT1")})
        CM = take(2, TT)

        def runs(d):
            return slice(NSTEP * d, NSTEP * d + NSTEP)

        loaded, taken = sem("pair_loaded"), sem("pair_taken")
        wk = {n: sem(n) for n in ("kk_sq", "kk_sum", "e_done", "b_done", "g_mm", "g_ev", "tr_mm", "tr_ev",
                                  "nt", "t1_mm", "t1_ev", "p_mm", "p_ev", "ab_mm", "ab_ev", "init",
                                  "r_mm", "r_ev", "u_mm", "u_lo", "u_hi", "s_mm", "s_ev", "o_mm", "o_ev",
                                  "ro_mm", "ro_v", "ro_a", "y_store", "u_mm2", "e2", "c_lo", "c_hi", "s2_mm", "o2_mm", "ro_s")}
        y_out = sem("y_out")
        with nc.Block() as block:
            @block.vector
            def _(v):
                nc.vector.memset(CM, 1.0)
                nc.vector.memset(VS, 0.0)
                for g in grp:
                    dlink(nc.vector.memset(g["ATB"], 0.0))
                c4 = CM.rearrange("p d (n t) -> p d n t", t=CH)
                dlink(nc.vector.memset(c4[:, 0, :, 0:1], 0.0))
                dlink(nc.vector.memset(c4[:, 1, :, CH - 1:CH], 0.0))

            @block.sync
            def _(sp):
                sp.dma_start(IN, rwkv_dram[0].rearrange("q p t -> p q t")).then_inc(loaded, 16)
                sp.dma_start(rwkv_dram[DT], rwkv_dram[0]).then_inc(y_out, 16)

        PREP_V, INV_V = 36, 4 * 6
        with nc.Fori(0, NPAIR) as i:
            with nc.Block() as block:
                @block.gpsimd
                def _(g):
                    for s in wk.values():
                        g.sem_clear(s)

            with nc.Block() as block:
                KK, A_, B_, C_, D_, E__, F_ = T

                @block.vector
                def _(v):
                    ch = Chain(wk["nt"])
                    def L(ins):
                        ch.link(v, ins)
                    v.wait_ge(loaded, i * 16 + 16)
                    for q, (n, k) in enumerate((("rwkv_k_k_2", 0), ("rwkv_k_a_2", 0), ("rwkv_r_k_2", 0), ("rwkv_ln_g_2", 0), ("rwkv_ln_b_2", 0))):
                        L(nc.vector.tensor_copy(PC[:, q:q + 1], VEC[:, bass.ds(i + VT[n][0], 1)]))
                    L(vts(PC[:, 5:6], PC[:, 1:2], -1.0, 1.0, ALU.mult, ALU.add))
                    vts(KK, IN[:, 1, :], PC[:, 0:1]).then_inc(wk["kk_sq"], 1)
                    L(nc.vector.tensor_copy(VS[:, CH:CH + TT], IN[:, 2, :]))
                    L(nc.vector.tensor_copy(GS, IN[:, 3, :]))
                    v.wait_ge(wk["kk_sum"], 2)
                    L(vtt(KK, KK, A_))
                    for d in range(2):
                        sl = slice(NSTEP * d, NSTEP * d + NSTEP)
                        r3 = lambda t: t.rearrange("p (n t) -> p n t", t=CH)
                        L(vts(B_, IN[:, 4 + d, :], -float(np.exp(-0.5))))
                        if d == 0:
                            L(nc.vector.tensor_tensor_scan(C_, CM[:, 0, :], B_, 0.0, ALU.mult, ALU.add))
                        else:
                            L(nc.vector.tensor_tensor_scan(C_[:, ::-1], CM[:, 1, ::-1], B_[:, ::-1], 0.0, ALU.mult, ALU.add))
                        vtt(B_, C_, B_, ALU.subtract).then_inc(wk["b_done"], 1)
                        L(vts(A_, IN[:, 6 + d, :], PC[:, 1:2], PC[:, 5:6], ALU.mult, ALU.add))
                        L(vtt(A_, A_, IN[:, 1, :]))
                        if d == 0:
                            L(nc.vector.tensor_copy(BON, A_))
                        else:
                            L(vtt(BON, BON, A_, ALU.add))
                        v.wait_ge(wk["e_done"], 3 * d + 3)
                        L(vtt(AR[:, sl, 1, :], r3(IN[:, 0, :]), r3(D_)))
                        L(stt(AR[:, sl, 0, :], r3(KK), -1.0, r3(F_), ALU.mult, ALU.mult))
                        for h in range(2):
                            hs = slice(64 * h, 64 * h + 64)
                            L(vtt(BK[hs, sl, 1 - h, :], r3(A_)[hs], r3(E__)[hs]))
                        L(vtt(A_, KK, IN[:, 6 + d, :]))
                        for h in range(2):
                            hs = slice(64 * h, 64 * h + 64)
                            L(vtt(BK[hs, sl, h, :], r3(A_)[hs], r3(E__)[hs]))
                        at = CH - 1 if d == 0 else 0
                        L(nc.vector.tensor_copy(EBC[:, sl].rearrange("p (n o) -> p n o", o=1), r3(D_)[:, :, at:at + 1]))
                    ch.inc(stt(BON, IN[:, 0, :], PC[:, 2:3], BON, ALU.mult, ALU.mult))
                    assert ch.n == PREP_V, ch.n

                @block.scalar
                def _(a):
                    a.wait_ge(wk["kk_sq"], 1)
                    act(B_, KK, ACT.Square).then_inc(wk["kk_sq"], 1)
                    a.wait_ge(wk["g_mm"], 1)
                    act(A_, PS[:, 0:TT], ACT.Ln, bias=TINY[:, 3:4]).then_inc(wk["kk_sum"], 1)
                    a.wait_ge(wk["kk_sum"], 1)
                    act(A_, A_, ACT.Exp, scale=-0.5).then_inc(wk["kk_sum"], 1)
                    for d in range(2):
                        a.wait_ge(wk["b_done"], d + 1)
                        act(F_, B_, ACT.Exp).then_inc(wk["e_done"], 1)
                        act(D_, C_, ACT.Exp).then_inc(wk["e_done"], 1)
                        act(E__, C_, ACT.Exp, scale=-1.0).then_inc(wk["e_done"], 1)

                @block.tensor
                def _(pe):
                    pe.wait_ge(wk["kk_sq"], 2)
                    product(PS[:, 0:TT], C("ones64"), B_, TT, True, True).then_inc(wk["g_mm"], 1)

            NG = NU // 4
            with nc.Block() as block:
                @block.sync
                def _(sp):
                    sp.wait_ge(y_out, i * 16 + 16)
                    sp.dma_start(IN, rwkv_dram[bass.ds(i + 1, 1)].rearrange("a q p t -> p (a q) t")).then_inc(loaded, 16)

                @block.tensor
                def _(pe):
                    for g in range(NG):
                        for h in range(2):
                            n = 2 * g + h
                            if n >= 4:
                                pe.wait_ge(wk["g_ev"], n - 3)
                            bank = (g % 2) * 2 + h
                            for q in range(4):
                                u = 4 * g + q
                                rows = slice(64 * h, 64 * h + 64)
                                o = 1 if h == 0 else -1
                                l, r = BK[rows, u].rearrange('p s t -> p (s t)'), AR[rows, u, ::o, :]
                                last = mm(PS[:, bank * 512 + q * P:bank * 512 + q * P + P], l, r)
                            last.then_inc(wk["tr_mm"], 1)
                    for rnd in range(2):
                        n = 8 if rnd == 0 else 4
                        for h in range(2):
                            rows = slice(64 * h, 64 * h + 64)
                            for c in range(n):
                                cc = 8 * rnd + c
                                last = nc.tensor.transpose(PS[:, 2048 + (2 * rnd + h) * 512 + c * CH:2048 + (2 * rnd + h) * 512 + (c + 1) * CH],
                                                           VS[rows, (cc + h) * CH:(cc + h) * CH + P], CON[rows, CT["ident"][0] + 64 * h:CT["ident"][0] + 64 * h + 64])
                            last.then_inc(wk["ab_mm"], 1)

                @block.vector
                def _(v):
                    for g in range(NG):
                        d = g // (NG // 2)
                        for h in range(2):
                            n = 2 * g + h
                            v.wait_ge(wk["tr_mm"], n + 1)
                            bank = (g % 2) * 2 + h
                            m = C("wkv_mask", d * 256 + h * P, P).rearrange("p (o t) -> p o t", o=1).broadcast_to([P, 4, P])
                            vtt(GM[:, 4 * g:4 * g + 4, h, :], PS[:, bank * 512:bank * 512 + 512].rearrange("p (q t) -> p q t", q=4), m).then_inc(wk["g_ev"], 1)
                    v.wait_ge(wk["tr_mm"], 2 * NG)
                    e = EBC.rearrange("p (n o) -> p n o", o=1).broadcast_to([P, NU, P])
                    b = BK.rearrange("p n s t -> p n (s t)")
                    vtt(b, b, e).then_inc(wk["init"], 1)
                    pass

                @block.scalar
                def _(a):
                    for rnd in range(2):
                        n = 8 if rnd == 0 else 4
                        for h in range(2):
                            a.wait_ge(wk["ab_mm"], 2 * rnd + h + 1)
                            src = PS[:, 2048 + (2 * rnd + h) * 512:2048 + (2 * rnd + h) * 512 + n * CH].rearrange("p (c t) -> p c t", t=CH)
                            for d in range(2):
                                act(UV[:, NSTEP * d + 8 * rnd:NSTEP * d + 8 * rnd + n, h, :], src, ACT.Copy)

            with nc.Block() as block:
                @block.tensor
                def _(pe):
                    for rnd in range(3):
                        for h in range(2):
                            rows = slice(64 * h, 64 * h + 64)
                            for q in range(8):
                                u = 8 * rnd + q
                                a_ = (2 * rnd + h) * 512 + q * CH
                                last = nc.tensor.transpose(PS[:, a_:a_ + CH], BK[rows, u].rearrange('p s t -> p (s t)'), CON[rows, CT["ident"][0] + 64 * h:CT["ident"][0] + 64 * h + 64])
                            last.then_inc(wk["s_mm"], 1)
                    for rnd in range(3):
                        bank = 6 + rnd if rnd < 2 else 0
                        if rnd == 2:
                            pe.wait_ge(wk["s_ev"], 1)
                        for q in range(8):
                            u = 8 * rnd + q
                            for h in range(2):
                                kr = slice(64, 128) if h == 0 else slice(0, 64)
                                last = mm(PS[64 * h:64 * h + 64, bank * 512 + q * CH:bank * 512 + (q + 1) * CH],
                                          GM[kr, u, h, 64 * h:64 * h + 64], UV[kr, u, h, :])
                        last.then_inc(wk["r_mm"], 1)

                @block.scalar
                def _(a):
                    for rnd in range(3):
                        for h in range(2):
                            a.wait_ge(wk["s_mm"], 2 * rnd + h + 1)
                            src = PS[:, (2 * rnd + h) * 512:(2 * rnd + h + 1) * 512].rearrange("p (c t) -> p c t", t=CH)
                            act(BKT[:, 8 * rnd:8 * rnd + 8, h, :], src, ACT.Copy).then_inc(wk["s_ev"], 1)

                @block.vector
                def _(v):
                    for rnd in range(3):
                        v.wait_ge(wk["r_mm"], rnd + 1)
                        bank = 6 + rnd if rnd < 2 else 0
                        nc.vector.tensor_copy(AV[:, 8 * rnd:8 * rnd + 8, :], PS[:, bank * 512:bank * 512 + 512].rearrange("p (c t) -> p c t", t=CH))

            NSUP = NG // 2
            identb = C("ident").rearrange("p (o t) -> p o t", o=1).broadcast_to([P, 4, P])

            def maskb(level):
                return C("inv_mask", level * P, P).rearrange("p (o t) -> p o t", o=1).broadcast_to([P, 4, P])

            def bank(n):
                return PS[:, n * 512:n * 512 + 512]

            def bank3(n):
                return bank(n).rearrange("p (q t) -> p q t", q=4)

            with nc.Block() as block:
                @block.tensor
                def _(pe):
                    for s in range(NSUP):
                        for e in range(2):
                            n = 2 * s + e
                            pe.wait_ge(wk["y_store"], n + 1)
                            if s >= 1:
                                pe.wait_ge(wk["o_ev"], (s * 2) * 5)
                            for q in range(4):
                                last = nc.tensor.transpose(bank(3 * e)[:, q * P:q * P + P], grp[e]["ATB"][:, q, :], C("ident"))
                            last.then_inc(wk["u_mm"], 1)
                        for lv in range(5):
                            for e in range(2):
                                n = (s * 5 + lv) * 2 + e
                                g = grp[e]
                                pe.wait_ge(wk["t1_ev"], n + 1)
                                pe.wait_ge(wk["o_mm"], n + 1)
                                for q in range(4):
                                    last = mm(bank(3 * e)[:, q * P:q * P + P], g["NT" + str(lv % 2)][:, q, :], g["PQ"][:, q, :])
                                last.then_inc(wk["t1_mm"], 1)
                            for e in range(2):
                                n = (s * 5 + lv) * 2 + e
                                g = grp[e]
                                pe.wait_ge(wk["p_mm"], n + 1)
                                for q in range(4):
                                    last = mm(bank(3 * e + 1)[:, q * P:q * P + P], g["T1"][:, q, :], g["PT"][:, q, :])
                                if lv < 4:
                                    for q in range(4):
                                        last = mm(bank(3 * e + 2)[:, q * P:q * P + P], g["PT"][:, q, :], g["T1"][:, q, :])
                                last.then_inc(wk["p_ev"], 1)

                @block.gpsimd
                def _(gp):
                    for s in range(NSUP):
                        for lv in range(5):
                            for e in range(2):
                                n = (s * 5 + lv) * 2 + e
                                if lv == 0:
                                    gp.wait_ge(wk["y_store"], 2 * s + e + 1)
                                if n >= 4:
                                    gp.wait_ge(wk["t1_mm"], n - 3)
                                nc.gpsimd.tensor_tensor(grp[e]["NT" + str(lv % 2)], grp[e]["ATB"], maskb(lv + 1), ALU.mult).then_inc(wk["t1_ev"], 1)

                @block.scalar
                def _(a):
                    for s in range(NSUP):
                        for lv in range(5):
                            for e in range(2):
                                n = (s * 5 + lv) * 2 + e
                                a.wait_ge(wk["t1_mm"], n + 1)
                                act(grp[e]["T1"], bank3(3 * e), ACT.Copy).then_inc(wk["p_mm"], 1)

                @block.vector
                def _(v):
                    ch = Chain(wk["u_lo"])
                    for s in range(NSUP):
                        for e in range(2):
                            n = 2 * s + e
                            g = grp[e]
                            if s >= 1:
                                v.wait_ge(wk["t1_ev"], s * 10)
                            us = slice(4 * n, 4 * n + 4)
                            ch.link(v, nc.vector.tensor_copy(g["ATB"][0:64, :, 0:64], GM[0:64, us, 0, 0:64]))
                            nc.vector.tensor_copy(g["ATB"][64:128, :, 64:128], GM[64:128, us, 1, 64:128]).then_inc(wk["y_store"], 1)
                        for e in range(2):
                            n = 2 * s + e
                            g = grp[e]
                            v.wait_ge(wk["y_store"], n + 1)
                            ch.link(v, vtt(g["PT"], g["ATB"], maskb(0)))
                            ch.link(v, vtt(g["PT"], g["PT"], identb, ALU.add))
                            v.wait_ge(wk["u_mm"], n + 1)
                            ch.link(v, vtt(g["PQ"], bank3(3 * e), maskb(0)))
                            vtt(g["PQ"], g["PQ"], identb, ALU.add).then_inc(wk["o_mm"], 1)
                        for lv in range(5):
                            for e in range(2):
                                n = (s * 5 + lv) * 2 + e
                                g = grp[e]
                                v.wait_ge(wk["p_ev"], n + 1)
                                if lv == 4:
                                    us = slice(4 * (2 * s + e), 4 * (2 * s + e) + 4)
                                    vtt(TINV[:, us, :], bank3(3 * e + 1), g["PT"], ALU.add).then_inc(wk["o_ev"], 1)
                                    continue
                                vtt(g["PT"], bank3(3 * e + 1), g["PT"], ALU.add).then_inc(wk["o_ev"], 1)
                                vtt(g["PQ"], bank3(3 * e + 2), g["PQ"], ALU.add).then_inc(wk["o_mm"], 1)
                    assert ch.n == INV_V, ch.n

            with nc.Block() as block:
                def units(step):
                    cf, cr = (NCX + step) % NSTEP, NSTEP - 1 - step
                    return cf, cr, (cf, NSTEP + cr)

                def both(t, step, *rest):
                    u0, u1 = units(step)[2]
                    return t[(slice(None) if not rest else rest[0], slice(u0, u1 + 1, u1 - u0)) + rest[1:]]

                @block.tensor
                def _(pe):
                    for st in range(NSTEP):
                        us = units(st)[2]
                        b0 = 4 * (st % 2)
                        S = S2 if st % 2 == 0 else S3
                        pe.wait_ge(wk["u_hi"], st + 1)
                        for d in range(2):
                            for h in range(2):
                                hs = slice(64 * h, 64 * h + 64)
                                last = mm(bank(b0)[hs, d * CH:d * CH + CH], AR[hs, us[d], 0, :], S[hs, d, :])
                        last.then_inc(wk["u_mm2"], 1)
                        pe.wait_ge(wk["r_ev"], st + 1)
                        for d in range(2):
                            last = mm(bank(b0 + 1)[:, d * CH:d * CH + CH], TINV[:, us[d], :], RS2[:, d, :])
                        last.then_inc(wk["e2"], 1)
                        if st >= 1:
                            pe.wait_ge(wk["ro_a"], 2 * st)
                        pe.wait_ge(wk["c_lo"], st + 1)
                        pe.wait_ge(wk["c_hi"], st + 1)
                        for d in range(2):
                            for h in range(2):
                                hs = slice(64 * h, 64 * h + 64)
                                last = mm(bank(b0 + 2)[hs, d * CH:d * CH + CH], BKT[:, us[d], h, :], UV[:, us[d], h, :])
                        last.then_inc(wk["s2_mm"], 1)
                        for d in range(2):
                            for h in range(2):
                                hs = slice(64 * h, 64 * h + 64)
                                rc = slice(64, 128) if h == 0 else slice(0, 64)
                                mm(bank(b0 + 3)[hs, d * CH:d * CH + CH], UV[:, us[d], h, :], GM[:, us[d], h, rc], True, False)
                                last = mm(bank(b0 + 3)[hs, d * CH:d * CH + CH], S[hs, d, :], AR[hs, us[d], 1, :], False, True)
                        last.then_inc(wk["o2_mm"], 1)

                @block.vector
                def _(v):
                    nc.vector.memset(S2, 0.0).then_inc(wk["u_hi"], 1)
                    for st in range(NSTEP):
                        us = units(st)[2]
                        b0 = 4 * (st % 2)
                        S, SN = (S2, S3) if st % 2 == 0 else (S3, S2)
                        v.wait_ge(wk["u_mm2"], st + 1)
                        vtt(RS2, bank(b0)[:, 0:P].rearrange("p (d t) -> p d t", d=2), both(AV, st), ALU.add).then_inc(wk["r_ev"], 1)
                        v.wait_ge(wk["e2"], st + 1)
                        nc.vector.tensor_copy(both(UV, st, slice(0, 64), 0), bank(b0 + 1)[0:64, 0:P].rearrange("p (d t) -> p d t", d=2)).then_inc(wk["c_lo"], 1)
                        v.wait_ge(wk["s2_mm"], st + 1)
                        if st == 0:
                            v.wait_ge(wk["u_hi"], 1)
                        if st >= 1:
                            v.wait_ge(wk["o2_mm"], st)
                            v.wait_ge(wk["u_hi"], st + 1)
                        for d in range(2):
                            ins = stt(SN[:, d, :], S[:, d, :], EBC[:, us[d]:us[d] + 1], bank(b0 + 2)[:, d * CH:d * CH + CH], ALU.mult, ALU.add)
                        ins.then_inc(wk["u_hi"], 1)

                @block.scalar
                def _(a):
                    for st in range(NSTEP):
                        cf, cr, us = units(st)
                        b0 = 4 * (st % 2)
                        a.wait_ge(wk["e2"], st + 1)
                        act(both(UV, st, slice(64, 128), 1), bank(b0 + 1)[64:128, 0:P].rearrange("p (d t) -> p d t", d=2), ACT.Copy).then_inc(wk["c_hi"], 1)
                        a.wait_ge(wk["o2_mm"], st + 1)
                        for d, c in ((0, cf), (1, cr)):
                            act(O2[:, d, c * CH:c * CH + CH], bank(b0 + 3)[:, d * CH:d * CH + CH], ACT.Copy).then_inc(wk["ro_a"], 1)

            with nc.Block() as block:
                OS, SQ, RS_ = AV.rearrange('p n t -> p (n t)')[:, 0:TT], T[1], T[2]

                @block.vector
                def _(v):
                    ch = Chain(wk["ro_v"])
                    ch.link(v, vtt(OS, O2[:, 0, :], O2[:, 1, :], ALU.add))
                    v.wait_ge(wk["ro_mm"], 2)
                    ch.link(v, stt(OS, PS[:, 0:TT], -1.0 / CH, OS, ALU.mult, ALU.add))
                    ch.link(v, vtt(BON, PS[:, 1024:1024 + TT], VS[:, CH:CH + TT]))
                    v.wait_ge(wk["ro_s"], 3)
                    ch.link(v, vtt(OS, OS, RS_))
                    ch.link(v, vts(OS, OS, PC[:, 3:4], PC[:, 4:5], ALU.mult, ALU.add))
                    ch.link(v, vtt(OS, OS, BON, ALU.add))
                    ch.inc(vtt(OS, OS, GS))

                @block.tensor
                def _(pe):
                    product(PS[:, 1024:1024 + TT], C("ones64"), BON, TT, True, True).then_inc(wk["ro_mm"], 1)
                    pe.wait_ge(wk["ro_v"], 1)
                    product(PS[:, 0:TT], C("ones64"), OS, TT, True, True).then_inc(wk["ro_mm"], 1)
                    pe.wait_ge(wk["ro_s"], 1)
                    product(PS[:, 2048:2048 + TT], C("ones64"), SQ, TT, True, True).then_inc(wk["ro_mm"], 1)

                @block.scalar
                def _(a):
                    a.wait_ge(wk["ro_v"], 2)
                    act(SQ, OS, ACT.Square).then_inc(wk["ro_s"], 1)
                    a.wait_ge(wk["ro_mm"], 3)
                    act(RS_, PS[:, 2048:2048 + TT], ACT.Ln, scale=1.0 / CH, bias=EPSC[GN_EPS]).then_inc(wk["ro_s"], 1)
                    a.wait_ge(wk["ro_s"], 2)
                    act(RS_, RS_, ACT.Exp, scale=-0.5).then_inc(wk["ro_s"], 1)

                @block.sync
                def _(sp):
                    sp.wait_ge(wk["ro_v"], 7)
                    sp.dma_start(y_dram[bass.ds(i, 1)].rearrange("a p t -> p (a t)"), OS).then_inc(y_out, 16)
                    pass

        take = carve()
        YR = take(DT, TT)
        with nc.Block() as block:
            @block.sync
            def _(sp):
                sp.wait_ge(y_out, 16 * (NPAIR + 1))
                sp.wait_ge(loaded, 16 * (NPAIR + 1))
                sp.dma_start(YR, y_dram.rearrange("k p t -> p k t")).then_inc(loads, 16)
                sp.dma_start(X.rearrange("p k t -> p (k t)"), x_dram).then_inc(loads, 16)
                sp.wait_ge(loads, 112)
        add_products("rwkvout", [YR[:, k, :] for k in range(DT)], TT, lambda m, c: MODL[:, 1, 16 + m, c:c + 1])

        NQ, NKV = 16, 8
        KTILES = TT // P
        SCALE = float(P) ** -0.5
        take = carve()
        G = take(NQ, TX)
        Q = take(NQ, TX)
        K = take(NKV, TT)
        VT_ = take(KTILES, D)
        H = take(DT, TT)
        PR = take(2, TT)
        ROPE = take(2, TX)
        STAT = take(2, 4)
        layer_input(2, (H[:, :, 0:TX], H[:, :, TX:TT]), TT, PR, Q[:, 0:2, :].rearrange("p a b -> p (a b)")[:, 0:TT])
        freed = sem("freed")
        kinds = [("q", m) for m in range(NQ)] + [("k", m) for m in range(NKV)] + [("v", m) for m in range(DT)] + [("g", m) for m in range(NQ)]

        def block_of(n):
            return START["attn_qk"] + (2 * n if n < 24 else n + 24)

        with nc.Block() as block:
            @block.sync
            def _(sp):
                sp.dma_start(ROPE.rearrange("p a t -> p (a t)"), rope).then_inc(loads, 16)
                sp.wait_ge(loads, 128)
                R.supply(sp, RINGT, weights, START["attnout"] + SLOTS)

            @block.tensor
            def _(pe):
                for n, (kind, m) in enumerate(kinds):
                    if n >= 3:
                        pe.wait_ge(freed, n - 2)
                    o = PS[:, (n % 3) * 1024:(n % 3) * 1024 + 1024]
                    if kind == "v":
                        s = R.take(pe)
                        w = RINGT[:, s, :].rearrange("p (k m) -> p k m", k=DT)
                        for t in range(KTILES):
                            for k in range(DT):
                                last = mm(o[:, t * P:t * P + P], H[:, k, t * P:t * P + P], w[:, k, :], k == 0, k == DT - 1)
                        last.then_inc(blocks_done, 1)
                    else:
                        width = TT if kind == "k" else TX
                        tile_product(pe, o, [H[:, k, :] for k in range(DT)], width)
                    if n < 24:
                        mod_block(pe, n)

            @block.scalar
            def _(a):
                for n, (kind, m) in enumerate(kinds):
                    a.wait_ge(blocks_done, block_of(n) + 1)
                    o = PS[:, (n % 3) * 1024:(n % 3) * 1024 + TT]
                    if kind == "v":
                        ins = act(VT_[:, :, m * P:m * P + P], o.rearrange("p (t v) -> p t v", t=KTILES), ACT.Copy)
                    elif kind == "k":
                        ins = act(K[:, m, :], o, ACT.Copy)
                    elif kind == "q":
                        ins = act(Q[:, m, :], o[:, 0:TX], ACT.Copy)
                    else:
                        ins = act(G[:, m, :], o[:, 0:TX], ACT.Silu)
                    ins.then_inc(freed, 1)

        tiles = [(Q[:, m, :], TX, V("attn_q_g_2")) for m in range(NQ)] + [(K[:, m, :], TT, V("attn_k_g_2")) for m in range(NKV)]
        sqd, summed, rst_, rs_used, normed, rotated, roped = (sem(n) for n in ("sqd", "summed", "rst", "rs_used", "normed", "rotated", "roped"))
        HF = H.rearrange("p a b -> p (a b)")
        SQ_ = [HF[:, n * TT:n * TT + TT] for n in range(2)]
        RS_ = [HF[:, (2 + n) * TT:(3 + n) * TT] for n in range(2)]
        SN_ = [HF[:, (4 + n) * TT:(4 + n) * TT + TX] for n in range(2)]
        NT_ = len(tiles)
        with nc.Block() as block:
            @block.scalar
            def _(a):
                for n in range(NT_ + 1):
                    if n < NT_:
                        x_, w, _g = tiles[n]
                        if n >= 2:
                            a.wait_ge(summed, n - 1)
                        act(SQ_[n % 2][:, 0:w], x_[:, 0:w], ACT.Square).then_inc(sqd, 1)
                    if n >= 1:
                        m = n - 1
                        x_, w, _g = tiles[m]
                        a.wait_ge(summed, m + 1)
                        if m >= 2:
                            a.wait_ge(normed, m - 1)
                        alink(act(RS_[m % 2][:, 0:w], PS[:, (m % 2) * 1024:(m % 2) * 1024 + w], ACT.Ln, scale=1.0 / P, bias=EPSC[EPS]))
                        act(RS_[m % 2][:, 0:w], RS_[m % 2][:, 0:w], ACT.Exp, scale=-0.5).then_inc(rst_, 1)

            @block.tensor
            def _(pe):
                for n in range(NT_ + 1):
                    if n < NT_:
                        pe.wait_ge(sqd, n + 1)
                        if n >= 2:
                            pe.wait_ge(rst_, n - 1)
                        product(PS[:, (n % 2) * 1024:(n % 2) * 1024 + tiles[n][1]], C("ones"), SQ_[n % 2], tiles[n][1], True, True).then_inc(summed, 1)
                    if n >= 1:
                        m = n - 1
                        pe.wait_ge(normed, m + 1)
                        if m >= 2:
                            pe.wait_ge(rotated, m - 1)
                        mm(PS[:, 2048 + (m % 2) * 512:2048 + (m % 2) * 512 + 512], C("rot"), tiles[m][0][:, 0:TX]).then_inc(roped, 1)

            @block.vector
            def _(v):
                mod_finish(3)
                for n in range(NT_ + 1):
                    if n < NT_:
                        x_, w, g_ = tiles[n]
                        v.wait_ge(rst_, n + 1)
                        stt(x_[:, 0:w], x_[:, 0:w], g_, RS_[n % 2][:, 0:w]).then_inc(normed, 1)
                    if n >= 1:
                        m = n - 1
                        x_ = tiles[m][0]
                        v.wait_ge(roped, m + 1)
                        dve_chain.inc(vtt(SN_[m % 2], PS[:, 2048 + (m % 2) * 512:2048 + (m % 2) * 512 + 512], ROPE[:, 1, :]))
                        vtt(x_[:, 0:TX], x_[:, 0:TX], ROPE[:, 0, :]).then_inc(rotated, 1)
                        dve_chain.wait(v)
                        v.wait_ge(rotated, m + 1)
                        dlink(vtt(x_[:, 0:TX], x_[:, 0:TX], SN_[m % 2], ALU.add))

        NQB = TX // P
        N = NQ * NQB
        PTS = HF.rearrange("p (e k t) -> p e k t", e=2, k=KTILES)
        s_done, negmax, exped, scaled, tr0, tr1, cp0, cp1, pv_done, o_read = (
            sem(n) for n in ("s_done", "negmax", "exped", "scaled", "tr0", "tr1", "cp0", "cp1", "pv_done", "o_read"))
        with nc.Block() as block:
            @block.tensor
            def _(pe):
                def scores(n):
                    h, qb = n // NQB, n % NQB
                    if n >= 2:
                        pe.wait_ge(exped, n - 1)
                    product(PS[:, (n % 2) * 1024:(n % 2) * 1024 + TT], Q[:, h, qb * P:qb * P + P], K[:, h // 2, :], TT, True, True).then_inc(s_done, 1)

                scores(0)
                for n in range(N):
                    h, qb = n // NQB, n % NQB
                    if n + 1 < N:
                        scores(n + 1)
                    pe.wait_ge(scaled, n + 1)
                    if n >= 1:
                        pe.wait_ge(cp0, n)
                    for k in range(4):
                        last = nc.tensor.transpose(PS[:, 2048 + k * P:2048 + k * P + P], PR[:, n % 2, k * P:k * P + P], C("ident"))
                    last.then_inc(tr0, 1)
                    if n >= 1:
                        pe.wait_ge(cp1, n)
                    for k in range(4, KTILES):
                        last = nc.tensor.transpose(PS[:, 2048 + k * P:2048 + k * P + P], PR[:, n % 2, k * P:k * P + P], C("ident"))
                    last.then_inc(tr1, 1)
                    if qb == NQB - 1:
                        pe.wait_ge(cp0, n + 1)
                        pe.wait_ge(cp1, n + 1)
                        if h >= 2:
                            pe.wait_ge(o_read, h - 1)
                        for k in range(KTILES):
                            last = mm(PS[:, 3072 + (h % 2) * 512:3072 + (h % 2) * 512 + 512], VT_[:, k, (h // 2) * P:(h // 2) * P + P],
                                      PTS[:, h % 2, k, :], k == 0, k == KTILES - 1)
                        last.then_inc(pv_done, 1)

            @block.vector
            def _(v):
                def maxima(n):
                    v.wait_ge(s_done, n + 1)
                    dlink(nc.vector.reduce_max(STAT[:, n % 2, 0:1], PS[:, (n % 2) * 1024:(n % 2) * 1024 + TT], AX.X))
                    vts(STAT[:, n % 2, 1:2], STAT[:, n % 2, 0:1], -SCALE).then_inc(negmax, 1)

                maxima(0)
                for n in range(N):
                    h, qb = n // NQB, n % NQB
                    if n + 1 < N:
                        maxima(n + 1)
                    v.wait_ge(exped, n + 1)
                    dlink(nc.vector.reciprocal(STAT[:, n % 2, 3:4], STAT[:, n % 2, 2:3]))
                    vts(PR[:, n % 2, :], PR[:, n % 2, :], STAT[:, n % 2, 3:4]).then_inc(scaled, 1)
                    v.wait_ge(tr1, n + 1)
                    if n >= 8 and qb == 0:
                        v.wait_ge(pv_done, h - 1)
                    nc.vector.tensor_copy(PTS[:, h % 2, 4:6, qb * P:qb * P + P],
                                          PS[:, 2560:2560 + 2 * P].rearrange("p (k t) -> p k t", k=2)).then_inc(cp1, 1)
                    if qb == 1 and h >= 1:
                        v.wait_ge(pv_done, h)
                        vtt(G[:, h - 1, :], PS[:, 3072 + ((h - 1) % 2) * 512:3072 + ((h - 1) % 2) * 512 + 512], G[:, h - 1, :]).then_inc(o_read, 1)
                v.wait_ge(pv_done, NQ)
                dlink(vtt(G[:, NQ - 1, :], PS[:, 3072 + 512:3072 + 1024], G[:, NQ - 1, :]))

            @block.scalar
            def _(a):
                for n in range(N):
                    h, qb = n // NQB, n % NQB
                    a.wait_ge(negmax, n + 1)
                    if n >= 2:
                        a.wait_ge(tr1, n - 1)
                    act(PR[:, n % 2, :], PS[:, (n % 2) * 1024:(n % 2) * 1024 + TT], ACT.Exp, bias=STAT[:, n % 2, 1:2],
                        scale=SCALE, accum_out=STAT[:, n % 2, 2:3]).then_inc(exped, 1)
                    a.wait_ge(tr0, n + 1)
                    if n >= 8 and qb == 0:
                        a.wait_ge(pv_done, h - 1)
                    act(PTS[:, h % 2, 0:4, qb * P:qb * P + P], PS[:, 2048:2560].rearrange("p (k t) -> p k t", k=4), ACT.Copy).then_inc(cp0, 1)

        added = sem("added")
        with nc.Block() as block:
            @block.sync
            def _(sp):
                R.supply(sp, RINGT, weights, START["conv1"] + SLOTS)

            @block.tensor
            def _(pe):
                for m in range(DT):
                    if m >= 2:
                        pe.wait_ge(added, m - 1)
                    for half in range(2):
                        s = R.take(pe)
                        w = RINGT[:, s, :].rearrange("p (k m) -> p k m", k=DT)
                        for k in range(DT):
                            last = mm(PS[:, (m % 2) * 512:(m % 2) * 512 + 512], w[:, k, :], G[:, 8 * half + k, :],
                                      half == 0 and k == 0, half == 1 and k == DT - 1)
                        last.then_inc(blocks_done, 1)

            @block.vector
            def _(v):
                for m in range(DT):
                    v.wait_ge(blocks_done, START["attnout"] + 2 * m + 2)
                    stt(X[:, m, 0:TX], PS[:, (m % 2) * 512:(m % 2) * 512 + 512], MODL[:, 2, 16 + m, 0:1], X[:, m, 0:TX],
                        ALU.mult, ALU.add).then_inc(added, 1)

        conv_layer(3, 1, TX, None)

        take = carve()
        sq = take(2, TT)
        RST = take(TT)
        OUT = take(DT, TX)
        norm_stats([X[:, k, 0:TX] for k in range(DT)], TX, "ones", 1.0 / D, EPS, RST[:, 0:TX],
                   [sq[:, 0, 0:TX], sq[:, 1, 0:TX]], PS)
        out_ready, out_stored = sem("out_ready"), sem("out_stored")
        with nc.Block() as block:
            @block.vector
            def _(v):
                for k in range(DT):
                    stt(OUT[:, k, :], X[:, k, 0:TX], V("final_g_2", k), RST[:, 0:TX]).then_inc(out_ready, 1)

            @block.sync
            def _(sp):
                for k in range(DT):
                    sp.wait_ge(out_ready, k + 1)
                    sp.dma_start(outT[k * P:k * P + P, :], OUT[:, k, :]).then_inc(out_stored, 16)
                sp.wait_ge(out_stored, 16 * DT)


def pack(inputs):
    a = {k: np.asarray(v) for k, v in inputs.items()}
    zeros = np.zeros((64, 64), np.float32)

    def pairs(w):
        return [np.block([[w[2 * m], zeros], [zeros, w[2 * m + 1]]]) for m in range(4)]

    def block(name, layer, m):
        if name == "rg":
            return np.concatenate(pairs(a["rg_wa"][0]) + pairs(a["rg_wx"][0]), 1)
        if name in ("lora_w1", "lora_a1"):
            w = a[f"rwkv_{name[5:]}_2"][0]
            w = np.concatenate([w[0], w[1]], 1)
            return w.reshape(DT, P, P).transpose(1, 0, 2).reshape(P, D)
        if name in ("lora_w2", "lora_a2"):
            return a[f"rwkv_{name[5:]}_2"][0].reshape(P, D)
        if name == "w_ple_proj":
            w = a[name][0].reshape(2, P, 2, 4, P)[:, :, m]
            return w.transpose(1, 2, 0, 3).reshape(P, D)
        if name == "attn_w_out_2":
            w = a[name][0][layer * D:(layer + 1) * D]
        else:
            w = a[name][layer]
        return w[:, m * P:(m + 1) * P].reshape(DT, P, P).transpose(1, 0, 2).reshape(P, D)

    weights = np.stack([block(*b) for b in PLAN])
    vectors = np.concatenate([a[n].reshape(-1, P).T for n in VT], 1)
    out = {"xT": a["x"][0].T, "pT": a["p"][0, 0].T, "ctxT": a["ctx_2"][0].T, "vectors": vectors,
           "consts": constants(), "rope": rope_tables(), "weights": weights}
    return {k: np.ascontiguousarray(v) for k, v in out.items()}


def kernel(**inputs):
    import concourse.bacc as bacc
    from concourse.bass_utils import run_bass_kernel_spmd

    nc = bacc.Bacc("TRN2", target_bir_lowering=False, num_devices=1)
    arrays = pack(inputs)
    args = [nc.dram_tensor(f"in_{n}", a.shape, mybir.dt.from_np(a.dtype), kind="ExternalInput").ap() for n, a in arrays.items()]
    out = nc.dram_tensor("out_T", (D, TX), F32, kind="ExternalOutput").ap()
    two_blocks(nc, *args, out)
    r = run_bass_kernel_spmd(nc, [{f"in_{n}": a for n, a in arrays.items()}], core_ids=[0])
    return np.ascontiguousarray(np.asarray(r.results[0]["out_T"]).T)[None]
```

```python
from contextlib import ExitStack

import numpy as np
import concourse.bass as bass
from concourse import mybir

P = 128
D = 1024
DT = D // P
TX, TC = 512, 256
TT = TX + TC
CH = 64
NCX, NCC = TX // CH, TC // CH
NSTEP = NCX + NCC
NPAIR = 8
NU = 2 * NSTEP
SLOTS = 4
EPS = 1e-6
LN_EPS = 1e-5
GN_EPS = 64e-5
TAPS = 31
PAD = TAPS // 2
XW, CW = TX + 2 * PAD, TC + 2 * PAD
YW = XW + CW

F32 = mybir.dt.float32
ALU = mybir.AluOpType
ACT = mybir.ActivationFunctionType
AX = mybir.AxisListType


def vector_table():
    sizes = [("norm_mix_w", 8), ("conv_w", 16), ("conv_b", 4), ("rg_ba", 4), ("rg_bx", 4),
             ("rg_lambda", 4), ("hg_lb", 8), ("hg_norm_w", 1), ("ple_norm_w", 8),
             ("b_ple_gate", 8), ("final_norm_w", 8), ("c_2", 8), ("c_ctx_2", 8),
             ("norm_g_2", 32), ("mod_b_2", 96), ("conv_dw_2", 496), ("conv_db_2", 16),
             ("conv_ln_g_2", 16), ("conv_ln_b_2", 16), ("rwkv_mu_2", 48), ("rwkv_w0_2", 16),
             ("rwkv_a0_2", 16), ("rwkv_k_k_2", 8), ("rwkv_k_a_2", 8), ("rwkv_r_k_2", 8),
             ("rwkv_ln_g_2", 8), ("rwkv_ln_b_2", 8), ("attn_q_g_2", 1), ("attn_k_g_2", 1),
             ("final_g_2", 8)]
    table, at = {}, 0
    for name, n in sizes:
        table[name] = (at, n)
        at += n
    return table, at


VT, NVEC = vector_table()

CT, NCONST = {}, 0
for _n, _w in (("ident", 128), ("ones", 128), ("ones64", 128), ("rot", 128),
               ("gla_mask", 128), ("inv_mask", 6 * 128), ("wkv_mask", 2 * 256)):
    CT[_n] = (NCONST, _w)
    NCONST += _w


def constants():
    out = np.zeros((P, NCONST), np.float32)
    i, j = np.arange(P)[:, None], np.arange(P)[None, :]

    def put(name, a):
        out[:, CT[name][0]:CT[name][0] + CT[name][1]] = a

    put("ident", i == j)
    put("ones", np.ones((P, P)))
    put("ones64", i // 64 == j // 64)
    put("rot", np.where((j % 64 < 32) & (i == j + 32), -1.0, 0) + np.where((j % 64 >= 32) & (i == j - 32), 1.0, 0))
    put("gla_mask", (i // CH == j // CH) & (i <= j))
    m = [((i // (2 * b) == j // (2 * b)) & (i // b != j // b)) for b in (1, 2, 4, 8, 16, 32)]
    put("inv_mask", np.concatenate(m, 1))
    s, t = i % 64, j % 64
    w = []
    for strict, incl in ((s < t, s <= t), (s > t, s >= t)):
        w += [np.where(j < 64, strict, incl), np.where(j < 64, incl, strict)]
    put("wkv_mask", np.concatenate(w, 1))
    return out


def rope_tables():
    row = np.repeat(np.arange(TX // 64), 64).astype(np.float32)
    col = (np.arange(TX) % 64).astype(np.float32)
    inv = (1.0 / (np.float32(10000.0) ** (np.arange(0, 64, 2, dtype=np.float32) / np.float32(64)))).astype(np.float32)
    ang = np.concatenate([inv[:, None] * row[None]] * 2 + [inv[:, None] * col[None]] * 2, 0).astype(np.float32)
    return np.concatenate([np.cos(ang), np.sin(ang)], 1).astype(np.float32)


def weight_plan():
    plan, start = [], {}

    def stage(name, body, mod=None):
        start[name] = len(plan)
        for n, b in enumerate(body):
            plan.append(b)
            if mod is not None and n < 24:
                plan.append(("mod_w_2", mod, n))

    stage("in1", [("w_in", 0, m) for m in range(24)], 0)
    stage("rg", [("rg", 0, 0)])
    stage("out1", [("w_out", 0, m) for m in range(8)])
    stage("gate1", [("w_ple_gate", 0, m) for m in range(8)] + [("w_ple_proj", 0, 0), ("w_ple_proj", 0, 1)])
    tri = [("conv_w_in_2", 0, 8 * part + m) for m in range(8) for part in (0, 1, 2)]
    stage("conv0", tri, 1)
    stage("convout0", [("conv_w_out_2", 0, m) for m in range(8)])
    stage("lora", [("lora_w1", 0, 0), ("lora_a1", 0, 0), ("lora_w2", 0, 0), ("lora_a2", 0, 0)])
    stage("rkvg", [(f"rwkv_w_{n}_2", 0, m) for n in "rkvg" for m in range(8)], 2)
    stage("rwkvout", [("rwkv_w_o_2", 0, m) for m in range(8)])
    stage("attn_qk", [("attn_w_in_2", 0, m) for m in range(24)], 3)
    stage("attn_v", [("attn_w_in_2", 0, 24 + m) for m in range(8)])
    stage("attn_g", [("attn_w_in_2", 0, 32 + m) for m in range(16)])
    stage("attnout", [("attn_w_out_2", k, m) for m in range(8) for k in (0, 1)])
    stage("conv1", [("conv_w_in_2", 1, 8 * part + m) for m in range(8) for part in (0, 1, 2)])
    stage("convout1", [("conv_w_out_2", 1, m) for m in range(8)])
    return plan, start


PLAN, START = weight_plan()
NB = len(PLAN)


class Ring:

    def __init__(self, ready, used):
        self.ready, self.used = ready, used
        self.issued = 0
        self.taken = 0

    def supply(self, sp, ring, weights, upto):
        upto = min(upto, NB)
        while self.issued < upto:
            b = self.issued
            n = (upto - b) // SLOTS
            if b % SLOTS == 0 and b >= SLOTS and n > 1:
                with sp.Fori(0, n) as i:
                    for s in range(SLOTS):
                        sp.wait_ge(self.used, i * SLOTS + (b + s - SLOTS + 1))
                        sp.dma_start(ring[:, s, :], weights[bass.ds(i * SLOTS + (b + s), 1), :, :]
                                     .rearrange("a p n -> (a p) n")).then_inc(self.ready[s], 16)
                self.issued += n * SLOTS
                continue
            if b >= SLOTS:
                sp.wait_ge(self.used, b - SLOTS + 1)
            sp.dma_start(ring[:, b % SLOTS, :], weights[b, :, :]).then_inc(self.ready[b % SLOTS], 16)
            self.issued += 1

    def take(self, pe):
        b = self.taken
        pe.wait_ge(self.ready[b % SLOTS], 16 * (b // SLOTS + 1))
        self.taken += 1
        return b % SLOTS


class Chain:

    def __init__(self, sem):
        self.sem, self.n, self.base = sem, 0, 0

    def inc(self, ins):
        self.n += 1
        ins.then_inc(self.sem, 1)

    def wait(self, eng):
        eng.wait_ge(self.sem, self.base + self.n)

    def link(self, eng, ins):
        self.inc(ins)
        self.wait(eng)


def two_blocks(nc, xT, pT, ctxT, vectors, consts, rope, weights, outT):
    ctx = ExitStack()
    names = [0]

    def sem(name):
        names[0] += 1
        return ctx.enter_context(nc.semaphore(f"{name}_{names[0]}"))

    def sb(name, shape):
        return ctx.enter_context(nc.sbuf_tensor(name, shape, F32))

    def ap(t):
        return t[tuple(slice(None) for _ in t.shape)]

    with ctx:
        X = ap(sb("stream", [P, DT, TT]))
        RINGT = ap(sb("ring", [P, SLOTS, DT * P]))
        VEC = ap(sb("vec", [P, NVEC]))
        CON = ap(sb("con", [P, NCONST]))
        MODL = ap(sb("mod", [P, 4, 24, 2]))
        SC = ap(sb("sc", [P, DT, 2]))
        GA = ap(sb("ga", [P, DT, 2]))
        TINY = ap(sb("tiny", [P, 128]))
        room = 212000 // 4 - DT * TT - SLOTS * DT * P - NVEC - NCONST - 192 - 32 - 128
        ARENA = ap(sb("arena", [P, room]))
        PS = ap(ctx.enter_context(nc.psum_tensor("ps", [P, 4096], F32)))
        PMOD = PS[:, 7 * 512:7 * 512 + 48].rearrange("p (m v) -> p m v", v=2)

        rwkv_dram = nc.dram_tensor("rwkv_spill", [DT + 1, 8, P, TT], F32, kind="Internal").ap()
        y_dram = nc.dram_tensor("y_spill", [DT, P, TT], F32, kind="Internal").ap()
        x_dram = nc.dram_tensor("x_spill", [P, DT * TT], F32, kind="Internal").ap()

        ring_ready = [sem(f"ring_ready{s}") for s in range(SLOTS)]
        blocks_done = sem("blocks_done")
        loads = sem("loads")
        stores = sem("stores")
        R = Ring(ring_ready, blocks_done)
        dve_chain = Chain(sem("dve_chain"))
        act_chain = Chain(sem("act_chain"))
        pool_chain = Chain(sem("pool_chain"))

        def V(name, k=0, n=1):
            return VEC[:, VT[name][0] + k:VT[name][0] + k + n]

        def C(name, k=0, n=None):
            a = CT[name][0] + k
            return CON[:, a:a + (CT[name][1] if n is None else n)]

        def carve():
            at = [0]

            def take(*shape):
                n = int(np.prod(shape))
                a = ARENA[:, at[0]:at[0] + n]
                at[0] += n
                assert at[0] <= room, (at[0], room)
                if len(shape) == 1:
                    return a
                names_ = "abcd"[:len(shape)]
                kw = {c: s for c, s in zip(names_, shape)}
                return a.rearrange(f"p ({' '.join(names_)}) -> p {' '.join(names_)}", **kw)
            return take

        def dlink(ins):
            dve_chain.link(nc.vector, ins)

        def alink(ins):
            act_chain.link(nc.scalar, ins)

        def plink(ins):
            pool_chain.link(nc.gpsimd, ins)

        def vtt(o, a, b, op=ALU.mult):
            return nc.vector.tensor_tensor(o, a, b, op)

        def vts(o, a, s1, s2=None, op0=ALU.mult, op1=None):
            if s2 is None:
                return nc.vector.tensor_scalar(o, a, s1, None, op0)
            return nc.vector.tensor_scalar(o, a, s1, s2, op0, op1)

        def stt(o, a, s, b, op0=ALU.mult, op1=ALU.mult):
            return nc.vector.scalar_tensor_tensor(out=o, in0=a, scalar=s, in1=b, op0=op0, op1=op1)

        def act(o, a, f, **kw):
            return nc.scalar.activation(o, a, f, **kw)

        def mm(o, l, r, start=True, stop=True):
            return nc.tensor.matmul(o, l, r, start=start, stop=stop)


        def mod_block(pe, n):
            s = R.take(pe)
            w = RINGT[:, s, :].rearrange("p (k m) -> p k m", k=DT)
            for k in range(DT):
                last = mm(PMOD[:, n, :], w[:, k, :], SC[:, k, :], k == 0, k == DT - 1)
            last.then_inc(blocks_done, 1)

        def mod_finish(layer):
            b = V("mod_b_2", 24 * layer, 24).rearrange("p (m o) -> p m o", o=1).broadcast_to([P, 24, 2])
            dlink(vtt(MODL[:, layer], PMOD, b, ALU.add))

        def mod_gain(layer):
            g = V("norm_g_2", 8 * layer, 8).rearrange("p (m o) -> p m o", o=1).broadcast_to([P, 8, 2])
            dlink(stt(GA, MODL[:, layer, 8:16], 1.0, g, ALU.add, ALU.mult))

        def product(o, l, rhs, width, start, stop):
            last = None
            for a in range(0, width, 512):
                b = min(a + 512, width)
                last = mm(o[:, a:b], l, rhs[:, a:b], start, stop)
            return last

        def tile_product(pe, o, rhs, width):
            s = R.take(pe)
            w = RINGT[:, s, :].rearrange("p (k m) -> p k m", k=DT)
            for k in range(DT):
                last = product(o, w[:, k, :], rhs[k], width, k == 0, k == DT - 1)
            last.then_inc(blocks_done, 1)

        EPSC = {}
        for n, e in enumerate((EPS, LN_EPS, GN_EPS, 1e-12)):
            EPSC[e] = TINY[:, n:n + 1]

        def norm_stats(src, width, ones_name, scale, eps, rstd, sq, psum):
            n = len(src)
            sq_ready, sq_used = sem("sq_ready"), sem("sq_used")
            with nc.Block() as block:
                @block.scalar
                def _(a):
                    for k in range(n):
                        if k >= 2:
                            a.wait_ge(sq_used, k - 1)
                        act(sq[k % 2], src[k], ACT.Square).then_inc(sq_ready, 1)
                    a.wait_ge(sq_used, n)
                    alink(act(rstd, psum[:, 0:width], ACT.Ln, scale=scale, bias=EPSC[eps]))
                    alink(act(rstd, rstd, ACT.Exp, scale=-0.5))

                @block.tensor
                def _(pe):
                    for k in range(n):
                        pe.wait_ge(sq_ready, k + 1)
                        product(psum, C(ones_name), sq[k % 2], width, k == 0, k == n - 1).then_inc(sq_used, 1)

        def layer_input(layer, H, width, sq, rst):
            norm_stats([X[:, k, 0:width] for k in range(DT)], width, "ones", 1.0 / D, EPS, rst[:, 0:width],
                       [sq[:, 0, 0:width], sq[:, 1, 0:width]], PS)
            scaled = sem("scaled")
            halves = [(0, TX, 0), (TX, TT, 1)][:1 if width == TX else 2]
            with nc.Block() as block:
                @block.vector
                def _(v):
                    mod_gain(layer)
                    for k in range(DT):
                        for a, b, c in halves:
                            stt(H[c][:, k, :], X[:, k, a:b], GA[:, k, c:c + 1], rst[:, a:b]).then_inc(scaled, 1)

                @block.scalar
                def _(a_):
                    n = 0
                    for k in range(DT):
                        for a, b, c in halves:
                            n += 1
                            a_.wait_ge(scaled, n)
                            act(H[c][:, k, :], H[c][:, k, :], ACT.Identity, bias=MODL[:, layer, k, c:c + 1])

        SP8N, SP8, LB, OMLB = TINY[:, 8:12], TINY[:, 12:16], TINY[:, 16:20], TINY[:, 20:24]
        with nc.Block() as block:
            @block.sync
            def _(sp):
                sp.dma_start(VEC, vectors).then_inc(loads, 16)
                sp.dma_start(X[:, :, 0:TX], xT.rearrange("(k p) t -> p k t", p=P)).then_inc(loads, 16)
                sp.dma_start(CON, consts).then_inc(loads, 16)
                sp.dma_start(X[:, :, TX:TT], ctxT.rearrange("(k p) t -> p k t", p=P)).then_inc(loads, 16)
                R.supply(sp, RINGT, weights, SLOTS)

            @block.scalar
            def _(a):
                a.wait_ge(loads, 64)
                act(SC[:, :, 0], V("c_2", 0, 8), ACT.Silu)
                alink(act(SC[:, :, 1], V("c_ctx_2", 0, 8), ACT.Silu))

            @block.gpsimd
            def _(g):
                for n, e in enumerate((EPS, LN_EPS, GN_EPS, 1e-12)):
                    nc.gpsimd.memset(TINY[:, n:n + 1], e)
                plink(nc.gpsimd.memset(TINY[:, 4:5], 1.0))

        with nc.Block() as block:
            t0, t1, t2, t3 = (TINY[:, 32 + 4 * n:36 + 4 * n] for n in range(4))
            e_ready, e_asked = sem("e_ready"), sem("e_asked")

            @block.vector
            def _(v):
                lam = V("rg_lambda", 0, 4)
                h0, h1 = V("hg_lb", 0, 4), V("hg_lb", 4, 4)
                dlink(vts(t0, lam, -1.0))
                dlink(vtt(t1, t0, lam, ALU.max))
                dlink(vtt(t2, h0, h1, ALU.max))
                dlink(vtt(TINY[:, 48:52], h0, t2, ALU.subtract))
                vtt(TINY[:, 52:56], h1, t2, ALU.subtract).then_inc(e_asked, 1)
                v.wait_ge(e_ready, 2)
                E_ = TINY[:, 56:60]
                dlink(vts(t2, E_, 2.0, None, ALU.add))
                dlink(nc.vector.reciprocal(t2, t2))
                dlink(vtt(t2, t2, E_))
                dlink(vtt(t3, t2, t2))
                dlink(vts(t1, t3, 1.0 / 19, 1.0 / 17, ALU.mult, ALU.add))
                for q in (15, 13, 11, 9, 7, 5, 3, 1):
                    dlink(vtt(t1, t1, t3))
                    dlink(vts(t1, t1, 1.0 / q, None, ALU.add))
                dlink(stt(t1, t1, 2.0, t2, ALU.mult, ALU.mult))
                dlink(vts(t0, t0, 0.0, None, ALU.max))
                dlink(vtt(t1, t1, t0, ALU.add))
                dlink(vts(SP8N, t1, -8.0))
                dlink(vts(SP8, t1, 8.0))
                a0, a1 = TINY[:, 60:64], TINY[:, 64:68]
                dlink(vtt(t2, a0, a1, ALU.add))
                dlink(nc.vector.reciprocal(t2, t2))
                dlink(vtt(LB, a0, t2))
                dlink(vtt(OMLB, a1, t2))

            @block.scalar
            def _(a):
                a.wait_ge(e_asked, 1)
                act(TINY[:, 56:60], t1, ACT.Exp, scale=-1.0).then_inc(e_ready, 1)
                act(TINY[:, 60:68], TINY[:, 48:56], ACT.Exp).then_inc(e_ready, 1)

        take = carve()
        H = take(DT, TX)
        RAW = take(20, TX)
        VTOK = take(4, 512)
        sq = take(2, TT)
        RST = take(TT)
        XAP = take(4, TX + 4)
        XC, RG, IG, AG, TH = (take(4, TX) for _ in range(5))

        norm_stats([X[:, k, 0:TX] for k in range(DT)], TX, "ones", 1.0 / D, EPS, RST[:, 0:TX],
                   [sq[:, 0, 0:TX], sq[:, 1, 0:TX]], PS)
        with nc.Block() as block:
            @block.vector
            def _(v):
                for k in range(DT):
                    stt(H[:, k, :], X[:, k, 0:TX], V("norm_mix_w", k), RST[:, 0:TX])
                dlink(nc.vector.memset(XAP[:, :, 0:3], 0.0))

        bank_free = sem("bank_free")
        with nc.Block() as block:
            @block.sync
            def _(sp):
                R.supply(sp, RINGT, weights, START["rg"] + SLOTS)

            @block.tensor
            def _(pe):
                for m in range(24):
                    if m >= 2:
                        pe.wait_ge(bank_free, m - 1)
                    bank = PS[:, (m % 2) * 512:(m % 2) * 512 + 512]
                    if 16 <= m < 20:
                        s = R.take(pe)
                        w = RINGT[:, s, :].rearrange("p (k m) -> p k m", k=DT)
                        for t in range(4):
                            for k in range(DT):
                                last = mm(bank[:, t * P:t * P + P], H[:, k, t * P:t * P + P], w[:, k, :], k == 0, k == DT - 1)
                        last.then_inc(blocks_done, 1)
                    else:
                        tile_product(pe, bank, [H[:, k, :] for k in range(DT)], TX)
                    mod_block(pe, m)

            @block.scalar
            def _(a):
                for m in range(24):
                    a.wait_ge(blocks_done, START["in1"] + 2 * m + 1)
                    bank = PS[:, (m % 2) * 512:(m % 2) * 512 + 512]
                    o, i_ = RAW[:, m if m < 16 else m - 4, :], bank
                    if m < 4:
                        o = XAP[:, m, 3:3 + TX]
                    if 16 <= m < 20:
                        o = VTOK.rearrange("p t (h v) -> p t h v", h=4)[:, :, m - 16, :]
                        i_ = bank.rearrange("p (t v) -> p t v", t=4)
                    act(o, i_, ACT.Copy).then_inc(bank_free, 1)

        xc_ready = sem("xc_ready")
        gates_done, rg_done = sem("gates_done"), sem("rg_done")
        Y1 = H
        with nc.Block() as block:
            @block.sync
            def _(sp):
                R.supply(sp, RINGT, weights, START["out1"] + SLOTS)

            @block.vector
            def _(v):
                mod_finish(0)
                for m in range(4):
                    dlink(vts(XC[:, m, :], XAP[:, m, 3:3 + TX], V("conv_w", 12 + m), V("conv_b", m), ALU.mult, ALU.add))
                    for j in range(3):
                        ins = stt(XC[:, m, :], XAP[:, m, j:j + TX], V("conv_w", 4 * j + m), XC[:, m, :], ALU.mult, ALU.add)
                        if j < 2:
                            dlink(ins)
                        else:
                            ins.then_inc(xc_ready, 1)

            @block.tensor
            def _(pe):
                s = R.take(pe)
                for m in range(4):
                    pe.wait_ge(xc_ready, m + 1)
                    for g in range(2):
                        bank = 2 * (m % 2) + g
                        if m >= 2:
                            pe.wait_ge(gates_done, 2 * (m - 2) + g + 1)
                        last = mm(PS[:, bank * 512:bank * 512 + 512], RINGT[:, s, (4 * g + m) * P:(4 * g + m + 1) * P], XC[:, m, :])
                        last.then_inc(rg_done, 1)
                mm(PS[:, 2048:2049], C("ident"), C("ident", 0, 1)).then_inc(blocks_done, 1)

            @block.scalar
            def _(a):
                act(RAW[:, 4:8, :], RAW[:, 4:8, :], ACT.Silu)
                act(RAW[:, 8:12, :], RAW[:, 8:12, :], ACT.Silu)
                act(RAW[:, 16:20, :], RAW[:, 16:20, :], ACT.Silu)
                for m in range(4):
                    for g in range(2):
                        a.wait_ge(rg_done, 2 * m + g + 1)
                        bank = 2 * (m % 2) + g
                        act((RG, IG)[g][:, m, :], PS[:, bank * 512:bank * 512 + 512], ACT.Sigmoid,
                            bias=V(("rg_ba", "rg_bx")[g], m)).then_inc(gates_done, 1)

        tanh_ready, root_asked, root_ready = sem("tanh_ready"), sem("root_asked"), sem("root_ready")
        with nc.Block() as block:
            @block.scalar
            def _(a):
                for m in range(4):
                    act(AG[:, m, :], RG[:, m, :], ACT.Exp, scale=SP8N[:, m:m + 1])
                    act(TH[:, m, :], RG[:, m, :], ACT.Tanh, scale=SP8[:, m:m + 1]).then_inc(tanh_ready, 1)
                for m in range(4):
                    a.wait_ge(root_asked, m + 1)
                    act(TH[:, m, :], TH[:, m, :], ACT.Sqrt).then_inc(root_ready, 1)

            @block.vector
            def _(v):
                for m in range(4):
                    v.wait_ge(tanh_ready, m + 1)
                    dlink(vtt(RG[:, m, :], AG[:, m, :], AG[:, m, :]))
                    stt(TH[:, m, :], RG[:, m, :], 1.0, TH[:, m, :], ALU.add, ALU.mult).then_inc(root_asked, 1)
                    dlink(vtt(IG[:, m, :], IG[:, m, :], XC[:, m, :]))
                for m in range(4):
                    v.wait_ge(root_ready, m + 1)
                    dlink(nc.vector.memset(TH[:, m, 0:1], 1.0))
                    dlink(vtt(IG[:, m, :], IG[:, m, :], TH[:, m, :]))
                    dlink(nc.vector.tensor_tensor_scan(XC[:, m, :], AG[:, m, :], IG[:, m, :], 0.0, ALU.mult, ALU.add))
                    dlink(vtt(Y1[:, m, :], XC[:, m, :], RAW[:, 4 + m, :]))

        SF, BC, EB, ENB, SM = XC, RG, IG, AG, TH
        Q, K = RAW[:, 8:12, :], RAW[:, 12:16, :]
        KT = SF
        ST = RAW[:, 0:8, :].rearrange("p a b -> p (a b)").rearrange("p (h n v) -> p h n v", h=4, n=NCX)
        CMASK = sq[:, 0, 0:TX]
        with nc.Block() as block:
            @block.scalar
            def _(a):
                act(EB, RAW[:, 12:16, :], ACT.Sigmoid)
                alink(act(K, K, ACT.Sigmoid, scale=-1.0))
                for m in range(4):
                    act(SF[:, m, :], EB[:, m, :], ACT.Ln, scale=OMLB[:, m:m + 1], bias=LB[:, m:m + 1])

            @block.vector
            def _(v):
                dlink(nc.vector.memset(CMASK, 1.0))
                dlink(nc.vector.memset(CMASK.rearrange("p (n t) -> p n t", t=CH)[:, :, 0:1], 0.0))
        with nc.Block() as block:
            @block.vector
            def _(v):
                for m in range(4):
                    dlink(nc.vector.tensor_tensor_scan(BC[:, m, :], CMASK, SF[:, m, :], 0.0, ALU.mult, ALU.add))
                for m in range(4):
                    dlink(vts(K[:, m, :], K[:, m, :], OMLB[:, m:m + 1]))
        BL = sq[:, 1, 0:32].rearrange('p (n o) -> p n o', o=1)
        b4 = BC.rearrange("p h (n t) -> p (h n) t", t=CH)
        eb_ready, db_ready, ed_ready = sem("eb_ready"), sem("db_ready"), sem("ed_ready")
        with nc.Block() as block:
            @block.scalar
            def _(a):
                act(EB, BC, ACT.Exp).then_inc(eb_ready, 1)
                act(ENB, BC, ACT.Exp, scale=-1.0).then_inc(eb_ready, 1)
                a.wait_ge(db_ready, 1)
                act(BC, BC, ACT.Exp).then_inc(ed_ready, 1)

            @block.vector
            def _(v):
                v.wait_ge(eb_ready, 2)
                dlink(nc.vector.tensor_copy(BL, b4[:, :, CH - 1:CH]))
                vtt(b4, BL.broadcast_to([P, 32, CH]), b4, ALU.subtract).then_inc(db_ready, 1)
                dlink(stt(Q, Q, float(P) ** -0.5, EB, ALU.mult, ALU.mult))
                dlink(vtt(ENB, ENB, K))
                v.wait_ge(ed_ready, 1)
                dlink(vtt(BC, BC, K))
        QE, KE, KD = Q, ENB, BC
        sc_done, sc_masked, kt_done, kt_read = (sem(n) for n in ("sc_done", "sc_masked", "kt_done", "kt_read"))
        gmask = C("gla_mask").rearrange("p (o t) -> p o t", o=1).broadcast_to([P, 4, P])
        with nc.Block() as block:
            @block.tensor
            def _(pe):
                for h in range(4):
                    for u in range(4):
                        last = mm(PS[:, h * 512 + u * P:h * 512 + u * P + P], KE[:, h, u * P:u * P + P], QE[:, h, u * P:u * P + P])
                    last.then_inc(sc_done, 1)
                    if h >= 2:
                        pe.wait_ge(kt_read, h - 1)
                    for u in range(4):
                        o = 2048 + (h % 2) * 512 + u * P
                        last = nc.tensor.transpose(PS[:, o:o + P], KD[:, h, u * P:u * P + P], C("ident"))
                    last.then_inc(kt_done, 1)

            @block.vector
            def _(v):
                for h in range(4):
                    v.wait_ge(sc_done, h + 1)
                    dlink(vtt(SM[:, h, :].rearrange("p (u t) -> p u t", u=4),
                              PS[:, h * 512:h * 512 + 512].rearrange("p (u t) -> p u t", u=4), gmask))

            @block.scalar
            def _(a):
                for h in range(4):
                    a.wait_ge(kt_done, h + 1)
                    o = 2048 + (h % 2) * 512
                    act(KT[:, h, :], PS[:, o:o + 512], ACT.Copy).then_inc(kt_read, 1)
        ds_done, st_ready, o_done = (sem(n) for n in ("ds_done", "st_ready", "o_done"))
        with nc.Block() as block:
            @block.tensor
            def _(pe):
                for h in range(4):
                    if h >= 1:
                        pe.wait_ge(st_ready, (NCX - 1) * h)
                    for e in range(2):
                        for u in range(4):
                            last = mm(PS[:, 2048 + e * 512 + u * P:2048 + e * 512 + u * P + P],
                                      KT[e * CH:e * CH + CH, h, u * P:u * P + P], VTOK[e * CH:e * CH + CH, u, h * P:h * P + P])
                        last.then_inc(ds_done, 1)
                for h in range(4):
                    pe.wait_ge(st_ready, (NCX - 1) * (h + 1))
                    for u in range(4):
                        o = PS[:, h * 512 + u * P:h * 512 + u * P + P]
                        mm(o, VTOK[:, u, h * P:h * P + P], SM[:, h, u * P:u * P + P], True, False)
                        for e in range(2):
                            n = 2 * u + e
                            last = mm(o[:, e * CH:e * CH + CH], ST[:, h, n, :], QE[:, h, n * CH:n * CH + CH], False, e == 1)
                    last.then_inc(o_done, 1)

            @block.vector
            def _(v):
                for h in range(4):
                    dlink(nc.vector.memset(ST[:, h, 0, :], 0.0))
                    v.wait_ge(ds_done, 2 * h + 2)
                    for n in range(NCX - 1):
                        o = 2048 + (n % 2) * 512 + (n // 2) * P
                        ins = stt(ST[:, h, n + 1, :], ST[:, h, n, :], EB[:, h, n * CH + CH - 1:n * CH + CH], PS[:, o:o + P], ALU.mult, ALU.add)
                        ins.then_inc(st_ready, 1)
                        v.wait_ge(st_ready, h * (NCX - 1) + n + 1)

            @block.scalar
            def _(a):
                for h in range(4):
                    a.wait_ge(o_done, h + 1)
                    act(KE[:, h, :], PS[:, h * 512:h * 512 + 512], ACT.Copy)
        O = KE
        osq, orst = SM, KD
        osq_ready, osum = sem('osq_ready'), sem('osum')
        with nc.Block() as block:
            @block.scalar
            def _(a):
                act(osq, O, ACT.Square).then_inc(osq_ready, 1)
                a.wait_ge(osum, 4)
                alink(act(orst, PS[:, 0:2048].rearrange("p (h t) -> p h t", h=4), ACT.Ln, scale=1.0 / P, bias=EPSC[EPS]))
                act(orst, orst, ACT.Exp, scale=-0.5).then_inc(osq_ready, 1)

            @block.tensor
            def _(pe):
                pe.wait_ge(osq_ready, 1)
                for h in range(4):
                    mm(PS[:, h * 512:h * 512 + 512], C("ones"), osq[:, h, :]).then_inc(osum, 1)

            @block.vector
            def _(v):
                v.wait_ge(osum, 4)
                dlink(stt(O, O, V("hg_norm_w"), RAW[:, 16:20, :], ALU.mult, ALU.mult))
                v.wait_ge(osq_ready, 2)
                dlink(vtt(Y1[:, 4:8, :], O, orst))

        def add_products(stage, rhs, width, gate):
            freed = sem("freed")
            halves = [(0, TX, 0), (TX, TT, 1)][:1 if width == TX else 2]
            with nc.Block() as block:
                @block.sync
                def _(sp):
                    R.supply(sp, RINGT, weights, START[stage] + 8 + SLOTS)

                @block.tensor
                def _(pe):
                    for m in range(DT):
                        if m >= 2:
                            pe.wait_ge(freed, len(halves) * (m - 1))
                        tile_product(pe, PS[:, (m % 2) * 1024:(m % 2) * 1024 + width], rhs, width)

                @block.vector
                def _(v):
                    for m in range(DT):
                        v.wait_ge(blocks_done, START[stage] + m + 1)
                        for a, b, c in halves:
                            p = PS[:, (m % 2) * 1024 + a:(m % 2) * 1024 + b]
                            if gate is None:
                                vtt(X[:, m, a:b], p, X[:, m, a:b], ALU.add).then_inc(freed, 1)
                            else:
                                stt(X[:, m, a:b], p, gate(m, c), X[:, m, a:b], ALU.mult, ALU.add).then_inc(freed, 1)

        add_products("out1", [Y1[:, k, :] for k in range(DT)], TX, None)

        take = carve()
        H = take(DT, TX)
        PE_ = take(2, TX)
        GT = take(DT, TX)
        sq = take(2, TT)
        RST = take(TT)
        norm_stats([X[:, k, 0:TX] for k in range(DT)], TX, "ones", 1.0 / D, EPS, RST[:, 0:TX],
                   [sq[:, 0, 0:TX], sq[:, 1, 0:TX]], PS)
        with nc.Block() as block:
            @block.sync
            def _(sp):
                sp.dma_start(PE_, pT.rearrange("(k p) t -> p k t", p=P)).then_inc(loads, 16)
                sp.wait_ge(loads, 80)

            @block.vector
            def _(v):
                for k in range(DT):
                    stt(H[:, k, :], X[:, k, 0:TX], V("ple_norm_w", k), RST[:, 0:TX])
        g_read, p_done, p_added = sem("g_read"), sem("p_done"), sem("p_added")
        gated = Chain(sem("gated"))
        with nc.Block() as block:
            @block.sync
            def _(sp):
                R.supply(sp, RINGT, weights, START["conv0"] + SLOTS)

            @block.tensor
            def _(pe):
                for m in range(DT):
                    if m >= 2:
                        pe.wait_ge(g_read, m - 1)
                    tile_product(pe, PS[:, (m % 2) * 512:(m % 2) * 512 + 512], [H[:, k, :] for k in range(DT)], TX)
                for half in range(2):
                    s = R.take(pe)
                    for j in range(4):
                        m = 4 * half + j
                        if m >= 2:
                            pe.wait_ge(p_added, m - 1)
                        for k in range(2):
                            last = mm(PS[:, 1024 + (m % 2) * 512:1536 + (m % 2) * 512],
                                      RINGT[:, s, (2 * j + k) * P:(2 * j + k + 1) * P], PE_[:, k, :], k == 0, k == 1)
                        last.then_inc(p_done, 1)
                    mm(PS[:, 2048:2049], C("ident"), C("ident", 0, 1)).then_inc(blocks_done, 1)

            @block.scalar
            def _(a):
                for m in range(DT):
                    a.wait_ge(blocks_done, START["gate1"] + m + 1)
                    act(GT[:, m, :], PS[:, (m % 2) * 512:(m % 2) * 512 + 512], ACT.Sigmoid, bias=V("b_ple_gate", m)).then_inc(g_read, 1)

            @block.vector
            def _(v):
                for m in range(DT):
                    v.wait_ge(g_read, m + 1)
                    v.wait_ge(p_done, m + 1)
                    vtt(GT[:, m, :], PS[:, 1024 + (m % 2) * 512:1536 + (m % 2) * 512], GT[:, m, :]).then_inc(p_added, 1)
                    v.wait_ge(p_added, m + 1)
                    dlink(vtt(X[:, m, 0:TX], X[:, m, 0:TX], GT[:, m, :], ALU.add))
        norm_stats([X[:, k, 0:TX] for k in range(DT)], TX, "ones", 1.0 / D, EPS, RST[:, 0:TX],
                   [sq[:, 0, 0:TX], sq[:, 1, 0:TX]], PS)
        with nc.Block() as block:
            @block.vector
            def _(v):
                for k in range(DT):
                    stt(X[:, k, 0:TX], X[:, k, 0:TX], V("final_norm_w", k), RST[:, 0:TX])

        def conv_layer(layer, j_, width, next_mod):
            take = carve()
            H = take(DT, TT)
            YP = take(DT, YW)
            G = take(DT, TT)
            Z = take(DT, TT)
            sa, sb_ = take(2, TT), take(2, TT)
            sq = take(2, TT)
            RST = take(TT)
            ME = sa[:, 0, :]
            halves = [(0, TX, 0), (TX, TT, 1)][:1 if width == TX else 2]
            yoff = (PAD, XW + PAD)
            layer_input(layer, (H[:, :, 0:TX], H[:, :, TX:TT]), width, sq, RST)
            stage = f"conv{j_}"
            y_ready, a_read, b_read, g_read, s_free = (sem(n) for n in ("y_ready", "a_read", "b_read", "g_read", "s_free"))
            step = 2 if next_mod is not None else 1
            nh = len(halves)
            with nc.Block() as block:
                @block.sync
                def _(sp):
                    R.supply(sp, RINGT, weights, START[f"convout{j_}"] + SLOTS)

                @block.tensor
                def _(pe):
                    for m in range(DT):
                        for part, read in enumerate((a_read, b_read, g_read)):
                            if m >= 1:
                                pe.wait_ge(read, m)
                            tile_product(pe, PS[:, part * 1024:part * 1024 + width], [H[:, k, :] for k in range(DT)], width)
                            if next_mod is not None:
                                mod_block(pe, 3 * m + part)

                @block.scalar
                def _(a):
                    for m in range(DT):
                        base = START[stage] + step * 3 * m + 1
                        if m >= 2:
                            a.wait_ge(s_free, nh * (m - 1))
                        a.wait_ge(blocks_done, base)
                        act(sa[:, m % 2, 0:width], PS[:, 0:width], ACT.Copy).then_inc(a_read, 1)
                        a.wait_ge(blocks_done, base + step)
                        act(sb_[:, m % 2, 0:width], PS[:, 1024:1024 + width], ACT.Sigmoid).then_inc(b_read, 1)
                        a.wait_ge(blocks_done, base + 2 * step)
                        act(G[:, m, 0:width], PS[:, 2048:2048 + width], ACT.Silu).then_inc(g_read, 1)

                @block.gpsimd
                def _(g):
                    plink(nc.gpsimd.memset(YP, 0.0))
                    for m in range(DT):
                        g.wait_ge(a_read, m + 1)
                        g.wait_ge(b_read, m + 1)
                        for (a, b, c) in halves:
                            nc.gpsimd.tensor_tensor(YP[:, m, yoff[c]:yoff[c] + b - a], sa[:, m % 2, a:b], sb_[:, m % 2, a:b], ALU.mult).then_inc(s_free, 1)

                @block.vector
                def _(v):
                    for m in range(DT):
                        v.wait_ge(s_free, nh * (m + 1))
                        pieces = [(0, TX, yoff[0]), (TX, TT, yoff[1])] if nh == 2 else [(0, TX // 2, yoff[0]), (TX // 2, TX, yoff[0] + TX // 2)]
                        for t in range(TAPS):
                            for n, (a, b, y) in enumerate(pieces):
                                src = YP[:, m, y + t - PAD:y + t - PAD + b - a]
                                wt = V("conv_dw_2", (j_ * TAPS + t) * DT + m)
                                if t == 0:
                                    ins = vts(Z[:, m, a:b], src, wt, V("conv_db_2", j_ * DT + m), ALU.mult, ALU.add)
                                else:
                                    if n == 0:
                                        dve_chain.wait(v)
                                    ins = stt(Z[:, m, a:b], src, wt, Z[:, m, a:b], ALU.mult, ALU.add)
                                dve_chain.inc(ins)
                        dve_chain.wait(v)

            z_summed, centred = sem("z_summed"), sem("centred")
            with nc.Block() as block:
                @block.tensor
                def _(pe):
                    for k in range(DT):
                        last = product(PS, C("ones"), Z[:, k, :], width, k == 0, k == DT - 1)
                    last.then_inc(z_summed, 1)

                @block.scalar
                def _(a):
                    a.wait_ge(z_summed, 1)
                    act(ME[:, 0:width], PS[:, 0:width], ACT.Copy, scale=1.0 / D).then_inc(centred, 1)

                @block.vector
                def _(v):
                    if next_mod is not None:
                        mod_finish(next_mod)
                    v.wait_ge(centred, 1)
                    for k in range(DT):
                        dlink(vtt(Z[:, k, 0:width], Z[:, k, 0:width], ME[:, 0:width], ALU.subtract))
            norm_stats([Z[:, k, 0:width] for k in range(DT)], width, "ones", 1.0 / D, LN_EPS, RST[:, 0:width],
                       [sq[:, 0, 0:width], sq[:, 1, 0:width]], PS)
            scaled, silued = sem("scaled"), sem("silued")
            with nc.Block() as block:
                @block.vector
                def _(v):
                    for k in range(DT):
                        vtt(Z[:, k, 0:width], Z[:, k, 0:width], RST[:, 0:width]).then_inc(scaled, 1)
                        if k >= 1:
                            v.wait_ge(silued, k)
                            vtt(Z[:, k - 1, 0:width], Z[:, k - 1, 0:width], G[:, k - 1, 0:width])
                    v.wait_ge(silued, DT)
                    dlink(vtt(Z[:, DT - 1, 0:width], Z[:, DT - 1, 0:width], G[:, DT - 1, 0:width]))

                @block.scalar
                def _(a):
                    for k in range(DT):
                        a.wait_ge(scaled, k + 1)
                        act(Z[:, k, 0:width], Z[:, k, 0:width], ACT.Silu, scale=V("conv_ln_g_2", j_ * DT + k),
                            bias=V("conv_ln_b_2", j_ * DT + k)).then_inc(silued, 1)
            add_products(f"convout{j_}", [Z[:, k, :] for k in range(DT)], width,
                         lambda m, c: MODL[:, layer, 16 + m, c:c + 1])

        conv_layer(0, 0, TT, 1)

        take = carve()
        HP = take(DT, TT + 4)
        XX = take(DT, TT)
        L2 = take(2, DT, TT)
        sq = L2[:, 0, 0:2, :]
        RST = L2[:, 0, 2, :]
        STG = take(4, TT)
        TW, TA = take(TT), take(TT)
        HALF = [(0, TX, 0), (TX, TT, 1)]
        hoff = (1, TX + 3)
        HH = (HP[:, :, 1:1 + TX], HP[:, :, TX + 3:TX + 3 + TC])
        layer_input(1, HH, TT, sq, RST)
        with nc.Block() as block:
            @block.vector
            def _(v):
                for z in (0, TX + 1, TX + 2, TX + TC + 3):
                    dlink(nc.vector.memset(HP[:, :, z:z + 1], 0.0))
                for a, b, c in HALF:
                    n, o = b - a, hoff[c]
                    dlink(vtt(XX[:, :, a:b], HP[:, :, o - 1:o - 1 + n], HP[:, :, o + 1:o + 1 + n], ALU.add))
                    dlink(stt(XX[:, :, a:b], XX[:, :, a:b], 0.5, HP[:, :, o:o + n], ALU.mult, ALU.subtract))

        lerps = [1, 4, 0, 2, 3, 5]
        l_ready = sem("l_ready")
        l_used, ev = sem("l_used"), sem("ev")
        slot_stored = [sem(f"slot_stored{s}") for s in range(4)]
        t_ready = sem("t_ready")
        outs = [("lora", 0), ("lora", 1)]
        outs += [("w", d, m) for m in range(DT) for d in range(2)]
        outs += [("a", d, m) for m in range(DT) for d in range(2)]
        outs += [("rkvg"[q], q, m) for q in range(4) for m in range(DT)]
        prod = sem("prod")
        NO = len(outs)
        with nc.Block() as block:
            @block.sync
            def _(sp):
                R.supply(sp, RINGT, weights, START["rwkvout"] + SLOTS)

            @block.vector
            def _(v):
                for n, mu in enumerate(lerps):
                    if n >= 2:
                        v.wait_ge(l_used, n - 1)
                    for k in range(DT):
                        for a, b, c in HALF:
                            ins = stt(L2[:, n % 2, k, a:b], XX[:, k, a:b], V("rwkv_mu_2", mu * DT + k),
                                      HP[:, k, hoff[c]:hoff[c] + b - a], ALU.mult, ALU.add)
                            ins.then_inc(l_ready, 1)

            @block.tensor
            def _(pe):
                done = 0

                def area(n):
                    return PS[:, (n % 3) * 1024:(n % 3) * 1024 + TT]

                for n in range(2):
                    pe.wait_ge(l_ready, 16 * (n + 1))
                    s = R.take(pe)
                    w = RINGT[:, s, :].rearrange("p (k m) -> p k m", k=DT)
                    for k in range(DT):
                        last = product(area(n), w[:, k, :], L2[:, n, k, :], TT, k == 0, k == DT - 1)
                    last.then_inc(prod, 1)
                    pe.wait_ge(prod, n + 1)
                    pe.nop().then_inc(blocks_done, 1)
                    pe.nop().then_inc(l_used, 1)
                done = 2
                for kind, T_ in (("w", TW), ("a", TA)):
                    s = R.take(pe)
                    for m in range(DT):
                        for d in range(2):
                            pe.wait_ge(ev, done - 1 if done - 1 > 2 else 2)
                            last = product(area(done), RINGT[d * 64:d * 64 + 64, s, m * P:m * P + P], T_[d * 64:d * 64 + 64, :], TT, True, True)
                            last.then_inc(prod, 1)
                            done += 1
                            pe.wait_ge(prod, done)
                    pe.nop().then_inc(blocks_done, 1)
                for q in range(4):
                    pe.wait_ge(l_ready, 16 * (q + 3))
                    for m in range(DT):
                        pe.wait_ge(ev, done - 2)
                        s = R.take(pe)
                        w = RINGT[:, s, :].rearrange("p (k m) -> p k m", k=DT)
                        for k in range(DT):
                            last = product(area(done), w[:, k, :], L2[:, q % 2, k, :], TT, k == 0, k == DT - 1)
                        last.then_inc(prod, 1)
                        done += 1
                        pe.wait_ge(prod, done)
                        pe.nop().then_inc(blocks_done, 1)
                        if q * DT + m < 24:
                            mod_block(pe, q * DT + m)
                    pe.nop().then_inc(l_used, 1)

            @block.scalar
            def _(a):
                for n, o in enumerate(outs):
                    a.wait_ge(prod, n + 1)
                    src = PS[:, (n % 3) * 1024:(n % 3) * 1024 + TT]
                    if o[0] == "lora":
                        act((TW, TA)[o[1]], src, (ACT.Tanh, ACT.Copy)[o[1]]).then_inc(ev, 1)
                        continue
                    sl = (n - 2) % 4
                    if n >= 6:
                        a.wait_ge(slot_stored[sl], 16 * ((n - 2) // 4))
                    kind, q, m = o
                    if kind in "wa":
                        ins = act(STG[:, sl, :], src, ACT.Sigmoid, bias=V({"w": "rwkv_w0_2", "a": "rwkv_a0_2"}[kind], q * DT + m))
                        at = (4 if kind == "w" else 6) + q
                    else:
                        ins = act(STG[:, sl, :], src, ACT.Silu if kind == "g" else ACT.Copy)
                        at = q
                    ins.then_inc(ev, 1)
                    a.wait_ge(ev, n + 1)
                    a.dma_start(rwkv_dram[m, at], STG[:, sl, :]).then_inc(slot_stored[sl], 16)

        with nc.Block() as block:
            @block.sync
            def _(sp):
                for sl in range(4):
                    sp.wait_ge(slot_stored[sl], 16 * ((NO - 2) // 4))
                sp.dma_start(x_dram, X.rearrange("p k t -> p (k t)")).then_inc(stores, 16)
                sp.wait_ge(stores, 16)

            @block.vector
            def _(v):
                mod_finish(2)

        take = carve()
        GM = [take(NSTEP, 2, P) for _ in range(2)]
        TINV = [take(NSTEP, P) for _ in range(2)]
        BKT = [take(NSTEP, 2, CH) for _ in range(2)]
        UV = [take(NSTEP, 2, CH) for _ in range(2)]
        AV = [take(NSTEP, CH) for _ in range(2)]
        AR = [take(NSTEP, 2, CH) for _ in range(2)]
        EBC = [take(NSTEP) for _ in range(2)]
        BK = take(NSTEP, 2, CH)
        VS = take(TT + 2 * CH)
        BON, BONV, GATE = take(TT), take(TT), take(TT)
        O2 = take(2, TT)
        KK, A_, B_, C_, D_, E_, F_ = (take(TT) for _ in range(7))
        OS = take(TT)
        ST = take(2, CH)
        RS = take(CH)
        PC = take(6)
        PCF = take(2)
        IN = X.rearrange("p k t -> p (k t)").rearrange("p (q t) -> p q t", q=8)
        GU = 3
        grp = [{n: take(GU, P) for n in ("AT", "PQ", "PT", "T1", "NT0", "NT1")} for _ in range(2)]
        CM = take(TT)
        NSUP = NSTEP // (2 * GU)
        NLV = 5

        loaded, y_out = sem("pair_loaded"), sem("y_out")
        m_sem = {n: sem(n) for n in ("dve_prep", "kk_ready", "kk_squared", "kk_summed", "kk_logged", "kk_root", "b_ready", "exp_ready",
                                     "a_laid", "a_turned", "dve_inv", "n_masked", "p_ready", "t_done", "t_copied", "up_done",
                                     "pt_added", "state_ready", "r_done", "r_added", "u_done", "u_low", "u_high",
                                     "s_done", "o_done", "o_copied")}
        q_sem = {n: sem(n) for n in ("dve_q", "ar_ready", "v_ready", "v_turned", "v_copied", "g_done", "g_masked", "bk_decayed",
                                     "av_done", "bk_turned", "bonus_done",
                                     "f_dve", "f_summed", "f_act", "bonus_read")}

        def chunk3(t):
            return t.rearrange("p (n t) -> p n t", t=CH)

        def bank(n, w=512):
            return PS[:, n * 512:n * 512 + w]

        HS = (slice(0, 64), slice(64, 128))

        def prep_vector(v, d, i):
            ch = Chain(m_sem["dve_prep"])
            if d == 0:
                v.wait_ge(loaded, i * 16 + 16)
                for q, n in enumerate(("rwkv_k_k_2", "rwkv_k_a_2", "rwkv_r_k_2", "rwkv_ln_g_2", "rwkv_ln_b_2")):
                    ch.link(v, nc.vector.tensor_copy(PC[:, q:q + 1], VEC[:, bass.ds(i + VT[n][0], 1)]))
                ch.link(v, vts(PC[:, 5:6], PC[:, 1:2], -1.0, 1.0, ALU.mult, ALU.add))
                vts(KK, IN[:, 1, :], PC[:, 0:1]).then_inc(m_sem["kk_ready"], 1)
                yield
            ch.link(v, vts(B_, IN[:, 4 + d, :], -float(np.exp(-0.5))))
            yield
            o = 1 if d == 0 else -1
            ch.link(v, nc.vector.tensor_tensor_scan(C_[:, ::o], CM, B_[:, ::o], 0.0, ALU.mult, ALU.add))
            yield
            vtt(B_, C_, B_, ALU.subtract).then_inc(m_sem["b_ready"], 1)
            yield
            ch.link(v, vts(A_, IN[:, 6 + d, :], PC[:, 1:2], PC[:, 5:6], ALU.mult, ALU.add))
            yield
            ch.link(v, vtt(A_, A_, IN[:, 1, :]))
            yield
            if d == 0:
                ch.link(v, nc.vector.tensor_copy(BON, A_))
            else:
                ch.link(v, vtt(BON, BON, A_, ALU.add))
                yield
                ch.link(v, stt(BON, IN[:, 0, :], PC[:, 2:3], BON, ALU.mult, ALU.mult))
            yield
            v.wait_ge(m_sem["exp_ready"], 3)
            for h in range(2):
                ch.link(v, vtt(BK[HS[h], :, 1 - h, :], chunk3(A_)[HS[h]], chunk3(E_)[HS[h]]))
                yield
            if d == 0:
                v.wait_ge(m_sem["kk_root"], 1)
                ch.link(v, vtt(KK, KK, OS))
                yield
            ch.link(v, vtt(A_, KK, IN[:, 6 + d, :]))
            yield
            for h in range(2):
                ch.inc(vtt(BK[HS[h], :, h, :], chunk3(A_)[HS[h]], chunk3(E_)[HS[h]]))
                yield

        def prep_scalar(a, d):
            if d == 0:
                a.wait_ge(m_sem["kk_ready"], 1)
                act(F_, KK, ACT.Square).then_inc(m_sem["kk_squared"], 1)
                yield
                for n, (lo, hi) in enumerate(((0, 512), (512, TT))):
                    a.wait_ge(m_sem["kk_summed"], n + 1)
                    act(OS[:, lo:hi], bank(4 + n, hi - lo), ACT.Ln, bias=EPSC[1e-12]).then_inc(m_sem["kk_logged"], 1)
                yield
                a.wait_ge(m_sem["kk_logged"], 2)
                act(OS, OS, ACT.Exp, scale=-0.5).then_inc(m_sem["kk_root"], 1)
                yield
            else:
                yield
                yield
                yield
            a.wait_ge(m_sem["b_ready"], 1)
            act(E_, C_, ACT.Exp, scale=-1.0).then_inc(m_sem["exp_ready"], 1)
            yield
            act(F_, B_, ACT.Exp).then_inc(m_sem["exp_ready"], 1)
            yield
            act(D_, C_, ACT.Exp).then_inc(m_sem["exp_ready"], 1)
            yield

        def prep_tensor(pe, d):
            if d == 0:
                pe.wait_ge(m_sem["kk_squared"], 1)
                mm(bank(4), C("ones64"), F_[:, 0:512]).then_inc(m_sem["kk_summed"], 1)
                mm(bank(5, TT - 512), C("ones64"), F_[:, 512:TT]).then_inc(m_sem["kk_summed"], 1)
                yield

        identb = C("ident").rearrange("p (o t) -> p o t", o=1).broadcast_to([P, GU, P])

        def maskb(level):
            return C("inv_mask", level * P, P).rearrange("p (o t) -> p o t", o=1).broadcast_to([P, GU, P])

        def bank3(n):
            return bank(n, GU * P).rearrange("p (q t) -> p q t", q=GU)

        INV_SLOTS = NSUP * (2 + 4 * NLV)

        def inv_tensor(pe, d, kk_beside):
            for s in range(NSUP):
                for e in range(2):
                    g, n = grp[e], 2 * s + e
                    pe.wait_ge(m_sem["a_laid"], n + 1)
                    for q in range(GU):
                        last = nc.tensor.transpose(bank(3 * e)[:, q * P:q * P + P], g["AT"][:, q, :], C("ident"))
                    last.then_inc(m_sem["a_turned"], 1)
                    yield
                for lv in range(NLV):
                    for e in range(2):
                        g, n = grp[e], (s * NLV + lv) * 2 + e
                        pe.wait_ge(m_sem["n_masked"], n + 1)
                        pe.wait_ge(m_sem["p_ready"], n + 1)
                        for q in range(GU):
                            last = mm(bank(3 * e)[:, q * P:q * P + P], g[f"NT{lv % 2}"][:, q, :], g["PQ"][:, q, :])
                        last.then_inc(m_sem["t_done"], 1)
                        yield
                    for e in range(2):
                        g, n = grp[e], (s * NLV + lv) * 2 + e
                        pe.wait_ge(m_sem["t_copied"], n + 1)
                        if lv > 0:
                            pe.wait_ge(m_sem["pt_added"], 2 * (s * (NLV - 1) + lv - 1) + e + 1)
                        if kk_beside and n == 1:
                            pe.wait_ge(m_sem["kk_logged"], 2)
                        for q in range(GU):
                            last = mm(bank(3 * e + 1)[:, q * P:q * P + P], g["T1"][:, q, :], g["PT"][:, q, :])
                        if lv < NLV - 1:
                            for q in range(GU):
                                last = mm(bank(3 * e + 2)[:, q * P:q * P + P], g["PT"][:, q, :], g["T1"][:, q, :])
                        last.then_inc(m_sem["up_done"], 1)
                        yield

        def inv_pool(gp):
            for s in range(NSUP):
                for lv in range(NLV):
                    for e in range(2):
                        g, n = grp[e], (s * NLV + lv) * 2 + e
                        if lv == 0:
                            gp.wait_ge(m_sem["a_laid"], 2 * s + e + 1)
                        if n >= 4:
                            gp.wait_ge(m_sem["t_done"], n - 3)
                        nc.gpsimd.tensor_tensor(g[f"NT{lv % 2}"], g["AT"], maskb(lv + 1), ALU.mult).then_inc(m_sem["n_masked"], 1)

        def inv_scalar(a):
            for s in range(NSUP):
                yield
                yield
                for lv in range(NLV):
                    for e in range(2):
                        n = (s * NLV + lv) * 2 + e
                        a.wait_ge(m_sem["t_done"], n + 1)
                        act(grp[e]["T1"], bank3(3 * e), ACT.Copy).then_inc(m_sem["t_copied"], 1)
                        yield
                    yield
                    yield

        def inv_vector(v, d):
            ch = Chain(m_sem["dve_inv"])
            for s in range(NSUP):
                for e in range(2):
                    g, n = grp[e], 2 * s + e
                    if s >= 1:
                        v.wait_ge(m_sem["n_masked"], s * 2 * NLV)
                    us = slice(GU * n, GU * n + GU)
                    ch.link(v, nc.vector.tensor_copy(g["AT"][0:64, :, 0:64], GM[d][0:64, us, 0, 0:64]))
                    nc.vector.tensor_copy(g["AT"][64:128, :, 64:128], GM[d][64:128, us, 1, 64:128]).then_inc(m_sem["a_laid"], 1)
                    v.wait_ge(m_sem["a_laid"], n + 1)
                    ch.link(v, vtt(g["PT"], g["AT"], maskb(0)))
                    ch.link(v, vtt(g["PT"], g["PT"], identb, ALU.add))
                    v.wait_ge(m_sem["a_turned"], n + 1)
                    ch.link(v, vtt(g["PQ"], bank3(3 * e), maskb(0)))
                    vtt(g["PQ"], g["PQ"], identb, ALU.add).then_inc(m_sem["p_ready"], 1)
                    yield
                for lv in range(NLV):
                    yield
                    yield
                    for e in range(2):
                        g, n = grp[e], (s * NLV + lv) * 2 + e
                        v.wait_ge(m_sem["up_done"], n + 1)
                        if lv > 0:
                            v.wait_ge(m_sem["pt_added"], 2 * (s * (NLV - 1) + lv - 1) + e + 1)
                        if lv == NLV - 1:
                            u0 = GU * (2 * s + e)
                            ch.inc(vtt(TINV[d][:, u0:u0 + GU, :], bank3(3 * e + 1), g["PT"], ALU.add))
                        else:
                            vtt(g["PQ"], bank3(3 * e + 2), g["PQ"], ALU.add).then_inc(m_sem["p_ready"], 1)
                            vtt(g["PT"], bank3(3 * e + 1), g["PT"], ALU.add).then_inc(m_sem["pt_added"], 1)
                        yield

        def chunk_of(d, st):
            return (NCX + st) % NSTEP if d == 0 else NSTEP - 1 - st

        R_, U_, S_ = (PS[:, 6 * 512 + n * CH:6 * 512 + n * CH + CH] for n in range(3))
        O_ = PS[:, 7 * 512:7 * 512 + CH]
        CHAIN_SLOTS = 3 * NSTEP

        def chain_tensor(pe, d):
            for st in range(NSTEP):
                u = chunk_of(d, st)
                S = ST[:, st % 2, :]
                pe.wait_ge(m_sem["state_ready"], st + 1)
                for h in range(2):
                    last = mm(R_[HS[h]], AR[d][HS[h], u, 0, :], S[HS[h]])
                last.then_inc(m_sem["r_done"], 1)
                yield
                pe.wait_ge(m_sem["r_added"], st + 1)
                mm(U_, TINV[d][:, u, :], RS).then_inc(m_sem["u_done"], 1)
                yield
                pe.wait_ge(m_sem["u_low"], st + 1)
                pe.wait_ge(m_sem["u_high"], st + 1)
                for h in range(2):
                    last = mm(S_[HS[h]], BKT[d][:, u, h, :], UV[d][:, u, h, :])
                last.then_inc(m_sem["s_done"], 1)
                if st >= 1:
                    pe.wait_ge(m_sem["o_copied"], st)
                for h in range(2):
                    rc = slice(64, 128) if h == 0 else slice(0, 64)
                    mm(O_[HS[h]], UV[d][:, u, h, :], GM[d][:, u, h, rc], True, False)
                    last = mm(O_[HS[h]], S[HS[h]], AR[d][HS[h], u, 1, :], False, True)
                last.then_inc(m_sem["o_done"], 1)
                yield

        def chain_vector(v, d):
            nc.vector.memset(ST[:, 0, :], 0.0).then_inc(m_sem["state_ready"], 1)
            for st in range(NSTEP):
                u = chunk_of(d, st)
                v.wait_ge(m_sem["r_done"], st + 1)
                vtt(RS, R_, AV[d][:, u, :], ALU.add).then_inc(m_sem["r_added"], 1)
                yield
                v.wait_ge(m_sem["u_done"], st + 1)
                nc.vector.tensor_copy(UV[d][0:64, u, 0, :], U_[0:64]).then_inc(m_sem["u_low"], 1)
                yield
                v.wait_ge(m_sem["s_done"], st + 1)
                if st >= 1:
                    v.wait_ge(m_sem["o_done"], st)
                v.wait_ge(m_sem["state_ready"], st + 1)
                stt(ST[:, (st + 1) % 2, :], ST[:, st % 2, :], EBC[d][:, u:u + 1], S_, ALU.mult, ALU.add).then_inc(m_sem["state_ready"], 1)
                yield

        def chain_scalar(a, d):
            for st in range(NSTEP):
                u = chunk_of(d, st)
                yield
                a.wait_ge(m_sem["u_done"], st + 1)
                act(UV[d][64:128, u, 1, :], U_[64:128], ACT.Copy).then_inc(m_sem["u_high"], 1)
                yield
                a.wait_ge(m_sem["o_done"], st + 1)
                act(O2[:, d, u * CH:u * CH + CH], O_, ACT.Copy).then_inc(m_sem["o_copied"], 1)
                yield

        def advance(gen):
            return next(gen, None) if gen is not None else None

        def interleave(inv, chain, prep):
            done = 0
            for t in range(INV_SLOTS if inv is not None else CHAIN_SLOTS):
                advance(inv)
                while chain is not None and done * INV_SLOTS < (t + 1) * CHAIN_SLOTS:
                    advance(chain)
                    done += 1
                if inv is None or (t % (2 + 4 * NLV) >= 2 and (t % (2 + 4 * NLV) - 2) % 4 < 2):
                    advance(prep)
            for gen in (inv, chain, prep):
                for _ in gen or ():
                    pass

        def long_block(inv_d, chain_d, prep_d, i, load):
            with nc.Block() as block:
                @block.sync
                def _(sp):
                    if load is not None:
                        sp.wait_ge(y_out, load * 16)
                        sp.dma_start(IN, rwkv_dram[bass.ds(load, 1)].rearrange("a q p t -> p (a q) t")).then_inc(loaded, 16)

                @block.tensor
                def _(pe):
                    interleave(None if inv_d is None else inv_tensor(pe, inv_d, prep_d == 0), None if chain_d is None else chain_tensor(pe, chain_d),
                               None if prep_d is None else prep_tensor(pe, prep_d))

                @block.vector
                def _(v):
                    interleave(None if inv_d is None else inv_vector(v, inv_d), None if chain_d is None else chain_vector(v, chain_d),
                               None if prep_d is None else prep_vector(v, prep_d, i))

                @block.scalar
                def _(a):
                    interleave(None if inv_d is None else inv_scalar(a), None if chain_d is None else chain_scalar(a, chain_d),
                               None if prep_d is None else prep_scalar(a, prep_d))

                @block.gpsimd
                def _(gp):
                    for s in q_sem.values():
                        gp.sem_clear(s)
                    if inv_d is not None:
                        inv_pool(gp)

        def products_block(d):
            with nc.Block() as block:
                @block.vector
                def _(v):
                    ch = Chain(q_sem["dve_q"])
                    if d == 0:
                        nc.vector.tensor_copy(VS[:, CH:CH + TT], IN[:, 2, :]).then_inc(q_sem["v_ready"], 1)
                    vtt(AR[d][:, :, 1, :], chunk3(IN[:, 0, :]), chunk3(D_)).then_inc(q_sem["ar_ready"], 1)
                    stt(AR[d][:, :, 0, :], chunk3(KK), -1.0, chunk3(F_), ALU.mult, ALU.mult).then_inc(q_sem["ar_ready"], 1)
                    at = CH - 1 if d == 0 else 0
                    ch.link(v, nc.vector.tensor_copy(EBC[d].rearrange("p (n o) -> p n o", o=1), chunk3(D_)[:, :, at:at + 1]))
                    for g in range(3):
                        for h in range(2):
                            n = 2 * g + h
                            v.wait_ge(q_sem["g_done"], n + 1)
                            m = C("wkv_mask", d * 256 + h * P, P).rearrange("p (o t) -> p o t", o=1).broadcast_to([P, 4, P])
                            vtt(GM[d][:, 4 * g:4 * g + 4, h, :], bank(2 * (g % 2) + h).rearrange("p (q t) -> p q t", q=4), m).then_inc(q_sem["g_masked"], 1)
                    e = EBC[d].rearrange("p (n o) -> p n o", o=1).broadcast_to([P, NSTEP, P])
                    b = BK.rearrange("p n s t -> p n (s t)")
                    vtt(b, b, e).then_inc(q_sem["bk_decayed"], 1)
                    if d == 1:
                        v.wait_ge(q_sem["bonus_done"], 1)
                        vtt(BONV, PS[:, 3072:3072 + TT], VS[:, CH:CH + TT])
                        nc.vector.tensor_copy(GATE, IN[:, 3, :])
                        nc.vector.tensor_copy(PCF, PC[:, 3:5])
                    v.wait_ge(q_sem["av_done"], 1)
                    nc.vector.tensor_copy(AV[d], chunk3(PS[:, 2048:2048 + TT]))

                @block.tensor
                def _(pe):
                    if d == 0:
                        pe.wait_ge(q_sem["v_ready"], 1)
                    for h in range(2):
                        idh = CON[HS[h], CT["ident"][0] + 64 * h:CT["ident"][0] + 64 * h + 64]
                        for c in range(NSTEP):
                            o = (4 + 2 * h) * 512 + c * CH
                            last = nc.tensor.transpose(PS[:, o:o + CH], VS[HS[h], (c + h) * CH:(c + h) * CH + P], idh)
                        last.then_inc(q_sem["v_turned"], 1)
                    pe.wait_ge(q_sem["ar_ready"], 2)
                    for g in range(3):
                        for h in range(2):
                            if g == 2:
                                pe.wait_ge(q_sem["g_masked"], h + 1)
                            o = 1 if h == 0 else -1
                            for q in range(4):
                                u = 4 * g + q
                                last = mm(bank(2 * (g % 2) + h)[:, q * P:q * P + P], BK[HS[h], u].rearrange("p s t -> p (s t)"), AR[d][HS[h], u, ::o, :])
                            last.then_inc(q_sem["g_done"], 1)
                    pe.wait_ge(q_sem["v_copied"], 2)
                    if d == 1:
                        product(PS[:, 3072:3072 + TT], C("ones64"), BON, TT, True, True).then_inc(q_sem["bonus_done"], 1)
                    pe.wait_ge(q_sem["g_masked"], 6)
                    for u in range(NSTEP):
                        for h in range(2):
                            kr = HS[1 - h]
                            last = mm(PS[HS[h], 2048 + u * CH:2048 + u * CH + CH], GM[d][kr, u, h, 64 * h:64 * h + 64], UV[d][kr, u, h, :])
                    last.then_inc(q_sem["av_done"], 1)
                    pe.wait_ge(q_sem["bk_decayed"], 1)
                    for h in range(2):
                        idh = CON[HS[h], CT["ident"][0] + 64 * h:CT["ident"][0] + 64 * h + 64]
                        for u in range(NSTEP):
                            o = h * 1024 + u * CH
                            last = nc.tensor.transpose(PS[:, o:o + CH], BK[HS[h], u].rearrange("p s t -> p (s t)"), idh)
                        last.then_inc(q_sem["bk_turned"], 1)

                @block.scalar
                def _(a):
                    for h in range(2):
                        a.wait_ge(q_sem["v_turned"], h + 1)
                        act(UV[d][:, :, h, :], chunk3(PS[:, (4 + 2 * h) * 512:(4 + 2 * h) * 512 + TT]), ACT.Copy).then_inc(q_sem["v_copied"], 1)
                    for h in range(2):
                        a.wait_ge(q_sem["bk_turned"], h + 1)
                        act(BKT[d][:, :, h, :], chunk3(PS[:, h * 1024:h * 1024 + TT]), ACT.Copy)

                @block.gpsimd
                def _(gp):
                    for s in m_sem.values():
                        gp.sem_clear(s)

        def readout_block(dst):
            SQ_, RT_ = A_, B_
            with nc.Block() as block:
                @block.vector
                def _(v):
                    ch = Chain(q_sem["f_dve"])
                    ch.link(v, vtt(OS, O2[:, 0, :], O2[:, 1, :], ALU.add))
                    v.wait_ge(q_sem["f_summed"], 1)
                    ch.link(v, stt(OS, PS[:, 0:TT], -1.0 / CH, OS, ALU.mult, ALU.add))
                    v.wait_ge(q_sem["f_act"], 3)
                    ch.link(v, vtt(OS, OS, RT_))
                    ch.link(v, vts(OS, OS, PCF[:, 0:1], PCF[:, 1:2], ALU.mult, ALU.add))
                    ch.link(v, vtt(OS, OS, BONV, ALU.add))
                    ch.inc(vtt(OS, OS, GATE))

                @block.tensor
                def _(pe):
                    pe.wait_ge(q_sem["f_dve"], 1)
                    product(PS[:, 0:TT], C("ones64"), OS, TT, True, True).then_inc(q_sem["f_summed"], 1)
                    pe.wait_ge(q_sem["f_act"], 1)
                    product(PS[:, 1024:1024 + TT], C("ones64"), SQ_, TT, True, True).then_inc(q_sem["f_summed"], 1)

                @block.scalar
                def _(a):
                    a.wait_ge(q_sem["f_dve"], 2)
                    act(SQ_, OS, ACT.Square).then_inc(q_sem["f_act"], 1)
                    a.wait_ge(q_sem["f_summed"], 2)
                    act(RT_, PS[:, 1024:1024 + TT], ACT.Ln, scale=1.0 / CH, bias=EPSC[GN_EPS]).then_inc(q_sem["f_act"], 1)
                    a.wait_ge(q_sem["f_act"], 2)
                    act(RT_, RT_, ACT.Exp, scale=-0.5).then_inc(q_sem["f_act"], 1)

                @block.sync
                def _(sp):
                    sp.wait_ge(q_sem["f_dve"], 6)
                    sp.dma_start(dst, OS).then_inc(y_out, 16)

        with nc.Block() as block:
            @block.vector
            def _(v):
                nc.vector.memset(CM, 1.0)
                nc.vector.memset(VS, 0.0)
                for g in grp:
                    dlink(nc.vector.memset(g["AT"], 0.0))
                dlink(nc.vector.memset(chunk3(CM)[:, :, 0:1], 0.0))

            @block.sync
            def _(sp):
                sp.dma_start(rwkv_dram[DT], rwkv_dram[0]).then_inc(y_out, 16)
                sp.dma_start(IN, rwkv_dram[0].rearrange("q p t -> p q t")).then_inc(loaded, 16)

        long_block(None, None, 0, 0, None)
        products_block(0)
        long_block(0, None, 1, 0, None)
        products_block(1)
        long_block(1, 0, 0, 1, 1)
        products_block(0)
        with nc.Fori(1, NPAIR) as i:
            long_block(0, 1, 1, i, None)
            readout_block(y_dram[bass.ds(i - 1, 1)].rearrange("a p t -> p (a t)"))
            products_block(1)
            long_block(1, 0, 0, i + 1, i + 1)
            products_block(0)
        long_block(None, 1, None, NPAIR, None)
        readout_block(y_dram[NPAIR - 1])

        take = carve()
        YR = take(DT, TT)
        with nc.Block() as block:
            @block.sync
            def _(sp):
                sp.wait_ge(y_out, 16 * (NPAIR + 1))
                sp.wait_ge(loaded, 16 * (NPAIR + 1))
                sp.dma_start(YR, y_dram.rearrange("k p t -> p k t")).then_inc(loads, 16)
                sp.dma_start(X.rearrange("p k t -> p (k t)"), x_dram).then_inc(loads, 16)
                sp.wait_ge(loads, 112)
        add_products("rwkvout", [YR[:, k, :] for k in range(DT)], TT, lambda m, c: MODL[:, 1, 16 + m, c:c + 1])

        NQ, NKV = 16, 8
        KTILES = TT // P
        SCALE = float(P) ** -0.5
        take = carve()
        G = take(NQ, TX)
        Q = take(NQ, TX)
        K = take(NKV, TT)
        VT_ = take(KTILES, D)
        H = take(DT, TT)
        PR = take(2, TT)
        ROPE = take(2, TX)
        STAT = take(2, 4)
        layer_input(2, (H[:, :, 0:TX], H[:, :, TX:TT]), TT, PR, Q[:, 0:2, :].rearrange("p a b -> p (a b)")[:, 0:TT])
        freed = sem("freed")
        kinds = [("q", m) for m in range(NQ)] + [("k", m) for m in range(NKV)] + [("v", m) for m in range(DT)] + [("g", m) for m in range(NQ)]

        def block_of(n):
            return START["attn_qk"] + (2 * n if n < 24 else n + 24)

        with nc.Block() as block:
            @block.sync
            def _(sp):
                sp.dma_start(ROPE.rearrange("p a t -> p (a t)"), rope).then_inc(loads, 16)
                sp.wait_ge(loads, 128)
                R.supply(sp, RINGT, weights, START["attnout"] + SLOTS)

            @block.tensor
            def _(pe):
                for n, (kind, m) in enumerate(kinds):
                    if n >= 3:
                        pe.wait_ge(freed, n - 2)
                    o = PS[:, (n % 3) * 1024:(n % 3) * 1024 + 1024]
                    if kind == "v":
                        s = R.take(pe)
                        w = RINGT[:, s, :].rearrange("p (k m) -> p k m", k=DT)
                        for t in range(KTILES):
                            for k in range(DT):
                                last = mm(o[:, t * P:t * P + P], H[:, k, t * P:t * P + P], w[:, k, :], k == 0, k == DT - 1)
                        last.then_inc(blocks_done, 1)
                    else:
                        width = TT if kind == "k" else TX
                        tile_product(pe, o, [H[:, k, :] for k in range(DT)], width)
                    if n < 24:
                        mod_block(pe, n)

            @block.scalar
            def _(a):
                for n, (kind, m) in enumerate(kinds):
                    a.wait_ge(blocks_done, block_of(n) + 1)
                    o = PS[:, (n % 3) * 1024:(n % 3) * 1024 + TT]
                    if kind == "v":
                        ins = act(VT_[:, :, m * P:m * P + P], o.rearrange("p (t v) -> p t v", t=KTILES), ACT.Copy)
                    elif kind == "k":
                        ins = act(K[:, m, :], o, ACT.Copy)
                    elif kind == "q":
                        ins = act(Q[:, m, :], o[:, 0:TX], ACT.Copy)
                    else:
                        ins = act(G[:, m, :], o[:, 0:TX], ACT.Silu)
                    ins.then_inc(freed, 1)

        tiles = [(Q[:, m, :], TX, V("attn_q_g_2")) for m in range(NQ)] + [(K[:, m, :], TT, V("attn_k_g_2")) for m in range(NKV)]
        sqd, summed, rst_, rs_used, normed, rotated, roped = (sem(n) for n in ("sqd", "summed", "rst", "rs_used", "normed", "rotated", "roped"))
        HF = H.rearrange("p a b -> p (a b)")
        SQ_ = [HF[:, n * TT:n * TT + TT] for n in range(2)]
        RS_ = [HF[:, (2 + n) * TT:(3 + n) * TT] for n in range(2)]
        SN_ = [HF[:, (4 + n) * TT:(4 + n) * TT + TX] for n in range(2)]
        NT_ = len(tiles)
        with nc.Block() as block:
            @block.scalar
            def _(a):
                for n in range(NT_ + 1):
                    if n < NT_:
                        x_, w, _g = tiles[n]
                        if n >= 2:
                            a.wait_ge(summed, n - 1)
                        act(SQ_[n % 2][:, 0:w], x_[:, 0:w], ACT.Square).then_inc(sqd, 1)
                    if n >= 1:
                        m = n - 1
                        x_, w, _g = tiles[m]
                        a.wait_ge(summed, m + 1)
                        if m >= 2:
                            a.wait_ge(normed, m - 1)
                        alink(act(RS_[m % 2][:, 0:w], PS[:, (m % 2) * 1024:(m % 2) * 1024 + w], ACT.Ln, scale=1.0 / P, bias=EPSC[EPS]))
                        act(RS_[m % 2][:, 0:w], RS_[m % 2][:, 0:w], ACT.Exp, scale=-0.5).then_inc(rst_, 1)

            @block.tensor
            def _(pe):
                for n in range(NT_ + 1):
                    if n < NT_:
                        pe.wait_ge(sqd, n + 1)
                        if n >= 2:
                            pe.wait_ge(rst_, n - 1)
                        product(PS[:, (n % 2) * 1024:(n % 2) * 1024 + tiles[n][1]], C("ones"), SQ_[n % 2], tiles[n][1], True, True).then_inc(summed, 1)
                    if n >= 1:
                        m = n - 1
                        pe.wait_ge(normed, m + 1)
                        if m >= 2:
                            pe.wait_ge(rotated, m - 1)
                        mm(PS[:, 2048 + (m % 2) * 512:2048 + (m % 2) * 512 + 512], C("rot"), tiles[m][0][:, 0:TX]).then_inc(roped, 1)

            @block.vector
            def _(v):
                mod_finish(3)
                for n in range(NT_ + 1):
                    if n < NT_:
                        x_, w, g_ = tiles[n]
                        v.wait_ge(rst_, n + 1)
                        stt(x_[:, 0:w], x_[:, 0:w], g_, RS_[n % 2][:, 0:w]).then_inc(normed, 1)
                    if n >= 1:
                        m = n - 1
                        x_ = tiles[m][0]
                        v.wait_ge(roped, m + 1)
                        dve_chain.inc(vtt(SN_[m % 2], PS[:, 2048 + (m % 2) * 512:2048 + (m % 2) * 512 + 512], ROPE[:, 1, :]))
                        vtt(x_[:, 0:TX], x_[:, 0:TX], ROPE[:, 0, :]).then_inc(rotated, 1)
                        dve_chain.wait(v)
                        v.wait_ge(rotated, m + 1)
                        dlink(vtt(x_[:, 0:TX], x_[:, 0:TX], SN_[m % 2], ALU.add))

        NQB = TX // P
        N = NQ * NQB
        PTS = HF.rearrange("p (e k t) -> p e k t", e=2, k=KTILES)
        s_done, negmax, exped, scaled, tr0, tr1, cp0, cp1, pv_done, o_read = (
            sem(n) for n in ("s_done", "negmax", "exped", "scaled", "tr0", "tr1", "cp0", "cp1", "pv_done", "o_read"))
        with nc.Block() as block:
            @block.tensor
            def _(pe):
                def scores(n):
                    h, qb = n // NQB, n % NQB
                    if n >= 2:
                        pe.wait_ge(exped, n - 1)
                    product(PS[:, (n % 2) * 1024:(n % 2) * 1024 + TT], Q[:, h, qb * P:qb * P + P], K[:, h // 2, :], TT, True, True).then_inc(s_done, 1)

                scores(0)
                for n in range(N):
                    h, qb = n // NQB, n % NQB
                    if n + 1 < N:
                        scores(n + 1)
                    pe.wait_ge(scaled, n + 1)
                    if n >= 1:
                        pe.wait_ge(cp0, n)
                    for k in range(4):
                        last = nc.tensor.transpose(PS[:, 2048 + k * P:2048 + k * P + P], PR[:, n % 2, k * P:k * P + P], C("ident"))
                    last.then_inc(tr0, 1)
                    if n >= 1:
                        pe.wait_ge(cp1, n)
                    for k in range(4, KTILES):
                        last = nc.tensor.transpose(PS[:, 2048 + k * P:2048 + k * P + P], PR[:, n % 2, k * P:k * P + P], C("ident"))
                    last.then_inc(tr1, 1)
                    if qb == NQB - 1:
                        pe.wait_ge(cp0, n + 1)
                        pe.wait_ge(cp1, n + 1)
                        if h >= 2:
                            pe.wait_ge(o_read, h - 1)
                        for k in range(KTILES):
                            last = mm(PS[:, 3072 + (h % 2) * 512:3072 + (h % 2) * 512 + 512], VT_[:, k, (h // 2) * P:(h // 2) * P + P],
                                      PTS[:, h % 2, k, :], k == 0, k == KTILES - 1)
                        last.then_inc(pv_done, 1)

            @block.vector
            def _(v):
                def maxima(n):
                    v.wait_ge(s_done, n + 1)
                    dlink(nc.vector.reduce_max(STAT[:, n % 2, 0:1], PS[:, (n % 2) * 1024:(n % 2) * 1024 + TT], AX.X))
                    vts(STAT[:, n % 2, 1:2], STAT[:, n % 2, 0:1], -SCALE).then_inc(negmax, 1)

                maxima(0)
                for n in range(N):
                    h, qb = n // NQB, n % NQB
                    if n + 1 < N:
                        maxima(n + 1)
                    v.wait_ge(exped, n + 1)
                    dlink(nc.vector.reciprocal(STAT[:, n % 2, 3:4], STAT[:, n % 2, 2:3]))
                    vts(PR[:, n % 2, :], PR[:, n % 2, :], STAT[:, n % 2, 3:4]).then_inc(scaled, 1)
                    v.wait_ge(tr1, n + 1)
                    if n >= 8 and qb == 0:
                        v.wait_ge(pv_done, h - 1)
                    nc.vector.tensor_copy(PTS[:, h % 2, 4:6, qb * P:qb * P + P],
                                          PS[:, 2560:2560 + 2 * P].rearrange("p (k t) -> p k t", k=2)).then_inc(cp1, 1)
                    if qb == 1 and h >= 1:
                        v.wait_ge(pv_done, h)
                        vtt(G[:, h - 1, :], PS[:, 3072 + ((h - 1) % 2) * 512:3072 + ((h - 1) % 2) * 512 + 512], G[:, h - 1, :]).then_inc(o_read, 1)
                v.wait_ge(pv_done, NQ)
                dlink(vtt(G[:, NQ - 1, :], PS[:, 3072 + 512:3072 + 1024], G[:, NQ - 1, :]))

            @block.scalar
            def _(a):
                for n in range(N):
                    h, qb = n // NQB, n % NQB
                    a.wait_ge(negmax, n + 1)
                    if n >= 2:
                        a.wait_ge(tr1, n - 1)
                    act(PR[:, n % 2, :], PS[:, (n % 2) * 1024:(n % 2) * 1024 + TT], ACT.Exp, bias=STAT[:, n % 2, 1:2],
                        scale=SCALE, accum_out=STAT[:, n % 2, 2:3]).then_inc(exped, 1)
                    a.wait_ge(tr0, n + 1)
                    if n >= 8 and qb == 0:
                        a.wait_ge(pv_done, h - 1)
                    act(PTS[:, h % 2, 0:4, qb * P:qb * P + P], PS[:, 2048:2560].rearrange("p (k t) -> p k t", k=4), ACT.Copy).then_inc(cp0, 1)

        added = sem("added")
        with nc.Block() as block:
            @block.sync
            def _(sp):
                R.supply(sp, RINGT, weights, START["conv1"] + SLOTS)

            @block.tensor
            def _(pe):
                for m in range(DT):
                    if m >= 2:
                        pe.wait_ge(added, m - 1)
                    for half in range(2):
                        s = R.take(pe)
                        w = RINGT[:, s, :].rearrange("p (k m) -> p k m", k=DT)
                        for k in range(DT):
                            last = mm(PS[:, (m % 2) * 512:(m % 2) * 512 + 512], w[:, k, :], G[:, 8 * half + k, :],
                                      half == 0 and k == 0, half == 1 and k == DT - 1)
                        last.then_inc(blocks_done, 1)

            @block.vector
            def _(v):
                for m in range(DT):
                    v.wait_ge(blocks_done, START["attnout"] + 2 * m + 2)
                    stt(X[:, m, 0:TX], PS[:, (m % 2) * 512:(m % 2) * 512 + 512], MODL[:, 2, 16 + m, 0:1], X[:, m, 0:TX],
                        ALU.mult, ALU.add).then_inc(added, 1)

        conv_layer(3, 1, TX, None)

        take = carve()
        sq = take(2, TT)
        RST = take(TT)
        OUT = take(DT, TX)
        norm_stats([X[:, k, 0:TX] for k in range(DT)], TX, "ones", 1.0 / D, EPS, RST[:, 0:TX],
                   [sq[:, 0, 0:TX], sq[:, 1, 0:TX]], PS)
        out_ready, out_stored = sem("out_ready"), sem("out_stored")
        with nc.Block() as block:
            @block.vector
            def _(v):
                for k in range(DT):
                    stt(OUT[:, k, :], X[:, k, 0:TX], V("final_g_2", k), RST[:, 0:TX]).then_inc(out_ready, 1)

            @block.sync
            def _(sp):
                for k in range(DT):
                    sp.wait_ge(out_ready, k + 1)
                    sp.dma_start(outT[k * P:k * P + P, :], OUT[:, k, :]).then_inc(out_stored, 16)
                sp.wait_ge(out_stored, 16 * DT)


def pack(inputs):
    a = {k: np.asarray(v) for k, v in inputs.items()}
    zeros = np.zeros((64, 64), np.float32)

    def pairs(w):
        return [np.block([[w[2 * m], zeros], [zeros, w[2 * m + 1]]]) for m in range(4)]

    def block(name, layer, m):
        if name == "rg":
            return np.concatenate(pairs(a["rg_wa"][0]) + pairs(a["rg_wx"][0]), 1)
        if name in ("lora_w1", "lora_a1"):
            w = a[f"rwkv_{name[5:]}_2"][0]
            w = np.concatenate([w[0], w[1]], 1)
            return w.reshape(DT, P, P).transpose(1, 0, 2).reshape(P, D)
        if name in ("lora_w2", "lora_a2"):
            return a[f"rwkv_{name[5:]}_2"][0].reshape(P, D)
        if name == "w_ple_proj":
            w = a[name][0].reshape(2, P, 2, 4, P)[:, :, m]
            return w.transpose(1, 2, 0, 3).reshape(P, D)
        if name == "attn_w_out_2":
            w = a[name][0][layer * D:(layer + 1) * D]
        else:
            w = a[name][layer]
        return w[:, m * P:(m + 1) * P].reshape(DT, P, P).transpose(1, 0, 2).reshape(P, D)

    weights = np.stack([block(*b) for b in PLAN])
    vectors = np.concatenate([a[n].reshape(-1, P).T for n in VT], 1)
    out = {"xT": a["x"][0].T, "pT": a["p"][0, 0].T, "ctxT": a["ctx_2"][0].T, "vectors": vectors,
           "consts": constants(), "rope": rope_tables(), "weights": weights}
    return {k: np.ascontiguousarray(v) for k, v in out.items()}


def kernel(**inputs):
    import concourse.bacc as bacc
    from concourse.bass_utils import run_bass_kernel_spmd

    nc = bacc.Bacc("TRN2", target_bir_lowering=False, num_devices=1)
    arrays = pack(inputs)
    args = [nc.dram_tensor(f"in_{n}", a.shape, mybir.dt.from_np(a.dtype), kind="ExternalInput").ap() for n, a in arrays.items()]
    out = nc.dram_tensor("out_T", (D, TX), F32, kind="ExternalOutput").ap()
    two_blocks(nc, *args, out)
    r = run_bass_kernel_spmd(nc, [{f"in_{n}": a for n, a in arrays.items()}], core_ids=[0])
    return np.ascontiguousarray(np.asarray(r.results[0]["out_T"]).T)[None]
```

```python
from contextlib import ExitStack

import numpy as np
import concourse.bass as bass
from concourse import mybir

P = 128
D = 1024
DT = D // P
TX, TC = 512, 256
TT = TX + TC
CH = 64
NCX, NCC = TX // CH, TC // CH
NSTEP = NCX + NCC
NPAIR = 8
NU = 2 * NSTEP
SLOTS = 4
EPS = 1e-6
LN_EPS = 1e-5
GN_EPS = 64e-5
TAPS = 31
LN_EXP = "natural_log_exp_and_others"
PAD = TAPS // 2
XW, CW = TX + 2 * PAD, TC + 2 * PAD
YW = XW + CW

F32 = mybir.dt.float32
F32R = mybir.dt.float32r
ALU = mybir.AluOpType
ACT = mybir.ActivationFunctionType
AX = mybir.AxisListType


def vector_table():
    sizes = [("norm_mix_w", 8), ("conv_w", 16), ("conv_b", 4), ("rg_ba", 4), ("rg_bx", 4),
             ("rg_lambda", 4), ("hg_lb", 8), ("hg_norm_w", 1), ("ple_norm_w", 8),
             ("b_ple_gate", 8), ("final_norm_w", 8), ("c_2", 8), ("c_ctx_2", 8),
             ("norm_g_2", 32), ("mod_b_2", 96), ("conv_dw_2", 496), ("conv_db_2", 16),
             ("conv_ln_g_2", 16), ("conv_ln_b_2", 16), ("rwkv_mu_2", 48), ("rwkv_w0_2", 16),
             ("rwkv_a0_2", 16), ("rwkv_k_k_2", 8), ("rwkv_k_a_2", 8), ("rwkv_r_k_2", 8),
             ("rwkv_ln_g_2", 8), ("rwkv_ln_b_2", 8), ("attn_q_g_2", 1), ("attn_k_g_2", 1),
             ("final_g_2", 8)]
    table, at = {}, 0
    for name, n in sizes:
        table[name] = (at, n)
        at += n
    return table, at


VT, NVEC = vector_table()

CT, NCONST = {}, 0
for _n, _w in (("ident", 128), ("ones", 128), ("ones64", 128), ("rot", 128),
               ("gla_mask", 128), ("inv_mask", 6 * 128), ("wkv_mask", 2 * 256)):
    CT[_n] = (NCONST, _w)
    NCONST += _w


def constants():
    out = np.zeros((P, NCONST), np.float32)
    i, j = np.arange(P)[:, None], np.arange(P)[None, :]

    def put(name, a):
        out[:, CT[name][0]:CT[name][0] + CT[name][1]] = a

    put("ident", i == j)
    put("ones", np.ones((P, P)))
    put("ones64", i // 64 == j // 64)
    put("rot", np.where((j % 64 < 32) & (i == j + 32), -1.0, 0) + np.where((j % 64 >= 32) & (i == j - 32), 1.0, 0))
    put("gla_mask", (i // CH == j // CH) & (i <= j))
    m = [((i // (2 * b) == j // (2 * b)) & (i // b != j // b)) for b in (1, 2, 4, 8, 16, 32)]
    put("inv_mask", np.concatenate(m, 1))
    s, t = i % 64, j % 64
    w = []
    for strict, incl in ((s < t, s <= t), (s > t, s >= t)):
        w += [np.where(j < 64, strict, incl), np.where(j < 64, incl, strict)]
    put("wkv_mask", np.concatenate(w, 1))
    return out


def rope_tables():
    row = np.repeat(np.arange(TX // 64), 64).astype(np.float32)
    col = (np.arange(TX) % 64).astype(np.float32)
    inv = (1.0 / (np.float32(10000.0) ** (np.arange(0, 64, 2, dtype=np.float32) / np.float32(64)))).astype(np.float32)
    ang = np.concatenate([inv[:, None] * row[None]] * 2 + [inv[:, None] * col[None]] * 2, 0).astype(np.float32)
    return np.concatenate([np.cos(ang), np.sin(ang)], 1).astype(np.float32)


def weight_plan():
    plan, start = [], {}

    def stage(name, body, mod=None):
        start[name] = len(plan)
        for n, b in enumerate(body):
            plan.append(b)
            if mod is not None and n < 24:
                plan.append(("mod_w_2", mod, n))

    stage("in1", [("w_in", 0, m) for m in range(24)], 0)
    stage("rg", [("rg", 0, 0)])
    stage("out1", [("w_out", 0, m) for m in range(8)])
    stage("gate1", [("w_ple_gate", 0, m) for m in range(8)] + [("w_ple_proj", 0, 0), ("w_ple_proj", 0, 1)])
    tri = [("conv_w_in_2", 0, 8 * part + m) for m in range(8) for part in (0, 1, 2)]
    stage("conv0", tri, 1)
    stage("convout0", [("conv_w_out_2", 0, m) for m in range(8)])
    stage("lora", [("lora_w1", 0, 0), ("lora_a1", 0, 0), ("lora_w2", 0, 0), ("lora_a2", 0, 0)])
    stage("rkvg", [(f"rwkv_w_{n}_2", 0, m) for n in "rkvg" for m in range(8)], 2)
    stage("rwkvout", [("rwkv_w_o_2", 0, m) for m in range(8)])
    stage("attn_qk", [("attn_w_in_2", 0, m) for m in range(24)], 3)
    stage("attn_v", [("attn_w_in_2", 0, 24 + m) for m in range(8)])
    stage("attn_g", [("attn_w_in_2", 0, 32 + m) for m in range(16)])
    stage("attnout", [("attn_w_out_2", k, m) for m in range(8) for k in (0, 1)])
    stage("conv1", [("conv_w_in_2", 1, 8 * part + m) for m in range(8) for part in (0, 1, 2)])
    stage("convout1", [("conv_w_out_2", 1, m) for m in range(8)])
    return plan, start


PLAN, START = weight_plan()
NB = len(PLAN)
DIRECT = ("mod_w_2", "rg", "lora_w2", "lora_a2", "w_ple_proj")
IS_SPLIT = [b[0] not in DIRECT for b in PLAN]
ORDER = [sum(IS_SPLIT[:b]) if IS_SPLIT[b] else b - sum(IS_SPLIT[:b]) for b in range(NB)]
SPLIT_BLOCK = [b for b in range(NB) if IS_SPLIT[b]]
PSTART = {n: sum(IS_SPLIT[:b]) for n, b in START.items()}


class Ring:

    def __init__(self, ready, parted, direct_done):
        self.ready, self.parted, self.direct_done = ready, parted, direct_done
        self.issued = 0
        self.direct_taken = 0

    def freed(self, b):
        return (self.parted if IS_SPLIT[b] else self.direct_done), ORDER[b] + 1

    def supply(self, sp, ring, weights, upto):
        upto = min(upto, NB)
        while self.issued < upto:
            b = self.issued
            if b < SLOTS:
                sp.dma_start(ring[:, b, :], weights[b, :, :]).then_inc(self.ready[b], 16)
                self.issued += 1
                continue
            n, sl = 0, range(SLOTS)
            while b % SLOTS == 0 and b + (n + 1) * SLOTS <= upto and all(
                    IS_SPLIT[b + (n - 1) * SLOTS + s] == IS_SPLIT[b - SLOTS + s]
                    and ORDER[b + (n - 1) * SLOTS + s] - ORDER[b - SLOTS + s] == n * (ORDER[b + s] - ORDER[b - SLOTS + s]) for s in sl):
                n += 1
            if n > 1:
                with sp.Fori(0, n) as i:
                    for s in sl:
                        sem, value = self.freed(b - SLOTS + s)
                        sp.wait_ge(sem, i * (ORDER[b + s] - ORDER[b - SLOTS + s]) + value)
                        sp.dma_start(ring[:, s, :], weights[bass.ds(i * SLOTS + (b + s), 1), :, :]
                                     .rearrange("a p n -> (a p) n")).then_inc(self.ready[s], 16)
                self.issued += n * SLOTS
                continue
            sem, value = self.freed(b - SLOTS)
            sp.wait_ge(sem, value)
            sp.dma_start(ring[:, b % SLOTS, :], weights[b, :, :]).then_inc(self.ready[b % SLOTS], 16)
            self.issued += 1

    def landed(self, eng, b):
        eng.wait_ge(self.ready[b % SLOTS], 16 * (b // SLOTS + 1))
        return b % SLOTS

    def take_direct(self, pe):
        b = [b for b in range(NB) if not IS_SPLIT[b]][self.direct_taken]
        self.direct_taken += 1
        return self.landed(pe, b)


class Chain:

    def __init__(self, sem):
        self.sem, self.n, self.base = sem, 0, 0

    def inc(self, ins):
        self.n += 1
        ins.then_inc(self.sem, 1)

    def wait(self, eng):
        eng.wait_ge(self.sem, self.base + self.n)

    def link(self, eng, ins):
        self.inc(ins)
        self.wait(eng)


def two_blocks(nc, xT, pT, ctxT, vectors, consts, rope, weights, outT):
    ctx = ExitStack()
    names = [0]

    def sem(name):
        names[0] += 1
        return ctx.enter_context(nc.semaphore(f"{name}_{names[0]}"))

    def sb(name, shape):
        return ctx.enter_context(nc.sbuf_tensor(name, shape, F32))

    def ap(t):
        return t[tuple(slice(None) for _ in t.shape)]

    with ctx:
        X = ap(sb("stream", [P, DT, TT]))
        RINGT = ap(sb("ring", [P, SLOTS, DT * P]))
        VEC = ap(sb("vec", [P, NVEC]))
        CON = ap(sb("con", [P, NCONST]))
        MODL = ap(sb("mod", [P, 4, 24, 2]))
        SC = ap(sb("sc", [P, DT, 2]))
        GA = ap(sb("ga", [P, DT, 2]))
        TINY = ap(sb("tiny", [P, 128]))
        ROOM = 212000 // 4 - DT * TT - SLOTS * DT * P - NVEC - NCONST - 192 - 32 - 128
        SPLIT = 2 * DT * TT + 4 * DT * P
        PARTS = {}
        PS = ap(ctx.enter_context(nc.psum_tensor("ps", [P, 4096], F32)))
        PMOD = PS[:, 7 * 512:7 * 512 + 48].rearrange("p (m v) -> p m v", v=2)

        rwkv_dram = nc.dram_tensor("rwkv_spill", [DT + 1, 8, P, TT], F32, kind="Internal").ap()
        y_dram = nc.dram_tensor("y_spill", [DT, P, TT], F32, kind="Internal").ap()
        x_dram = nc.dram_tensor("x_spill", [P, DT * TT], F32, kind="Internal").ap()

        ring_ready = [sem(f"ring_ready{s}") for s in range(SLOTS)]
        blocks_done = sem("blocks_done")
        rounded, parted, direct_done = sem("rounded"), sem("parted"), sem("direct_done")
        loads = sem("loads")
        stores = sem("stores")
        R = Ring(ring_ready, parted, direct_done)
        dve_chain = Chain(sem("dve_chain"))
        act_chain = Chain(sem("act_chain"))
        pool_chain = Chain(sem("pool_chain"))

        def V(name, k=0, n=1):
            return VEC[:, VT[name][0] + k:VT[name][0] + k + n]

        def C(name, k=0, n=None):
            a = CT[name][0] + k
            return CON[:, a:a + (CT[name][1] if n is None else n)]

        kept_scope, area_scope, parts_scope = (ctx.enter_context(ExitStack()) for _ in range(3))
        AREA = {}

        def memory(name, split, room=ROOM):
            parts_scope.close()
            area_scope.close()
            size = room - SPLIT if split else room
            area("area", name, size)
            if split:
                parts(name, DT, TT)

        def kept(name, size):
            parts_scope.close()
            area_scope.close()
            kept_scope.close()
            return ap(kept_scope.enter_context(nc.sbuf_tensor(f"kept_{name}", [P, size], F32))) if size else None

        def area(scope, name, size):
            scope = area_scope if scope == "area" else parts_scope
            AREA["a"] = ap(scope.enter_context(nc.sbuf_tensor(f"scratch_{name}", [P, size], F32)))
            AREA["room"] = size

        def parts(name, tiles, width):
            PARTS["H"] = ap(parts_scope.enter_context(nc.sbuf_tensor(f"h_parts_{name}", [P, 2, tiles, width], F32R)))
            PARTS["W"] = ap(parts_scope.enter_context(nc.sbuf_tensor(f"w_parts_{name}", [P, 2, 2, DT * P], F32R)))

        def carve():
            at = [0]
            area, room = AREA["a"], AREA["room"]

            def take(*shape):
                n = int(np.prod(shape))
                a = area[:, at[0]:at[0] + n]
                at[0] += n
                assert at[0] <= room, (at[0], room)
                if len(shape) == 1:
                    return a
                names_ = "abcd"[:len(shape)]
                kw = {c: s for c, s in zip(names_, shape)}
                return a.rearrange(f"p ({' '.join(names_)}) -> p {' '.join(names_)}", **kw)
            return take

        def dlink(ins):
            dve_chain.link(nc.vector, ins)

        def alink(ins):
            act_chain.link(nc.scalar, ins)

        def plink(ins):
            pool_chain.link(nc.gpsimd, ins)

        def vtt(o, a, b, op=ALU.mult):
            return nc.vector.tensor_tensor(o, a, b, op)

        def vts(o, a, s1, s2=None, op0=ALU.mult, op1=None):
            if s2 is None:
                return nc.vector.tensor_scalar(o, a, s1, None, op0)
            return nc.vector.tensor_scalar(o, a, s1, s2, op0, op1)

        def stt(o, a, s, b, op0=ALU.mult, op1=ALU.mult):
            return nc.vector.scalar_tensor_tensor(out=o, in0=a, scalar=s, in1=b, op0=op0, op1=op1)

        def act(o, a, f, **kw):
            return nc.scalar.activation(o, a, f, **kw)

        def mm(o, l, r, start=True, stop=True):
            return nc.tensor.matmul(o, l, r, start=start, stop=stop)


        def mod_block(pe, n):
            s = R.take_direct(pe)
            w = RINGT[:, s, :].rearrange("p (k m) -> p k m", k=DT)
            for k in range(DT):
                last = mm(PMOD[:, n, :], w[:, k, :], SC[:, k, :], k == 0, k == DT - 1)
            last.then_inc(direct_done, 1)

        def mod_finish(layer):
            b = V("mod_b_2", 24 * layer, 24).rearrange("p (m o) -> p m o", o=1).broadcast_to([P, 24, 2])
            dlink(vtt(MODL[:, layer], PMOD, b, ALU.add))

        def mod_gain(layer):
            g = V("norm_g_2", 8 * layer, 8).rearrange("p (m o) -> p m o", o=1).broadcast_to([P, 8, 2])
            dlink(stt(GA, MODL[:, layer, 8:16], 1.0, g, ALU.add, ALU.mult))

        def product(o, l, rhs, width, start, stop):
            last = None
            for a in range(0, width, 512):
                b = min(a + 512, width)
                last = mm(o[:, a:b], l, rhs[:, a:b], start, stop)
            return last

        done = {"round": 0, "part": 0, "take": 0}

        def round_block(a, upto):
            while done["round"] < upto:
                j = done["round"]
                s = R.landed(a, SPLIT_BLOCK[j])
                if j >= 2:
                    a.wait_ge(blocks_done, j - 1)
                act(PARTS["W"][:, j % 2, 0, :], RINGT[:, s, :], ACT.Copy).then_inc(rounded, 1)
                done["round"] += 1

        def part_block(g, upto):
            while done["part"] < upto:
                j = done["part"]
                s = SPLIT_BLOCK[j] % SLOTS
                g.wait_ge(rounded, j + 1)
                nc.gpsimd.tensor_tensor(PARTS["W"][:, j % 2, 1, :], RINGT[:, s, :], PARTS["W"][:, j % 2, 0, :].bitcast(F32),
                                        ALU.subtract).then_inc(parted, 1)
                done["part"] += 1

        def tile_product(pe, o, width, area=None, start=True, stop=True, fresh=None, used=None):
            j = done["take"]
            done["take"] += 1
            pe.wait_ge(parted, j + 1)
            W = PARTS["W"][:, j % 2].rearrange("p e (k m) -> p e k m", k=DT)
            Hh, Hl = (PARTS["H"][:, e] for e in range(2)) if area is None else area
            for k in range(DT):
                if fresh is not None:
                    pe.wait_ge(fresh[0], fresh[1] + k + 1)
                product(o, W[:, 0, k, :], Hh[:, k, :], width, start and k == 0, False)
                product(o, W[:, 0, k, :], Hl[:, k, :], width, False, False)
                last = product(o, W[:, 1, k, :], Hh[:, k, :], width, False, stop and k == DT - 1)
                if used is not None and k < DT - 1:
                    last.then_inc(used, 1)
            last.then_inc(blocks_done, 1)

        def split_tiles(src, width, limit, area=None):
            base = next_use("split", len(src))
            Hh, Hl = (PARTS["H"][:, e] for e in range(2)) if area is None else area
            with nc.Block() as block:
                @block.scalar
                def _(a):
                    for k, x_ in enumerate(src):
                        act(Hh[:, k, 0:width], x_[:, 0:width], ACT.Copy).then_inc(split_hi, 1)
                    round_block(a, limit)

                @block.vector
                def _(v):
                    for k, x_ in enumerate(src):
                        v.wait_ge(split_hi, base + k + 1)
                        vtt(Hl[:, k, 0:width], x_[:, 0:width], Hh[:, k, 0:width].bitcast(F32), ALU.subtract)

                @block.gpsimd
                def _(g):
                    part_block(g, limit)

        def next_use(name, n):
            uses[name] = uses.get(name, 0) + n
            return uses[name] - n

        uses = {}
        sq_ready, sq_used, in_scaled, in_hi, split_hi, split_low, freed_add = (
            sem(n) for n in ("sq_ready", "sq_used", "in_scaled", "in_hi", "split_hi", "split_low", "freed_add"))
        EPSC = {}
        for n, e in enumerate((EPS, LN_EPS, GN_EPS, 1e-12)):
            EPSC[e] = TINY[:, n:n + 1]

        def norm_stats(src, width, ones_name, scale, eps, rstd, sq, psum):
            n = len(src)
            base = next_use("norm", n)
            with nc.Block() as block:
                @block.scalar
                def _(a):
                    a.preload_act_table_set(LN_EXP)
                    for k in range(n):
                        if k >= 2:
                            a.wait_ge(sq_used, base + k - 1)
                        act(sq[k % 2], src[k], ACT.Square).then_inc(sq_ready, 1)
                    a.wait_ge(sq_used, base + n)
                    alink(act(rstd, psum[:, 0:width], ACT.Ln, scale=scale, bias=EPSC[eps]))
                    alink(act(rstd, rstd, ACT.Exp, scale=-0.5))

                @block.tensor
                def _(pe):
                    for k in range(n):
                        pe.wait_ge(sq_ready, base + k + 1)
                        product(psum, C(ones_name), sq[k % 2], width, k == 0, k == n - 1).then_inc(sq_used, 1)

        def layer_input(layer, T_, width, sq, rst, limit, keep=None):
            norm_stats([X[:, k, 0:width] for k in range(DT)], width, "ones", 1.0 / D, EPS, rst[:, 0:width],
                       [sq[:, 0, 0:width], sq[:, 1, 0:width]], PS)
            halves = [(0, TX, 0), (TX, TT, 1)][:1 if width == TX else 2]
            Hh, Hl = PARTS["H"][:, 0], PARTS["H"][:, 1]
            tiles = [(k, a, b, c) for k in range(DT) for a, b, c in halves]
            base, base_hi = next_use("scaled", len(tiles)), next_use("hi", len(tiles) if keep is None else 0)
            with nc.Block() as block:
                @block.vector
                def _(v):
                    mod_gain(layer)
                    for n in range(len(tiles) + 2):
                        if n < len(tiles):
                            k, a, b, c = tiles[n]
                            o = T_[:, k, a:b] if keep is None else keep[c][:, k, :]
                            stt(o, X[:, k, a:b], GA[:, k, c:c + 1], rst[:, a:b]).then_inc(in_scaled, 1)
                        if n >= 2 and keep is None:
                            k, a, b, c = tiles[n - 2]
                            v.wait_ge(in_hi, base_hi + n - 1)
                            stt(Hl[:, k, a:b], T_[:, k, a:b], MODL[:, layer, k, c:c + 1], Hh[:, k, a:b].bitcast(F32), ALU.add, ALU.subtract)

                @block.scalar
                def _(a_):
                    for n, (k, a, b, c) in enumerate(tiles):
                        a_.wait_ge(in_scaled, base + n + 1)
                        if keep is None:
                            act(Hh[:, k, a:b], T_[:, k, a:b], ACT.Identity, bias=MODL[:, layer, k, c:c + 1]).then_inc(in_hi, 1)
                        else:
                            act(keep[c][:, k, :], keep[c][:, k, :], ACT.Identity, bias=MODL[:, layer, k, c:c + 1])
                    round_block(a_, limit)

                @block.gpsimd
                def _(g):
                    part_block(g, limit)

        memory("block1", True)
        SP8N, SP8, LB, OMLB = TINY[:, 8:12], TINY[:, 12:16], TINY[:, 16:20], TINY[:, 20:24]
        with nc.Block() as block:
            @block.sync
            def _(sp):
                sp.dma_start(VEC, vectors).then_inc(loads, 16)
                sp.dma_start(X[:, :, 0:TX], xT.rearrange("(k p) t -> p k t", p=P)).then_inc(loads, 16)
                sp.dma_start(CON, consts).then_inc(loads, 16)
                sp.dma_start(X[:, :, TX:TT], ctxT.rearrange("(k p) t -> p k t", p=P)).then_inc(loads, 16)
                R.supply(sp, RINGT, weights, SLOTS)

            @block.scalar
            def _(a):
                a.wait_ge(loads, 64)
                act(SC[:, :, 0], V("c_2", 0, 8), ACT.Silu)
                alink(act(SC[:, :, 1], V("c_ctx_2", 0, 8), ACT.Silu))

            @block.gpsimd
            def _(g):
                for n, e in enumerate((EPS, LN_EPS, GN_EPS, 1e-12)):
                    nc.gpsimd.memset(TINY[:, n:n + 1], e)
                plink(nc.gpsimd.memset(TINY[:, 4:5], 1.0))

        with nc.Block() as block:
            t0, t1, t2, t3 = (TINY[:, 32 + 4 * n:36 + 4 * n] for n in range(4))
            e_ready, e_asked = sem("e_ready"), sem("e_asked")

            @block.vector
            def _(v):
                lam = V("rg_lambda", 0, 4)
                h0, h1 = V("hg_lb", 0, 4), V("hg_lb", 4, 4)
                dlink(vts(t0, lam, -1.0))
                dlink(vtt(t1, t0, lam, ALU.max))
                dlink(vtt(t2, h0, h1, ALU.max))
                dlink(vtt(TINY[:, 48:52], h0, t2, ALU.subtract))
                vtt(TINY[:, 52:56], h1, t2, ALU.subtract).then_inc(e_asked, 1)
                v.wait_ge(e_ready, 2)
                E_ = TINY[:, 56:60]
                dlink(vts(t2, E_, 2.0, None, ALU.add))
                dlink(nc.vector.reciprocal(t2, t2))
                dlink(vtt(t2, t2, E_))
                dlink(vtt(t3, t2, t2))
                dlink(vts(t1, t3, 1.0 / 19, 1.0 / 17, ALU.mult, ALU.add))
                for q in (15, 13, 11, 9, 7, 5, 3, 1):
                    dlink(vtt(t1, t1, t3))
                    dlink(vts(t1, t1, 1.0 / q, None, ALU.add))
                dlink(stt(t1, t1, 2.0, t2, ALU.mult, ALU.mult))
                dlink(vts(t0, t0, 0.0, None, ALU.max))
                dlink(vtt(t1, t1, t0, ALU.add))
                dlink(vts(SP8N, t1, -8.0))
                dlink(vts(SP8, t1, 8.0))
                a0, a1 = TINY[:, 60:64], TINY[:, 64:68]
                dlink(vtt(t2, a0, a1, ALU.add))
                dlink(nc.vector.reciprocal(t2, t2))
                dlink(vtt(LB, a0, t2))
                dlink(vtt(OMLB, a1, t2))

            @block.scalar
            def _(a):
                a.wait_ge(e_asked, 1)
                act(TINY[:, 56:60], t1, ACT.Exp, scale=-1.0).then_inc(e_ready, 1)
                act(TINY[:, 60:68], TINY[:, 48:56], ACT.Exp).then_inc(e_ready, 1)

        take = carve()
        RAW = take(20, TX)
        VTOK = take(4, 512)
        XAP = take(4, TX + 4)
        XC, RG, IG, AG = (take(4, TX) for _ in range(4))
        TH = XAP[:, :, 0:TX]
        CMASK, BL_ = take(TX), take(32)
        sq, RST = RG.rearrange("p a b -> p (a b)")[:, 0:2 * TX].rearrange("p (a b) -> p a b", a=2), XC[:, 0, :]
        NORM1 = RAW[:, 4:12, :]

        norm_stats([X[:, k, 0:TX] for k in range(DT)], TX, "ones", 1.0 / D, EPS, RST, [sq[:, 0], sq[:, 1]], PS)
        with nc.Block() as block:
            @block.vector
            def _(v):
                for k in range(DT):
                    stt(NORM1[:, k, :], X[:, k, 0:TX], V("norm_mix_w", k), RST)
                dlink(nc.vector.memset(XAP[:, :, 0:3], 0.0))
        split_tiles([NORM1[:, k, :] for k in range(DT)], TX, 2)

        bank_free, v_turned, v_read = sem("bank_free"), sem("v_turned"), sem("v_read")
        with nc.Block() as block:
            @block.sync
            def _(sp):
                R.supply(sp, RINGT, weights, START["rg"] + SLOTS)

            @block.tensor
            def _(pe):
                for m in range(24):
                    if m >= 2:
                        pe.wait_ge(bank_free, m - 1)
                    bank = PS[:, (m % 2) * 512:(m % 2) * 512 + 512]
                    tile_product(pe, bank, TX)
                    mod_block(pe, m)
                    if 17 <= m < 21:
                        pe.wait_ge(bank_free, m)
                        if m >= 19:
                            pe.wait_ge(v_read, m - 18)
                        o = 1024 + (m % 2) * 512
                        for t in range(4):
                            last = nc.tensor.transpose(PS[:, o + t * P:o + t * P + P], RAW[:, m - 17, t * P:t * P + P], C("ident"))
                        last.then_inc(v_turned, 1)

            @block.vector
            def _(v):
                for h in range(4):
                    v.wait_ge(v_turned, h + 1)
                    o = 1024 + ((h + 17) % 2) * 512
                    nc.vector.tensor_copy(VTOK.rearrange("p t (h v) -> p t h v", h=4)[:, :, h, :],
                                          PS[:, o:o + 512].rearrange("p (t v) -> p t v", t=4)).then_inc(v_read, 1)

            @block.gpsimd
            def _(g):
                part_block(g, 26)

            @block.scalar
            def _(a):
                for m in range(24):
                    round_block(a, m + 3)
                    a.wait_ge(blocks_done, PSTART["in1"] + m + 1)
                    bank = PS[:, (m % 2) * 512:(m % 2) * 512 + 512]
                    o, i_ = RAW[:, m if m < 16 else m - 4, :], bank
                    if m < 4:
                        o = XAP[:, m, 3:3 + TX]
                    if 16 <= m < 20:
                        o = RAW[:, m - 16, :]
                    act(o, i_, ACT.Copy).then_inc(bank_free, 1)

        xc_ready = sem("xc_ready")
        gates_done, rg_done = sem("gates_done"), sem("rg_done")
        with nc.Block() as block:
            @block.sync
            def _(sp):
                R.supply(sp, RINGT, weights, START["out1"] + SLOTS)

            @block.vector
            def _(v):
                mod_finish(0)
                for m in range(4):
                    dlink(vts(XC[:, m, :], XAP[:, m, 3:3 + TX], V("conv_w", 12 + m), V("conv_b", m), ALU.mult, ALU.add))
                    for j in range(3):
                        ins = stt(XC[:, m, :], XAP[:, m, j:j + TX], V("conv_w", 4 * j + m), XC[:, m, :], ALU.mult, ALU.add)
                        if j < 2:
                            dlink(ins)
                        else:
                            ins.then_inc(xc_ready, 1)

            @block.tensor
            def _(pe):
                s = R.take_direct(pe)
                for m in range(4):
                    pe.wait_ge(xc_ready, m + 1)
                    for g in range(2):
                        bank = 2 * (m % 2) + g
                        if m >= 2:
                            pe.wait_ge(gates_done, 2 * (m - 2) + g + 1)
                        last = mm(PS[:, bank * 512:bank * 512 + 512], RINGT[:, s, (4 * g + m) * P:(4 * g + m + 1) * P], XC[:, m, :])
                        last.then_inc(rg_done, 1)
                pe.wait_ge(rg_done, 8)
                pe.nop().then_inc(direct_done, 1)

            @block.scalar
            def _(a):
                act(RAW[:, 4:8, :], RAW[:, 4:8, :], ACT.Silu)
                act(RAW[:, 8:12, :], RAW[:, 8:12, :], ACT.Silu)
                act(RAW[:, 16:20, :], RAW[:, 16:20, :], ACT.Silu)
                for m in range(4):
                    for g in range(2):
                        a.wait_ge(rg_done, 2 * m + g + 1)
                        bank = 2 * (m % 2) + g
                        act((RG, IG)[g][:, m, :], PS[:, bank * 512:bank * 512 + 512], ACT.Sigmoid,
                            bias=V(("rg_ba", "rg_bx")[g], m)).then_inc(gates_done, 1)

        tanh_ready, root_asked, root_ready = sem("tanh_ready"), sem("root_asked"), sem("root_ready")
        with nc.Block() as block:
            @block.scalar
            def _(a):
                for m in range(4):
                    act(AG[:, m, :], RG[:, m, :], ACT.Exp, scale=SP8N[:, m:m + 1])
                    act(TH[:, m, :], RG[:, m, :], ACT.Tanh, scale=SP8[:, m:m + 1]).then_inc(tanh_ready, 1)
                for m in range(4):
                    a.wait_ge(root_asked, m + 1)
                    act(TH[:, m, :], TH[:, m, :], ACT.Sqrt).then_inc(root_ready, 1)

            @block.vector
            def _(v):
                for m in range(4):
                    v.wait_ge(tanh_ready, m + 1)
                    dlink(vtt(RG[:, m, :], AG[:, m, :], AG[:, m, :]))
                    stt(TH[:, m, :], RG[:, m, :], 1.0, TH[:, m, :], ALU.add, ALU.mult).then_inc(root_asked, 1)
                    dlink(vtt(IG[:, m, :], IG[:, m, :], XC[:, m, :]))
                for m in range(4):
                    v.wait_ge(root_ready, m + 1)
                    dlink(nc.vector.memset(TH[:, m, 0:1], 1.0))
                    dlink(vtt(IG[:, m, :], IG[:, m, :], TH[:, m, :]))
                    dlink(nc.vector.tensor_tensor_scan(XC[:, m, :], AG[:, m, :], IG[:, m, :], 0.0, ALU.mult, ALU.add))
                    dlink(vtt(XC[:, m, :], XC[:, m, :], RAW[:, 4 + m, :]))
        split_tiles([XC[:, k, :] for k in range(4)], TX, 2 + PSTART["out1"])

        SF, BC, EB, ENB, SM = XC, RG, IG, AG, TH
        Q, K = RAW[:, 8:12, :], RAW[:, 12:16, :]
        KT = SF
        ST = RAW[:, 0:8, :].rearrange("p a b -> p (a b)").rearrange("p (h n v) -> p h n v", h=4, n=NCX)
        with nc.Block() as block:
            @block.scalar
            def _(a):
                act(EB, RAW[:, 12:16, :], ACT.Sigmoid)
                alink(act(K, K, ACT.Sigmoid, scale=-1.0))
                for m in range(4):
                    act(SF[:, m, :], EB[:, m, :], ACT.Ln, scale=OMLB[:, m:m + 1], bias=LB[:, m:m + 1])

            @block.vector
            def _(v):
                dlink(nc.vector.memset(CMASK, 1.0))
                dlink(nc.vector.memset(CMASK.rearrange("p (n t) -> p n t", t=CH)[:, :, 0:1], 0.0))
        with nc.Block() as block:
            @block.vector
            def _(v):
                for m in range(4):
                    dlink(nc.vector.tensor_tensor_scan(BC[:, m, :], CMASK, SF[:, m, :], 0.0, ALU.mult, ALU.add))
                for m in range(4):
                    dlink(vts(K[:, m, :], K[:, m, :], OMLB[:, m:m + 1]))
        BL = BL_.rearrange('p (n o) -> p n o', o=1)
        b4 = BC.rearrange("p h (n t) -> p (h n) t", t=CH)
        eb_ready, db_ready, ed_ready = sem("eb_ready"), sem("db_ready"), sem("ed_ready")
        with nc.Block() as block:
            @block.scalar
            def _(a):
                a.preload_act_table_set(LN_EXP)
                act(EB, BC, ACT.Exp).then_inc(eb_ready, 1)
                act(ENB, BC, ACT.Exp, scale=-1.0).then_inc(eb_ready, 1)
                a.wait_ge(db_ready, 1)
                act(BC, BC, ACT.Exp).then_inc(ed_ready, 1)

            @block.vector
            def _(v):
                v.wait_ge(eb_ready, 2)
                dlink(nc.vector.tensor_copy(BL, b4[:, :, CH - 1:CH]))
                vtt(b4, BL.broadcast_to([P, 32, CH]), b4, ALU.subtract).then_inc(db_ready, 1)
                dlink(stt(Q, Q, float(P) ** -0.5, EB, ALU.mult, ALU.mult))
                dlink(vtt(ENB, ENB, K))
                v.wait_ge(ed_ready, 1)
                dlink(vtt(BC, BC, K))
        QE, KE, KD = Q, ENB, BC
        sc_done, sc_masked, kt_done, kt_read = (sem(n) for n in ("sc_done", "sc_masked", "kt_done", "kt_read"))
        gmask = C("gla_mask").rearrange("p (o t) -> p o t", o=1).broadcast_to([P, 4, P])
        with nc.Block() as block:
            @block.tensor
            def _(pe):
                for h in range(4):
                    for u in range(4):
                        last = mm(PS[:, h * 512 + u * P:h * 512 + u * P + P], KE[:, h, u * P:u * P + P], QE[:, h, u * P:u * P + P])
                    last.then_inc(sc_done, 1)
                    if h >= 2:
                        pe.wait_ge(kt_read, h - 1)
                    for u in range(4):
                        o = 2048 + (h % 2) * 512 + u * P
                        last = nc.tensor.transpose(PS[:, o:o + P], KD[:, h, u * P:u * P + P], C("ident"))
                    last.then_inc(kt_done, 1)

            @block.vector
            def _(v):
                for h in range(4):
                    v.wait_ge(sc_done, h + 1)
                    dlink(vtt(SM[:, h, :].rearrange("p (u t) -> p u t", u=4),
                              PS[:, h * 512:h * 512 + 512].rearrange("p (u t) -> p u t", u=4), gmask))

            @block.scalar
            def _(a):
                for h in range(4):
                    a.wait_ge(kt_done, h + 1)
                    o = 2048 + (h % 2) * 512
                    act(KT[:, h, :], PS[:, o:o + 512], ACT.Copy).then_inc(kt_read, 1)
        ds_done, st_ready, o_done = (sem(n) for n in ("ds_done", "st_ready", "o_done"))
        with nc.Block() as block:
            @block.tensor
            def _(pe):
                for h in range(4):
                    if h >= 1:
                        pe.wait_ge(st_ready, (NCX - 1) * h)
                    for e in range(2):
                        for u in range(4):
                            last = mm(PS[:, 2048 + e * 512 + u * P:2048 + e * 512 + u * P + P],
                                      KT[e * CH:e * CH + CH, h, u * P:u * P + P], VTOK[e * CH:e * CH + CH, u, h * P:h * P + P])
                        last.then_inc(ds_done, 1)
                for h in range(4):
                    pe.wait_ge(st_ready, (NCX - 1) * (h + 1))
                    for u in range(4):
                        o = PS[:, h * 512 + u * P:h * 512 + u * P + P]
                        mm(o, VTOK[:, u, h * P:h * P + P], SM[:, h, u * P:u * P + P], True, False)
                        for e in range(2):
                            n = 2 * u + e
                            last = mm(o[:, e * CH:e * CH + CH], ST[:, h, n, :], QE[:, h, n * CH:n * CH + CH], False, e == 1)
                    last.then_inc(o_done, 1)

            @block.vector
            def _(v):
                for h in range(4):
                    dlink(nc.vector.memset(ST[:, h, 0, :], 0.0))
                    v.wait_ge(ds_done, 2 * h + 2)
                    for n in range(NCX - 1):
                        o = 2048 + (n % 2) * 512 + (n // 2) * P
                        ins = stt(ST[:, h, n + 1, :], ST[:, h, n, :], EB[:, h, n * CH + CH - 1:n * CH + CH], PS[:, o:o + P], ALU.mult, ALU.add)
                        ins.then_inc(st_ready, 1)
                        v.wait_ge(st_ready, h * (NCX - 1) + n + 1)

            @block.scalar
            def _(a):
                for h in range(4):
                    a.wait_ge(o_done, h + 1)
                    act(KE[:, h, :], PS[:, h * 512:h * 512 + 512], ACT.Copy)
        O = KE
        osq, orst = SM, KD
        osq_ready, osum = sem('osq_ready'), sem('osum')
        with nc.Block() as block:
            @block.scalar
            def _(a):
                act(osq, O, ACT.Square).then_inc(osq_ready, 1)
                a.wait_ge(osum, 4)
                alink(act(orst, PS[:, 0:2048].rearrange("p (h t) -> p h t", h=4), ACT.Ln, scale=1.0 / P, bias=EPSC[EPS]))
                act(orst, orst, ACT.Exp, scale=-0.5).then_inc(osq_ready, 1)

            @block.tensor
            def _(pe):
                pe.wait_ge(osq_ready, 1)
                for h in range(4):
                    mm(PS[:, h * 512:h * 512 + 512], C("ones"), osq[:, h, :]).then_inc(osum, 1)

            @block.vector
            def _(v):
                v.wait_ge(osum, 4)
                dlink(stt(O, O, V("hg_norm_w"), RAW[:, 16:20, :], ALU.mult, ALU.mult))
                v.wait_ge(osq_ready, 2)
                dlink(vtt(O, O, orst))
        Hh, Hl = PARTS["H"][:, 0, 4:8], PARTS["H"][:, 1, 4:8]
        split_tiles([O[:, k, :] for k in range(4)], TX, 2 + PSTART["out1"], (Hh, Hl))

        def plain_split(src, width):
            def high(a, base, base_low):
                for k, x_ in enumerate(src):
                    act(PARTS["H"][:, 0, k, 0:width], x_[:, 0:width], ACT.Copy).then_inc(split_hi, 1)

            def low(v, base, base_low):
                for k, x_ in enumerate(src):
                    v.wait_ge(split_hi, base + k + 1)
                    vtt(PARTS["H"][:, 1, k, 0:width], x_[:, 0:width], PARTS["H"][:, 0, k, 0:width].bitcast(F32), ALU.subtract).then_inc(split_low, 1)
            return high, low

        def add_products(stage, width, gate, ahead=2, split=None):
            base_hi = next_use("split", DT) if split else 0
            base_low = next_use("low", DT) if split else 0
            halves = [(0, TX, 0), (TX, TT, 1)][:1 if width == TX else 2]
            base = next_use("add", len(halves) * DT)
            limit = PSTART[stage] + DT + ahead
            with nc.Block() as block:
                @block.sync
                def _(sp):
                    R.supply(sp, RINGT, weights, START[stage] + 8 + SLOTS)

                @block.scalar
                def _(a):
                    if split:
                        round_block(a, PSTART[stage] + 2)
                        split[0](a, base_hi, base_low)
                    round_block(a, limit)

                @block.gpsimd
                def _(g):
                    part_block(g, limit)

                @block.tensor
                def _(pe):
                    for m in range(DT):
                        if m >= 2:
                            pe.wait_ge(freed_add, base + len(halves) * (m - 1))
                        tile_product(pe, PS[:, (m % 2) * 1024:(m % 2) * 1024 + width], width,
                                     fresh=(split_low, base_low) if split and m == 0 else None)

                @block.vector
                def _(v):
                    if split:
                        split[1](v, base_hi, base_low)
                    for m in range(DT):
                        v.wait_ge(blocks_done, PSTART[stage] + m + 1)
                        for a, b, c in halves:
                            p = PS[:, (m % 2) * 1024 + a:(m % 2) * 1024 + b]
                            if gate is None:
                                vtt(X[:, m, a:b], p, X[:, m, a:b], ALU.add).then_inc(freed_add, 1)
                            else:
                                stt(X[:, m, a:b], p, gate(m, c), X[:, m, a:b], ALU.mult, ALU.add).then_inc(freed_add, 1)

        add_products("out1", TX, None)

        take = carve()
        H = take(DT, TX)
        PE_ = take(2, TX)
        GT = take(DT, TX)
        sq = take(2, TT)
        RST = take(TT)
        norm_stats([X[:, k, 0:TX] for k in range(DT)], TX, "ones", 1.0 / D, EPS, RST[:, 0:TX],
                   [sq[:, 0, 0:TX], sq[:, 1, 0:TX]], PS)
        with nc.Block() as block:
            @block.sync
            def _(sp):
                sp.dma_start(PE_, pT.rearrange("(k p) t -> p k t", p=P)).then_inc(loads, 16)
                sp.wait_ge(loads, 80)

            @block.vector
            def _(v):
                for k in range(DT):
                    stt(H[:, k, :], X[:, k, 0:TX], V("ple_norm_w", k), RST[:, 0:TX])
        split_tiles([H[:, k, :] for k in range(DT)], TX, PSTART["gate1"] + 2)
        g_read, p_done, p_added = sem("g_read"), sem("p_done"), sem("p_added")
        gated = Chain(sem("gated"))
        with nc.Block() as block:
            @block.sync
            def _(sp):
                R.supply(sp, RINGT, weights, START["conv0"] + SLOTS)

            @block.tensor
            def _(pe):
                for m in range(DT):
                    if m >= 2:
                        pe.wait_ge(g_read, m - 1)
                    tile_product(pe, PS[:, (m % 2) * 512:(m % 2) * 512 + 512], TX)
                for half in range(2):
                    s = R.take_direct(pe)
                    for j in range(4):
                        m = 4 * half + j
                        if m >= 2:
                            pe.wait_ge(p_added, m - 1)
                        for k in range(2):
                            last = mm(PS[:, 1024 + (m % 2) * 512:1536 + (m % 2) * 512],
                                      RINGT[:, s, (2 * j + k) * P:(2 * j + k + 1) * P], PE_[:, k, :], k == 0, k == 1)
                        last.then_inc(p_done, 1)
                    pe.wait_ge(p_done, 4 * half + 4)
                    pe.nop().then_inc(direct_done, 1)

            @block.gpsimd
            def _(g):
                part_block(g, PSTART["gate1"] + DT + 2)

            @block.scalar
            def _(a):
                for m in range(DT):
                    round_block(a, PSTART["gate1"] + m + 3)
                    a.wait_ge(blocks_done, PSTART["gate1"] + m + 1)
                    act(GT[:, m, :], PS[:, (m % 2) * 512:(m % 2) * 512 + 512], ACT.Sigmoid, bias=V("b_ple_gate", m)).then_inc(g_read, 1)

            @block.vector
            def _(v):
                for m in range(DT):
                    v.wait_ge(g_read, m + 1)
                    v.wait_ge(p_done, m + 1)
                    vtt(GT[:, m, :], PS[:, 1024 + (m % 2) * 512:1536 + (m % 2) * 512], GT[:, m, :]).then_inc(p_added, 1)
                    v.wait_ge(p_added, m + 1)
                    dlink(vtt(X[:, m, 0:TX], X[:, m, 0:TX], GT[:, m, :], ALU.add))
        norm_stats([X[:, k, 0:TX] for k in range(DT)], TX, "ones", 1.0 / D, EPS, RST[:, 0:TX],
                   [sq[:, 0, 0:TX], sq[:, 1, 0:TX]], PS)
        with nc.Block() as block:
            @block.vector
            def _(v):
                for k in range(DT):
                    stt(X[:, k, 0:TX], X[:, k, 0:TX], V("final_norm_w", k), RST[:, 0:TX])

        def conv_layer(layer, j_, width, next_mod):
            take = carve()
            SHARE = TAPS - 9
            YP = take(2, YW)
            G = take(DT, TT)
            Z = take(DT, TT)
            sa, sb_ = take(2, TT), take(2, TT)
            sq = sa
            RST = take(TT)
            Z2 = take(2, TT)
            TAP = take(3, TT)
            ME = sb_[:, 0, :]
            halves = [(0, TX, 0), (TX, TT, 1)][:1 if width == TX else 2]
            yoff = (PAD, XW + PAD)
            stage = f"conv{j_}"
            layer_input(layer, Z, width, sq, RST, PSTART[stage] + 2)
            a_read, b_read, g_read, s_free, z2_ready, z2_used = (sem(n) for n in ("a_read", "b_read", "g_read", "s_free", "z2_ready", "z2_used"))
            tap_ready, tap_used = sem("tap_ready"), sem("tap_used")
            sections = [range(SHARE + 3 * s, SHARE + 3 * s + 3) for s in range(3)]

            def tap_buffer(m, t):
                if t == SHARE:
                    return None, Z2[:, m % 2]
                j = m * (TAPS - SHARE - 1) + t - SHARE - 1
                return j, TAP[:, j % 3]

            def multiply_taps(a, m, s):
                for t in sections[s]:
                    j, o = tap_buffer(m, t)
                    if j is None and m >= 2:
                        a.wait_ge(z2_used, m - 1)
                    if j is None:
                        a.wait_ge(s_free, nh * (m + 1))
                    elif j >= 3:
                        a.wait_ge(tap_used, 2 * (j - 2))
                    for (p, q, y) in pieces:
                        act(o[:, p:q], YP[:, m % 2, y + t - PAD:y + t - PAD + q - p], ACT.Copy,
                            scale=V("conv_dw_2", (j_ * TAPS + t) * DT + m)).then_inc(tap_ready, 1)

            def add_taps(g, m, s):
                for t in sections[s]:
                    j, o = tap_buffer(m, t)
                    g.wait_ge(tap_ready, 2 * (m * (TAPS - SHARE) + t - SHARE + 1))
                    if j is not None:
                        g.wait_ge(tap_used, 2 * j)
                        for (p, q, y) in pieces:
                            nc.gpsimd.tensor_tensor(Z2[:, m % 2, p:q], Z2[:, m % 2, p:q], o[:, p:q], ALU.add).then_inc(tap_used, 1)
                if s == 2:
                    g.wait_ge(tap_used, 2 * (m + 1) * (TAPS - SHARE - 1))
                    g.nop().then_inc(z2_ready, 1)

            nh = len(halves)
            pieces = [(0, TX, yoff[0]), (TX, TT, yoff[1])] if nh == 2 else [(0, TX // 2, yoff[0]), (TX // 2, TX, yoff[0] + TX // 2)]
            with nc.Block() as block:
                @block.sync
                def _(sp):
                    R.supply(sp, RINGT, weights, START[f"convout{j_}"] + SLOTS)

                @block.tensor
                def _(pe):
                    for m in range(DT):
                        for part, read in enumerate((a_read, b_read, g_read)):
                            if m >= 1:
                                pe.wait_ge(read, m)
                            tile_product(pe, PS[:, part * 1024:part * 1024 + width], width)
                            if next_mod is not None:
                                mod_block(pe, 3 * m + part)

                @block.scalar
                def _(a):
                    for m in range(DT):
                        base = PSTART[stage] + 3 * m + 1
                        round_block(a, base + 1)
                        if m >= 2:
                            a.wait_ge(s_free, nh * (m - 1))
                        a.wait_ge(blocks_done, base)
                        act(sa[:, m % 2, 0:width], PS[:, 0:width], ACT.Copy).then_inc(a_read, 1)
                        if m >= 1:
                            multiply_taps(a, m - 1, 0)
                        round_block(a, base + 2)
                        a.wait_ge(blocks_done, base + 1)
                        act(sb_[:, m % 2, 0:width], PS[:, 1024:1024 + width], ACT.Sigmoid).then_inc(b_read, 1)
                        if m >= 1:
                            multiply_taps(a, m - 1, 1)
                        round_block(a, base + 3)
                        a.wait_ge(blocks_done, base + 2)
                        act(G[:, m, 0:width], PS[:, 2048:2048 + width], ACT.Silu).then_inc(g_read, 1)
                        if m >= 1:
                            multiply_taps(a, m - 1, 2)
                    round_block(a, PSTART[stage] + 3 * DT + 2)
                    for s in range(3):
                        multiply_taps(a, DT - 1, s)

                @block.gpsimd
                def _(g):
                    plink(nc.gpsimd.memset(YP, 0.0))
                    for m in range(DT):
                        part_block(g, PSTART[stage] + 3 * m + 2)
                        if m >= 1:
                            add_taps(g, m - 1, 0)
                        part_block(g, PSTART[stage] + 3 * m + 3)
                        if m >= 1:
                            add_taps(g, m - 1, 1)
                        part_block(g, PSTART[stage] + 3 * m + 4)
                        if m >= 2:
                            g.wait_ge(z2_used, m - 1)
                        g.wait_ge(a_read, m + 1)
                        g.wait_ge(b_read, m + 1)
                        for (a, b, c) in halves:
                            nc.gpsimd.tensor_tensor(YP[:, m % 2, yoff[c]:yoff[c] + b - a], sa[:, m % 2, a:b], sb_[:, m % 2, a:b], ALU.mult).then_inc(s_free, 1)
                        if m >= 1:
                            add_taps(g, m - 1, 2)
                    part_block(g, PSTART[stage] + 3 * DT + 2)
                    for s in range(3):
                        add_taps(g, DT - 1, s)

                @block.vector
                def _(v):
                    for m in range(DT):
                        v.wait_ge(s_free, nh * (m + 1))
                        for t in range(SHARE):
                            for n, (a, b, y) in enumerate(pieces):
                                src = YP[:, m % 2, y + t - PAD:y + t - PAD + b - a]
                                wt = V("conv_dw_2", (j_ * TAPS + t) * DT + m)
                                if t == 0:
                                    ins = vts(Z[:, m, a:b], src, wt, V("conv_db_2", j_ * DT + m), ALU.mult, ALU.add)
                                else:
                                    if n == 0:
                                        dve_chain.wait(v)
                                    ins = stt(Z[:, m, a:b], src, wt, Z[:, m, a:b], ALU.mult, ALU.add)
                                dve_chain.inc(ins)
                        dve_chain.wait(v)
                        v.wait_ge(z2_ready, m + 1)
                        vtt(Z[:, m, 0:width], Z[:, m, 0:width], Z2[:, m % 2, 0:width], ALU.add).then_inc(z2_used, 1)

            z_summed, centred = sem("z_summed"), sem("centred")
            with nc.Block() as block:
                @block.tensor
                def _(pe):
                    for k in range(DT):
                        last = product(PS, C("ones"), Z[:, k, :], width, k == 0, k == DT - 1)
                    last.then_inc(z_summed, 1)

                @block.scalar
                def _(a):
                    a.wait_ge(z_summed, 1)
                    act(ME[:, 0:width], PS[:, 0:width], ACT.Copy, scale=1.0 / D).then_inc(centred, 1)

                @block.vector
                def _(v):
                    if next_mod is not None:
                        mod_finish(next_mod)
                    v.wait_ge(centred, 1)
                    for k in range(DT):
                        dlink(vtt(Z[:, k, 0:width], Z[:, k, 0:width], ME[:, 0:width], ALU.subtract))
            norm_stats([Z[:, k, 0:width] for k in range(DT)], width, "ones", 1.0 / D, LN_EPS, RST[:, 0:width],
                       [sq[:, 0, 0:width], sq[:, 1, 0:width]], PS)
            scaled, silued, gated_ = sem("scaled"), sem("silued"), sem("gated_")
            Hh, Hl = PARTS["H"][:, 0], PARTS["H"][:, 1]

            def silu_and_high(a, base, base_low):
                for k in range(DT + 1):
                    if k < DT:
                        a.wait_ge(scaled, k + 1)
                        act(Z[:, k, 0:width], Z[:, k, 0:width], ACT.Silu, scale=V("conv_ln_g_2", j_ * DT + k),
                            bias=V("conv_ln_b_2", j_ * DT + k)).then_inc(silued, 1)
                    if k >= 1:
                        a.wait_ge(gated_, k)
                        act(Hh[:, k - 1, 0:width], Z[:, k - 1, 0:width], ACT.Copy).then_inc(split_hi, 1)

            def gate_and_low(v, base, base_low):
                for k in range(DT + 2):
                    if k < DT:
                        vtt(Z[:, k, 0:width], Z[:, k, 0:width], RST[:, 0:width]).then_inc(scaled, 1)
                    if 1 <= k <= DT:
                        v.wait_ge(silued, k)
                        vtt(Z[:, k - 1, 0:width], Z[:, k - 1, 0:width], G[:, k - 1, 0:width]).then_inc(gated_, 1)
                    if k >= 2:
                        v.wait_ge(split_hi, base + k - 1)
                        vtt(Hl[:, k - 2, 0:width], Z[:, k - 2, 0:width], Hh[:, k - 2, 0:width].bitcast(F32), ALU.subtract).then_inc(split_low, 1)

            add_products(f"convout{j_}", width, lambda m, c: MODL[:, layer, 16 + m, c:c + 1],
                         2 if j_ == 0 else 0, split=(silu_and_high, gate_and_low))

        conv_layer(0, 0, TT, 1)

        take = carve()
        HP = take(DT, TT + 4)
        XX = take(DT, TT)
        LF = take(DT, TT)
        STG = take(4, TT)
        TW, TA = take(TT), take(TT)
        HALF = [(0, TX, 0), (TX, TT, 1)]
        hoff = (1, TX + 3)
        layer_input(1, None, TT, LF[:, 0:2, :], LF[:, 2, :], PSTART["lora"] + 2, (HP[:, :, 1:1 + TX], HP[:, :, TX + 3:TX + 3 + TC]))
        with nc.Block() as block:
            @block.vector
            def _(v):
                for z in (0, TX + 1, TX + 2, TX + TC + 3):
                    dlink(nc.vector.memset(HP[:, :, z:z + 1], 0.0))
                for a, b, c in HALF:
                    n, o = b - a, hoff[c]
                    dlink(vtt(XX[:, :, a:b], HP[:, :, o - 1:o - 1 + n], HP[:, :, o + 1:o + 1 + n], ALU.add))
                    dlink(stt(XX[:, :, a:b], XX[:, :, a:b], 0.5, HP[:, :, o:o + n], ALU.mult, ALU.subtract))

        groups = [(1, [("lora", 0, 0)]), (4, [("lora", 1, 0)])]
        groups += [(mu, [("rkvg"[q], q, m) for m in range(DT)]) for q, mu in enumerate((0, 2, 3, 5))]
        second = [("w", d, m) for m in range(DT) for d in range(2)] + [("a", d, m) for m in range(DT) for d in range(2)]
        seq = groups[0][1] + groups[1][1] + second + [o for _, g in groups[2:] for o in g]
        l_ready, hi_ready, h_split, h_used, prod, ev = (sem(n) for n in ("l_ready", "hi_ready", "h_split", "h_used", "prod", "ev"))
        slot_stored = [sem(f"slot_stored{s}") for s in range(4)]
        NO = len(seq)
        limit = PSTART["rwkvout"]
        with nc.Block() as block:
            @block.sync
            def _(sp):
                R.supply(sp, RINGT, weights, START["rwkvout"] + SLOTS)

            @block.vector
            def _(v):
                for n, (mu, _g) in enumerate(groups):
                    for k in range(DT):
                        for a, b, c in HALF:
                            stt(LF[:, k, a:b], XX[:, k, a:b], V("rwkv_mu_2", mu * DT + k),
                                HP[:, k, hoff[c]:hoff[c] + b - a], ALU.mult, ALU.add).then_inc(l_ready, 1)
                    for k in range(DT):
                        v.wait_ge(hi_ready, DT * n + k + 1)
                        vtt(PARTS["H"][:, 1, k, :], LF[:, k, :], PARTS["H"][:, 0, k, :].bitcast(F32), ALU.subtract).then_inc(h_split, 1)
                    v.wait_ge(h_split, DT * (n + 1))

            @block.tensor
            def _(pe):
                n = 0

                def area():
                    return PS[:, (n % 3) * 1024:(n % 3) * 1024 + TT]

                for e, (_mu, prods) in enumerate(groups):
                    if e == 2:
                        for T_ in (TW, TA):
                            s = R.take_direct(pe)
                            for m in range(DT):
                                for d in range(2):
                                    pe.wait_ge(ev, max(n - 2, 2))
                                    product(area(), RINGT[d * 64:d * 64 + 64, s, m * P:m * P + P], T_[d * 64:d * 64 + 64, :], TT, True, True).then_inc(prod, 1)
                                    n += 1
                                    pe.wait_ge(prod, 1 + n - 1)
                            pe.nop().then_inc(direct_done, 1)
                    for kind, q, m in prods:
                        if n >= 3:
                            pe.wait_ge(ev, n - 2)
                        tile_product(pe, area(), TT, fresh=(h_split, DT * e) if m == 0 else None,
                                     used=h_used if (kind, q, m) == prods[-1] and e + 1 < len(groups) else None)
                        pe.wait_ge(blocks_done, done["take"])
                        pe.nop().then_inc(prod, 1)
                        n += 1
                        if e >= 2 and (e - 2) * DT + m < 24:
                            mod_block(pe, (e - 2) * DT + m)

            @block.gpsimd
            def _(g):
                part_block(g, limit)

            @block.scalar
            def _(a):
                taken = PSTART["lora"]

                def split_input(e):
                    for k in range(DT):
                        a.wait_ge(l_ready, 2 * (DT * e + k + 1))
                        if e >= 1 and k < DT - 1:
                            a.wait_ge(h_used, (DT - 1) * (e - 1) + k + 1)
                        elif e >= 1:
                            a.wait_ge(blocks_done, PSTART["lora"] + (e if e <= 2 else 2 + DT * (e - 2)))
                        act(PARTS["H"][:, 0, k, :], LF[:, k, :], ACT.Copy).then_inc(hi_ready, 1)

                split_input(0)
                e = 1
                for n, (kind, q, m) in enumerate(seq):
                    if kind not in "wa":
                        taken += 1
                        round_block(a, min(taken + 1, limit))
                    if n == 0 or n == 1 or (kind in "rkv" and m == DT - 1):
                        split_input(e)
                        e += 1
                    a.wait_ge(prod, n + 1)
                    src = PS[:, (n % 3) * 1024:(n % 3) * 1024 + TT]
                    if kind == "lora":
                        act((TW, TA)[q], src, (ACT.Tanh, ACT.Copy)[q]).then_inc(ev, 1)
                        continue
                    sl = (n - 2) % 4
                    if n >= 6:
                        a.wait_ge(slot_stored[sl], 16 * ((n - 2) // 4))
                    if kind in "wa":
                        ins = act(STG[:, sl, :], src, ACT.Sigmoid, bias=V({"w": "rwkv_w0_2", "a": "rwkv_a0_2"}[kind], q * DT + m))
                        at = (4 if kind == "w" else 6) + q
                    else:
                        ins = act(STG[:, sl, :], src, ACT.Silu if kind == "g" else ACT.Copy)
                        at = q
                    ins.then_inc(ev, 1)
                    a.wait_ge(ev, n + 1)
                    a.dma_start(rwkv_dram[m, at], STG[:, sl, :]).then_inc(slot_stored[sl], 16)

        with nc.Block() as block:
            @block.sync
            def _(sp):
                for sl in range(4):
                    sp.wait_ge(slot_stored[sl], 16 * ((NO - 2) // 4))
                sp.dma_start(x_dram, X.rearrange("p k t -> p (k t)")).then_inc(stores, 16)
                sp.wait_ge(stores, 16)

            @block.vector
            def _(v):
                mod_finish(2)

        memory("scan", False)
        take = carve()
        GM = [take(NSTEP, 2, P) for _ in range(2)]
        TINV = [take(NSTEP, P) for _ in range(2)]
        BKT = [take(NSTEP, 2, CH) for _ in range(2)]
        UV = [take(NSTEP, 2, CH) for _ in range(2)]
        AV = [take(NSTEP, CH) for _ in range(2)]
        AR = [take(NSTEP, 2, CH) for _ in range(2)]
        EBC = [take(NSTEP) for _ in range(2)]
        BK = take(NSTEP, 2, CH)
        VS = take(TT + 2 * CH)
        BON, BONV, GATE = take(TT), take(TT), take(TT)
        O2 = take(2, TT)
        KK, A_, B_, C_, D_, E_, F_ = (take(TT) for _ in range(7))
        OS = take(TT)
        ST = take(2, CH)
        RS = take(CH)
        PC = take(6)
        PCF = take(2)
        IN = X.rearrange("p k t -> p (k t)").rearrange("p (q t) -> p q t", q=8)
        GU = 3
        grp = [{n: take(GU, P) for n in ("AT", "T1", "NT0", "NT1")} for _ in range(2)]
        for g_ in grp:
            g_["PQ"], g_["PT"] = [take(GU, P) for _ in range(2)], [take(GU, P) for _ in range(2)]
        CM = take(TT)
        NSUP = NSTEP // (2 * GU)
        NLV = 5

        loaded, y_out = sem("pair_loaded"), sem("y_out")
        m_sem = {n: sem(n) for n in ("dve_prep", "kk_ready", "kk_squared", "kk_summed", "kk_logged", "kk_root", "b_ready", "exp_ready",
                                     "a_laid", "a_turned", "dve_inv", "n_masked", "p_ready", "t_done", "t_copied", "up_done",
                                     "pt_added", "state_ready", "r_done", "r_added", "u_done", "u_low", "u_high",
                                     "s_done", "o_done", "o_copied")}
        q_sem = {n: sem(n) for n in ("dve_q", "ar_ready", "v_ready", "v_turned", "v_copied", "g_done", "g_masked", "bk_decayed",
                                     "av_done", "bk_turned", "bonus_done", "a_laid", "a_turned", "p_ready",
                                     "f_dve", "f_summed", "f_act", "bonus_read")}

        def chunk3(t):
            return t.rearrange("p (n t) -> p n t", t=CH)

        def bank(n, w=512):
            return PS[:, n * 512:n * 512 + w]

        HS = (slice(0, 64), slice(64, 128))

        def prep_vector(v, d, i):
            ch = Chain(m_sem["dve_prep"])
            if d == 0:
                v.wait_ge(loaded, i * 16 + 16)
                for q, n in enumerate(("rwkv_k_k_2", "rwkv_k_a_2", "rwkv_r_k_2", "rwkv_ln_g_2", "rwkv_ln_b_2")):
                    ch.link(v, nc.vector.tensor_copy(PC[:, q:q + 1], VEC[:, bass.ds(i + VT[n][0], 1)]))
                ch.link(v, vts(PC[:, 5:6], PC[:, 1:2], -1.0, 1.0, ALU.mult, ALU.add))
                vts(KK, IN[:, 1, :], PC[:, 0:1]).then_inc(m_sem["kk_ready"], 1)
                yield
            ch.link(v, vts(B_, IN[:, 4 + d, :], -float(np.exp(-0.5))))
            yield
            o = 1 if d == 0 else -1
            ch.link(v, nc.vector.tensor_tensor_scan(C_[:, ::o], CM, B_[:, ::o], 0.0, ALU.mult, ALU.add))
            yield
            vtt(B_, C_, B_, ALU.subtract).then_inc(m_sem["b_ready"], 1)
            yield
            ch.link(v, vts(A_, IN[:, 6 + d, :], PC[:, 1:2], PC[:, 5:6], ALU.mult, ALU.add))
            yield
            ch.link(v, vtt(A_, A_, IN[:, 1, :]))
            yield
            if d == 0:
                ch.link(v, nc.vector.tensor_copy(BON, A_))
            else:
                ch.link(v, vtt(BON, BON, A_, ALU.add))
                yield
                ch.link(v, stt(BON, IN[:, 0, :], PC[:, 2:3], BON, ALU.mult, ALU.mult))
            yield
            v.wait_ge(m_sem["exp_ready"], 3)
            for h in range(2):
                ch.link(v, vtt(BK[HS[h], :, 1 - h, :], chunk3(A_)[HS[h]], chunk3(E_)[HS[h]]))
                yield
            if d == 0:
                v.wait_ge(m_sem["kk_root"], 1)
                ch.link(v, vtt(KK, KK, OS))
                yield
            ch.link(v, vtt(A_, KK, IN[:, 6 + d, :]))
            yield
            for h in range(2):
                ch.inc(vtt(BK[HS[h], :, h, :], chunk3(A_)[HS[h]], chunk3(E_)[HS[h]]))
                yield

        def prep_scalar(a, d):
            if d == 0:
                a.wait_ge(m_sem["kk_ready"], 1)
                act(F_, KK, ACT.Square).then_inc(m_sem["kk_squared"], 1)
                yield
                yield
                yield
                for n, (lo, hi) in enumerate(((0, 512), (512, TT))):
                    a.wait_ge(m_sem["kk_summed"], n + 1)
                    act(OS[:, lo:hi], bank(2 + 3 * n, hi - lo), ACT.Ln, bias=EPSC[1e-12]).then_inc(m_sem["kk_logged"], 1)
                yield
                a.wait_ge(m_sem["kk_logged"], 2)
                act(OS, OS, ACT.Exp, scale=-0.5).then_inc(m_sem["kk_root"], 1)
                yield
            else:
                yield
                yield
                yield
            a.wait_ge(m_sem["b_ready"], 1)
            act(E_, C_, ACT.Exp, scale=-1.0).then_inc(m_sem["exp_ready"], 1)
            yield
            act(F_, B_, ACT.Exp).then_inc(m_sem["exp_ready"], 1)
            yield
            act(D_, C_, ACT.Exp).then_inc(m_sem["exp_ready"], 1)
            yield

        def kk_sums(pe):
            pe.wait_ge(m_sem["kk_squared"], 1)
            mm(bank(2), C("ones64"), F_[:, 0:512]).then_inc(m_sem["kk_summed"], 1)
            mm(bank(5, TT - 512), C("ones64"), F_[:, 512:TT]).then_inc(m_sem["kk_summed"], 1)

        identb = C("ident").rearrange("p (o t) -> p o t", o=1).broadcast_to([P, GU, P])

        def maskb(level):
            return C("inv_mask", level * P, P).rearrange("p (o t) -> p o t", o=1).broadcast_to([P, GU, P])

        def bank3(n):
            return bank(n, GU * P).rearrange("p (q t) -> p q t", q=GU)

        INV_SLOTS = NSUP * 4 * NLV
        LOAD_SLOTS = 8
        KK_LEVEL = 3

        def lay_out(v, d, s, e, ch, sems, n):
            g = grp[e]
            us = slice(GU * (2 * s + e), GU * (2 * s + e) + GU)
            ch.link(v, nc.vector.tensor_copy(g["AT"][0:64, :, 0:64], GM[d][0:64, us, 0, 0:64]))
            nc.vector.tensor_copy(g["AT"][64:128, :, 64:128], GM[d][64:128, us, 1, 64:128]).then_inc(sems["a_laid"], 1)
            v.wait_ge(sems["a_laid"], n)
            ch.link(v, vtt(g["PT"][s % 2], g["AT"], maskb(0)))
            ch.link(v, vtt(g["PT"][s % 2], g["PT"][s % 2], identb, ALU.add))

        def turn(pe, e, into, sems, n):
            pe.wait_ge(sems["a_laid"], n)
            for q in range(GU):
                last = nc.tensor.transpose(bank(into)[:, q * P:q * P + P], grp[e]["AT"][:, q, :], C("ident"))
            last.then_inc(sems["a_turned"], 1)

        def first_p(v, s, e, ch, source, sems, n):
            v.wait_ge(sems["a_turned"], n)
            PQ = grp[e]["PQ"][s % 2]
            ch.link(v, vtt(PQ, bank3(source), maskb(0)))
            vtt(PQ, PQ, identb, ALU.add).then_inc(sems["p_ready"], 1)

        def starts_next(s, lv):
            return lv == NLV - 1 and s + 1 < NSUP

        def inv_tensor(pe, d, kk_beside):
            for s in range(NSUP):
                for lv in range(NLV):
                    for e in range(2):
                        g, n = grp[e], (s * NLV + lv) * 2 + e
                        if n >= 2:
                            pe.wait_ge(m_sem["n_masked"], n - 1)
                            pe.wait_ge(m_sem["p_ready"], n - 1)
                        for q in range(GU):
                            last = mm(bank(3 * e)[:, q * P:q * P + P], g[f"NT{(s * NLV + lv) % 2}"][:, q, :], g["PQ"][s % 2][:, q, :])
                        last.then_inc(m_sem["t_done"], 1)
                        if kk_beside and s == 0 and lv == KK_LEVEL and e == 1:
                            kk_sums(pe)
                        yield
                    for e in range(2):
                        g, n = grp[e], (s * NLV + lv) * 2 + e
                        if starts_next(s, lv):
                            turn(pe, e, 3 * e + 2, m_sem, 2 * s + e + 1)
                        pe.wait_ge(m_sem["t_copied"], n + 1)
                        if lv > 0:
                            pe.wait_ge(m_sem["pt_added"], 2 * (s * (NLV - 1) + lv - 1) + e + 1)
                        if kk_beside and s == 0 and lv == KK_LEVEL:
                            pe.wait_ge(m_sem["kk_logged"], e + 1)
                        for q in range(GU):
                            last = mm(bank(3 * e + 1)[:, q * P:q * P + P], g["T1"][:, q, :], g["PT"][s % 2][:, q, :])
                        if lv < NLV - 1:
                            for q in range(GU):
                                last = mm(bank(3 * e + 2)[:, q * P:q * P + P], g["PT"][s % 2][:, q, :], g["T1"][:, q, :])
                        last.then_inc(m_sem["up_done"], 1)
                        yield

        def inv_pool(gp):
            for s in range(NSUP):
                for lv in range(NLV):
                    for e in range(2):
                        g, n = grp[e], (s * NLV + lv) * 2 + e
                        if n < 2:
                            continue
                        if lv == 0:
                            gp.wait_ge(m_sem["a_laid"], 2 * (s - 1) + e + 1)
                        if n >= 4:
                            gp.wait_ge(m_sem["t_done"], n - 3)
                        nc.gpsimd.tensor_tensor(g[f"NT{(s * NLV + lv) % 2}"], g["AT"], maskb(lv + 1), ALU.mult).then_inc(m_sem["n_masked"], 1)

        def inv_scalar(a):
            for s in range(NSUP):
                for lv in range(NLV):
                    for e in range(2):
                        n = (s * NLV + lv) * 2 + e
                        a.wait_ge(m_sem["t_done"], n + 1)
                        act(grp[e]["T1"], bank3(3 * e), ACT.Copy).then_inc(m_sem["t_copied"], 1)
                        yield
                    yield
                    yield

        def inv_vector(v, d):
            ch = Chain(m_sem["dve_inv"])
            for s in range(NSUP):
                for lv in range(NLV):
                    for e in range(2):
                        if starts_next(s, lv):
                            if e == 0:
                                v.wait_ge(m_sem["n_masked"], (s + 1) * 2 * NLV - 2)
                            lay_out(v, d, s + 1, e, ch, m_sem, 2 * s + e + 1)
                        yield
                    for e in range(2):
                        g, n = grp[e], (s * NLV + lv) * 2 + e
                        PQ, PT = g["PQ"][s % 2], g["PT"][s % 2]
                        v.wait_ge(m_sem["up_done"], n + 1)
                        if lv > 0:
                            v.wait_ge(m_sem["pt_added"], 2 * (s * (NLV - 1) + lv - 1) + e + 1)
                        if lv == NLV - 1:
                            u0 = GU * (2 * s + e)
                            ch.inc(vtt(TINV[d][:, u0:u0 + GU, :], bank3(3 * e + 1), PT, ALU.add))
                        else:
                            vtt(PQ, bank3(3 * e + 2), PQ, ALU.add).then_inc(m_sem["p_ready"], 1)
                            vtt(PT, bank3(3 * e + 1), PT, ALU.add).then_inc(m_sem["pt_added"], 1)
                        if starts_next(s, lv):
                            first_p(v, s + 1, e, ch, 3 * e + 2, m_sem, 2 * s + e + 1)
                        yield

        def chunk_of(d, st):
            return (NCX + st) % NSTEP if d == 0 else NSTEP - 1 - st

        R_, U_, S_ = (PS[:, 6 * 512 + n * CH:6 * 512 + n * CH + CH] for n in range(3))
        O_ = PS[:, 7 * 512:7 * 512 + CH]
        CHAIN_SLOTS = 3 * NSTEP

        def chain_tensor(pe, d):
            for st in range(NSTEP):
                u = chunk_of(d, st)
                S = ST[:, st % 2, :]
                pe.wait_ge(m_sem["state_ready"], st + 1)
                for h in range(2):
                    last = mm(R_[HS[h]], AR[d][HS[h], u, 0, :], S[HS[h]])
                last.then_inc(m_sem["r_done"], 1)
                yield
                pe.wait_ge(m_sem["r_added"], st + 1)
                mm(U_, TINV[d][:, u, :], RS).then_inc(m_sem["u_done"], 1)
                yield
                pe.wait_ge(m_sem["u_low"], st + 1)
                pe.wait_ge(m_sem["u_high"], st + 1)
                for h in range(2):
                    last = mm(S_[HS[h]], BKT[d][:, u, h, :], UV[d][:, u, h, :])
                last.then_inc(m_sem["s_done"], 1)
                if st >= 1:
                    pe.wait_ge(m_sem["o_copied"], st)
                for h in range(2):
                    rc = slice(64, 128) if h == 0 else slice(0, 64)
                    mm(O_[HS[h]], UV[d][:, u, h, :], GM[d][:, u, h, rc], True, False)
                    last = mm(O_[HS[h]], S[HS[h]], AR[d][HS[h], u, 1, :], False, True)
                last.then_inc(m_sem["o_done"], 1)
                yield

        def chain_vector(v, d):
            nc.vector.memset(ST[:, 0, :], 0.0).then_inc(m_sem["state_ready"], 1)
            for st in range(NSTEP):
                u = chunk_of(d, st)
                v.wait_ge(m_sem["r_done"], st + 1)
                vtt(RS, R_, AV[d][:, u, :], ALU.add).then_inc(m_sem["r_added"], 1)
                yield
                v.wait_ge(m_sem["u_done"], st + 1)
                nc.vector.tensor_copy(UV[d][0:64, u, 0, :], U_[0:64]).then_inc(m_sem["u_low"], 1)
                yield
                v.wait_ge(m_sem["s_done"], st + 1)
                if st >= 1:
                    v.wait_ge(m_sem["o_done"], st)
                v.wait_ge(m_sem["state_ready"], st + 1)
                stt(ST[:, (st + 1) % 2, :], ST[:, st % 2, :], EBC[d][:, u:u + 1], S_, ALU.mult, ALU.add).then_inc(m_sem["state_ready"], 1)
                yield

        def chain_scalar(a, d):
            for st in range(NSTEP):
                u = chunk_of(d, st)
                yield
                a.wait_ge(m_sem["u_done"], st + 1)
                act(UV[d][64:128, u, 1, :], U_[64:128], ACT.Copy).then_inc(m_sem["u_high"], 1)
                yield
                a.wait_ge(m_sem["o_done"], st + 1)
                act(O2[:, d, u * CH:u * CH + CH], O_, ACT.Copy).then_inc(m_sem["o_copied"], 1)
                yield

        def advance(gen):
            return next(gen, None) if gen is not None else None

        def interleave(inv, chain, prep, start=0):
            done = 0
            for t in range(INV_SLOTS if inv is not None else CHAIN_SLOTS):
                advance(inv)
                while chain is not None and done * INV_SLOTS < (t + 1) * CHAIN_SLOTS:
                    advance(chain)
                    done += 1
                if inv is None or (t >= start and t % 4 < 2):
                    advance(prep)
            for gen in (inv, chain, prep):
                for _ in gen or ():
                    pass

        def long_block(inv_d, chain_d, prep_d, i, load):
            with nc.Block() as block:
                @block.sync
                def _(sp):
                    if load is not None:
                        sp.wait_ge(y_out, load * 16)
                        sp.dma_start(IN, rwkv_dram[bass.ds(load, 1)].rearrange("a q p t -> p (a q) t")).then_inc(loaded, 16)

                @block.tensor
                def _(pe):
                    if inv_d is None and prep_d == 0:
                        kk_sums(pe)
                    interleave(None if inv_d is None else inv_tensor(pe, inv_d, prep_d == 0), None if chain_d is None else chain_tensor(pe, chain_d), None)

                @block.vector
                def _(v):
                    interleave(None if inv_d is None else inv_vector(v, inv_d), None if chain_d is None else chain_vector(v, chain_d),
                               None if prep_d is None else prep_vector(v, prep_d, i), LOAD_SLOTS if prep_d == 0 else 0)

                @block.scalar
                def _(a):
                    interleave(None if inv_d is None else inv_scalar(a), None if chain_d is None else chain_scalar(a, chain_d),
                               None if prep_d is None else prep_scalar(a, prep_d), LOAD_SLOTS if prep_d == 0 else 0)

                @block.gpsimd
                def _(gp):
                    for s in q_sem.values():
                        gp.sem_clear(s)
                    if inv_d is not None:
                        inv_pool(gp)

        def products_block(d):
            with nc.Block() as block:
                @block.vector
                def _(v):
                    ch = Chain(q_sem["dve_q"])
                    if d == 0:
                        nc.vector.tensor_copy(VS[:, CH:CH + TT], IN[:, 2, :]).then_inc(q_sem["v_ready"], 1)
                    vtt(AR[d][:, :, 1, :], chunk3(IN[:, 0, :]), chunk3(D_)).then_inc(q_sem["ar_ready"], 1)
                    stt(AR[d][:, :, 0, :], chunk3(KK), -1.0, chunk3(F_), ALU.mult, ALU.mult).then_inc(q_sem["ar_ready"], 1)
                    at = CH - 1 if d == 0 else 0
                    ch.link(v, nc.vector.tensor_copy(EBC[d].rearrange("p (n o) -> p n o", o=1), chunk3(D_)[:, :, at:at + 1]))
                    for g in range(3):
                        if g == 2:
                            v.wait_ge(q_sem["g_masked"], 4)
                            for e_ in range(2):
                                lay_out(v, d, 0, e_, ch, q_sem, e_ + 1)
                        for h in range(2):
                            n = 2 * g + h
                            v.wait_ge(q_sem["g_done"], n + 1)
                            m = C("wkv_mask", d * 256 + h * P, P).rearrange("p (o t) -> p o t", o=1).broadcast_to([P, 4, P])
                            vtt(GM[d][:, 4 * g:4 * g + 4, h, :], bank(2 * (g % 2) + h).rearrange("p (q t) -> p q t", q=4), m).then_inc(q_sem["g_masked"], 1)
                    e = EBC[d].rearrange("p (n o) -> p n o", o=1).broadcast_to([P, NSTEP, P])
                    b = BK.rearrange("p n s t -> p n (s t)")
                    vtt(b, b, e).then_inc(q_sem["bk_decayed"], 1)
                    for e_ in range(2):
                        first_p(v, 0, e_, ch, e_, q_sem, e_ + 1)
                    if d == 1:
                        v.wait_ge(q_sem["bonus_done"], 1)
                        vtt(BONV, PS[:, 3072:3072 + TT], VS[:, CH:CH + TT])
                        nc.vector.tensor_copy(GATE, IN[:, 3, :])
                        nc.vector.tensor_copy(PCF, PC[:, 3:5])
                    v.wait_ge(q_sem["av_done"], 1)
                    nc.vector.tensor_copy(AV[d], chunk3(PS[:, 2048:2048 + TT]))

                @block.tensor
                def _(pe):
                    if d == 0:
                        pe.wait_ge(q_sem["v_ready"], 1)
                    for h in range(2):
                        idh = CON[HS[h], CT["ident"][0] + 64 * h:CT["ident"][0] + 64 * h + 64]
                        for c in range(NSTEP):
                            o = (4 + 2 * h) * 512 + c * CH
                            last = nc.tensor.transpose(PS[:, o:o + CH], VS[HS[h], (c + h) * CH:(c + h) * CH + P], idh)
                        last.then_inc(q_sem["v_turned"], 1)
                    pe.wait_ge(q_sem["ar_ready"], 2)
                    for g in range(3):
                        for h in range(2):
                            if g == 2:
                                pe.wait_ge(q_sem["g_masked"], h + 1)
                            o = 1 if h == 0 else -1
                            for q in range(4):
                                u = 4 * g + q
                                last = mm(bank(2 * (g % 2) + h)[:, q * P:q * P + P], BK[HS[h], u].rearrange("p s t -> p (s t)"), AR[d][HS[h], u, ::o, :])
                            last.then_inc(q_sem["g_done"], 1)
                    pe.wait_ge(q_sem["v_copied"], 2)
                    if d == 1:
                        product(PS[:, 3072:3072 + TT], C("ones64"), BON, TT, True, True).then_inc(q_sem["bonus_done"], 1)
                    pe.wait_ge(q_sem["g_masked"], 6)
                    for u in range(NSTEP):
                        for h in range(2):
                            kr = HS[1 - h]
                            last = mm(PS[HS[h], 2048 + u * CH:2048 + u * CH + CH], GM[d][kr, u, h, 64 * h:64 * h + 64], UV[d][kr, u, h, :])
                        if u == 2:
                            for e_ in range(2):
                                turn(pe, e_, e_, q_sem, e_ + 1)
                    last.then_inc(q_sem["av_done"], 1)
                    pe.wait_ge(q_sem["bk_decayed"], 1)
                    for h in (1, 0):
                        if h == 0:
                            pe.wait_ge(q_sem["p_ready"], 2)
                        idh = CON[HS[h], CT["ident"][0] + 64 * h:CT["ident"][0] + 64 * h + 64]
                        for u in range(NSTEP):
                            o = h * 1024 + u * CH
                            last = nc.tensor.transpose(PS[:, o:o + CH], BK[HS[h], u].rearrange("p s t -> p (s t)"), idh)
                        last.then_inc(q_sem["bk_turned"], 1)

                @block.scalar
                def _(a):
                    for h in range(2):
                        a.wait_ge(q_sem["v_turned"], h + 1)
                        act(UV[d][:, :, h, :], chunk3(PS[:, (4 + 2 * h) * 512:(4 + 2 * h) * 512 + TT]), ACT.Copy).then_inc(q_sem["v_copied"], 1)
                    for h in (1, 0):
                        a.wait_ge(q_sem["bk_turned"], 2 - h)
                        act(BKT[d][:, :, h, :], chunk3(PS[:, h * 1024:h * 1024 + TT]), ACT.Copy)

                @block.gpsimd
                def _(gp):
                    for s in m_sem.values():
                        gp.sem_clear(s)
                    for e in range(2):
                        gp.wait_ge(q_sem["a_laid"], e + 1)
                        nc.gpsimd.tensor_tensor(grp[e]["NT0"], grp[e]["AT"], maskb(1), ALU.mult)

        def readout_block(dst):
            SQ_, RT_ = A_, B_
            with nc.Block() as block:
                @block.vector
                def _(v):
                    ch = Chain(q_sem["f_dve"])
                    ch.link(v, vtt(OS, O2[:, 0, :], O2[:, 1, :], ALU.add))
                    v.wait_ge(q_sem["f_summed"], 1)
                    ch.link(v, stt(OS, PS[:, 0:TT], -1.0 / CH, OS, ALU.mult, ALU.add))
                    v.wait_ge(q_sem["f_act"], 3)
                    ch.link(v, vtt(OS, OS, RT_))
                    ch.link(v, vts(OS, OS, PCF[:, 0:1], PCF[:, 1:2], ALU.mult, ALU.add))
                    ch.link(v, vtt(OS, OS, BONV, ALU.add))
                    ch.inc(vtt(OS, OS, GATE))

                @block.tensor
                def _(pe):
                    pe.wait_ge(q_sem["f_dve"], 1)
                    product(PS[:, 0:TT], C("ones64"), OS, TT, True, True).then_inc(q_sem["f_summed"], 1)
                    pe.wait_ge(q_sem["f_act"], 1)
                    product(PS[:, 1024:1024 + TT], C("ones64"), SQ_, TT, True, True).then_inc(q_sem["f_summed"], 1)

                @block.scalar
                def _(a):
                    a.wait_ge(q_sem["f_dve"], 2)
                    act(SQ_, OS, ACT.Square).then_inc(q_sem["f_act"], 1)
                    a.wait_ge(q_sem["f_summed"], 2)
                    act(RT_, PS[:, 1024:1024 + TT], ACT.Ln, scale=1.0 / CH, bias=EPSC[GN_EPS]).then_inc(q_sem["f_act"], 1)
                    a.wait_ge(q_sem["f_act"], 2)
                    act(RT_, RT_, ACT.Exp, scale=-0.5).then_inc(q_sem["f_act"], 1)

                @block.sync
                def _(sp):
                    sp.wait_ge(q_sem["f_dve"], 6)
                    sp.dma_start(dst, OS).then_inc(y_out, 16)

        with nc.Block() as block:
            @block.scalar
            def _(a):
                a.preload_act_table_set(LN_EXP)

            @block.vector
            def _(v):
                nc.vector.memset(CM, 1.0)
                nc.vector.memset(VS, 0.0)
                for g in grp:
                    dlink(nc.vector.memset(g["AT"], 0.0))
                dlink(nc.vector.memset(chunk3(CM)[:, :, 0:1], 0.0))

            @block.sync
            def _(sp):
                sp.dma_start(rwkv_dram[DT], rwkv_dram[0]).then_inc(y_out, 16)
                sp.dma_start(IN, rwkv_dram[0].rearrange("q p t -> p q t")).then_inc(loaded, 16)

        long_block(None, None, 0, 0, None)
        products_block(0)
        long_block(0, None, 1, 0, None)
        products_block(1)
        long_block(1, 0, 0, 1, 1)
        products_block(0)
        with nc.Fori(1, NPAIR) as i:
            long_block(0, 1, 1, i, None)
            readout_block(y_dram[bass.ds(i - 1, 1)].rearrange("a p t -> p (a t)"))
            products_block(1)
            long_block(1, 0, 0, i + 1, i + 1)
            products_block(0)
        long_block(None, 1, None, NPAIR, None)
        readout_block(y_dram[NPAIR - 1])

        memory("rwkv_out", True)
        take = carve()
        YR = take(DT, TT)
        with nc.Block() as block:
            @block.sync
            def _(sp):
                sp.wait_ge(y_out, 16 * (NPAIR + 1))
                sp.wait_ge(loaded, 16 * (NPAIR + 1))
                sp.dma_start(YR, y_dram.rearrange("k p t -> p k t")).then_inc(loads, 16)
                sp.dma_start(X.rearrange("p k t -> p (k t)"), x_dram).then_inc(loads, 16)
                sp.wait_ge(loads, 112)
        add_products("rwkvout", TT, lambda m, c: MODL[:, 1, 16 + m, c:c + 1], 0,
                     split=plain_split([YR[:, k, :] for k in range(DT)], TT))

        NQ, NKV = 16, 8
        KTILES = TT // P
        SCALE = float(P) ** -0.5
        GF = kept("gate", NQ * TX)
        G = GF.rearrange("p (h t) -> p h t", h=NQ)
        memory("attn", True, ROOM - NQ * TX)
        take = carve()
        Q = take(NQ, TX)
        VT_ = take(KTILES, D)
        K = X
        layer_input(2, GF[:, 0:DT * TT].rearrange("p (k t) -> p k t", k=DT), TT, VT_.rearrange("p a b -> p (a b)")[:, 0:2 * TT].rearrange("p (a b) -> p a b", a=2),
                    VT_.rearrange("p a b -> p (a b)")[:, 2 * TT:3 * TT], PSTART["attn_qk"] + 2)
        VF = GF[:, NQ * TX - 2 * TT:].rearrange("p (a t) -> p a t", a=2)
        freed, v_turned, v_read = sem("freed"), sem("v_turned"), sem("v_read")
        kinds = [("q", m) for m in range(NQ)] + [("k", m) for m in range(NKV)] + [("v", m) for m in range(DT)] + [("g", m) for m in range(NQ)]
        limit = PSTART["attnout"]
        with nc.Block() as block:
            @block.sync
            def _(sp):
                sp.dma_start(x_dram, X.rearrange("p k t -> p (k t)")).then_inc(stores, 16)
                R.supply(sp, RINGT, weights, START["attnout"] + SLOTS)

            @block.tensor
            def _(pe):
                for n, (kind, m) in enumerate(kinds):
                    if n >= 3:
                        pe.wait_ge(freed, n - 2)
                    o = PS[:, (n % 3) * 1024:(n % 3) * 1024 + 1024]
                    tile_product(pe, o, TT if kind in "kv" else TX)
                    if n < 24:
                        mod_block(pe, n)
                    if kinds[n - 1][0] == "v":
                        pe.wait_ge(freed, n)
                        pe.wait_ge(v_read, kinds[n - 1][1] + 1)
                        for t in range(KTILES):
                            last = nc.tensor.transpose(PS[:, 3072 + t * P:3072 + t * P + P], VF[:, kinds[n - 1][1] % 2, t * P:t * P + P], C("ident"))
                        last.then_inc(v_turned, 1)

            @block.vector
            def _(v):
                v.wait_ge(direct_done, ORDER[PLAN.index(("mod_w_2", 3, 23))] + 1)
                mod_finish(3)
                v.nop().then_inc(v_read, 1)
                for m in range(NKV):
                    v.wait_ge(v_turned, m + 1)
                    nc.vector.tensor_copy(VT_[:, :, m * P:m * P + P],
                                          PS[:, 3072:3072 + TT].rearrange("p (t v) -> p t v", t=KTILES)).then_inc(v_read, 1)

            @block.gpsimd
            def _(g):
                part_block(g, limit)

            @block.scalar
            def _(a):
                for n, (kind, m) in enumerate(kinds):
                    round_block(a, min(PSTART["attn_qk"] + n + 3, limit))
                    a.wait_ge(blocks_done, PSTART["attn_qk"] + n + 1)
                    if n == NQ:
                        a.wait_ge(stores, 32)
                    o = PS[:, (n % 3) * 1024:(n % 3) * 1024 + TT]
                    if kind == "v":
                        if m >= 2:
                            a.wait_ge(v_turned, m - 1)
                        ins = act(VF[:, m % 2, :], o, ACT.Copy)
                    elif kind == "k":
                        ins = act(K[:, m, :], o, ACT.Copy)
                    elif kind == "q":
                        ins = act(Q[:, m, :], o[:, 0:TX], ACT.Copy)
                    else:
                        ins = act(G[:, m, :], o[:, 0:TX], ACT.Silu)
                    ins.then_inc(freed, 1)

        tiles = [(Q[:, m, :], TX, V("attn_q_g_2")) for m in range(NQ)] + [(K[:, m, :], TT, V("attn_k_g_2")) for m in range(NKV)]
        sqd, summed, rst_, rs_used, normed, rotated, roped = (sem(n) for n in ("sqd", "summed", "rst", "rs_used", "normed", "rotated", "roped"))
        parts_scope.close()
        area("parts", "softmax", SPLIT)
        take = carve()
        HF = take(DT * TT)
        PR = take(2, TT)
        ROPE = take(2, TX)
        STAT = take(2, 4)
        SQ_ = [HF[:, n * TT:n * TT + TT] for n in range(2)]
        RS_ = [HF[:, (2 + n) * TT:(3 + n) * TT] for n in range(2)]
        SN_ = [HF[:, (4 + n) * TT:(4 + n) * TT + TX] for n in range(2)]
        NT_ = len(tiles)
        with nc.Block() as block:
            @block.sync
            def _(sp):
                sp.dma_start(ROPE.rearrange("p a t -> p (a t)"), rope).then_inc(loads, 16)

            @block.scalar
            def _(a):
                a.preload_act_table_set(LN_EXP)
                for n in range(NT_ + 1):
                    if n < NT_:
                        x_, w, _g = tiles[n]
                        if n >= 2:
                            a.wait_ge(summed, n - 1)
                        act(SQ_[n % 2][:, 0:w], x_[:, 0:w], ACT.Square).then_inc(sqd, 1)
                    if n >= 1:
                        m = n - 1
                        x_, w, _g = tiles[m]
                        a.wait_ge(summed, m + 1)
                        if m >= 2:
                            a.wait_ge(normed, m - 1)
                        alink(act(RS_[m % 2][:, 0:w], PS[:, (m % 2) * 1024:(m % 2) * 1024 + w], ACT.Ln, scale=1.0 / P, bias=EPSC[EPS]))
                        act(RS_[m % 2][:, 0:w], RS_[m % 2][:, 0:w], ACT.Exp, scale=-0.5).then_inc(rst_, 1)

            @block.tensor
            def _(pe):
                for n in range(NT_ + 1):
                    if n < NT_:
                        pe.wait_ge(sqd, n + 1)
                        if n >= 2:
                            pe.wait_ge(rst_, n - 1)
                        product(PS[:, (n % 2) * 1024:(n % 2) * 1024 + tiles[n][1]], C("ones"), SQ_[n % 2], tiles[n][1], True, True).then_inc(summed, 1)
                    if n >= 1:
                        m = n - 1
                        pe.wait_ge(normed, m + 1)
                        if m >= 2:
                            pe.wait_ge(rotated, m - 1)
                        mm(PS[:, 2048 + (m % 2) * 512:2048 + (m % 2) * 512 + 512], C("rot"), tiles[m][0][:, 0:TX]).then_inc(roped, 1)

            @block.vector
            def _(v):
                v.wait_ge(loads, 128)
                for n in range(NT_ + 1):
                    if n < NT_:
                        x_, w, g_ = tiles[n]
                        v.wait_ge(rst_, n + 1)
                        stt(x_[:, 0:w], x_[:, 0:w], g_, RS_[n % 2][:, 0:w]).then_inc(normed, 1)
                    if n >= 1:
                        m = n - 1
                        x_ = tiles[m][0]
                        v.wait_ge(roped, m + 1)
                        dve_chain.inc(vtt(SN_[m % 2], PS[:, 2048 + (m % 2) * 512:2048 + (m % 2) * 512 + 512], ROPE[:, 1, :]))
                        vtt(x_[:, 0:TX], x_[:, 0:TX], ROPE[:, 0, :]).then_inc(rotated, 1)
                        dve_chain.wait(v)
                        v.wait_ge(rotated, m + 1)
                        dlink(vtt(x_[:, 0:TX], x_[:, 0:TX], SN_[m % 2], ALU.add))

        NQB = TX // P
        N = NQ * NQB
        PTS = HF.rearrange("p (e k t) -> p e k t", e=2, k=KTILES)
        s_done, negmax, exped, scaled, tr0, tr1, cp0, cp1, pv_done, o_read = (
            sem(n) for n in ("s_done", "negmax", "exped", "scaled", "tr0", "tr1", "cp0", "cp1", "pv_done", "o_read"))
        with nc.Block() as block:
            @block.tensor
            def _(pe):
                def scores(n):
                    h, qb = n // NQB, n % NQB
                    if n >= 2:
                        pe.wait_ge(exped, n - 1)
                    product(PS[:, (n % 2) * 1024:(n % 2) * 1024 + TT], Q[:, h, qb * P:qb * P + P], K[:, h // 2, :], TT, True, True).then_inc(s_done, 1)

                def output(h):
                    pe.wait_ge(cp0, NQB * (h + 1))
                    pe.wait_ge(cp1, NQB * (h + 1))
                    if h >= 2:
                        pe.wait_ge(o_read, h - 1)
                    for k in range(KTILES):
                        last = mm(PS[:, 3072 + (h % 2) * 512:3072 + (h % 2) * 512 + 512], VT_[:, k, (h // 2) * P:(h // 2) * P + P],
                                  PTS[:, h % 2, k, :], k == 0, k == KTILES - 1)
                    last.then_inc(pv_done, 1)

                scores(0)
                scores(1)
                for n in range(N):
                    h, qb = n // NQB, n % NQB
                    if n + 2 < N:
                        scores(n + 2)
                    pe.wait_ge(scaled, n + 1)
                    if n >= 1:
                        pe.wait_ge(cp0, n)
                    for k in range(4):
                        last = nc.tensor.transpose(PS[:, 2048 + k * P:2048 + k * P + P], PR[:, n % 2, k * P:k * P + P], C("ident"))
                    last.then_inc(tr0, 1)
                    if n >= 1:
                        pe.wait_ge(cp1, n)
                    for k in range(4, KTILES):
                        last = nc.tensor.transpose(PS[:, 2048 + k * P:2048 + k * P + P], PR[:, n % 2, k * P:k * P + P], C("ident"))
                    last.then_inc(tr1, 1)
                    if qb == 0 and h >= 1:
                        output(h - 1)
                output(NQ - 1)

            @block.vector
            def _(v):
                def maxima(n):
                    v.wait_ge(s_done, n + 1)
                    dlink(nc.vector.reduce_max(STAT[:, n % 2, 0:1], PS[:, (n % 2) * 1024:(n % 2) * 1024 + TT], AX.X))
                    vts(STAT[:, n % 2, 1:2], STAT[:, n % 2, 0:1], -SCALE).then_inc(negmax, 1)

                maxima(0)
                def turned(n):
                    h, qb = n // NQB, n % NQB
                    v.wait_ge(tr1, n + 1)
                    if n >= 8 and qb == 0:
                        v.wait_ge(pv_done, h - 1)
                    nc.vector.tensor_copy(PTS[:, h % 2, 4:6, qb * P:qb * P + P],
                                          PS[:, 2560:2560 + 2 * P].rearrange("p (k t) -> p k t", k=2)).then_inc(cp1, 1)
                    if qb == 2 and h >= 1:
                        v.wait_ge(pv_done, h)
                        vtt(G[:, h - 1, :], PS[:, 3072 + ((h - 1) % 2) * 512:3072 + ((h - 1) % 2) * 512 + 512], G[:, h - 1, :]).then_inc(o_read, 1)

                for n in range(N):
                    if n + 1 < N:
                        maxima(n + 1)
                    if n >= 1:
                        turned(n - 1)
                    v.wait_ge(exped, n + 1)
                    dlink(nc.vector.reciprocal(STAT[:, n % 2, 3:4], STAT[:, n % 2, 2:3]))
                    vts(PR[:, n % 2, :], PR[:, n % 2, :], STAT[:, n % 2, 3:4]).then_inc(scaled, 1)
                turned(N - 1)
                v.wait_ge(pv_done, NQ)
                dlink(vtt(G[:, NQ - 1, :], PS[:, 3072 + 512:3072 + 1024], G[:, NQ - 1, :]))

            @block.scalar
            def _(a):
                def exponentials(n):
                    a.wait_ge(negmax, n + 1)
                    if n >= 2:
                        a.wait_ge(tr1, n - 1)
                    act(PR[:, n % 2, :], PS[:, (n % 2) * 1024:(n % 2) * 1024 + TT], ACT.Exp, bias=STAT[:, n % 2, 1:2],
                        scale=SCALE, accum_out=STAT[:, n % 2, 2:3]).then_inc(exped, 1)

                def turned(n):
                    h, qb = n // NQB, n % NQB
                    a.wait_ge(tr0, n + 1)
                    if n >= 8 and qb == 0:
                        a.wait_ge(pv_done, h - 1)
                    act(PTS[:, h % 2, 0:4, qb * P:qb * P + P], PS[:, 2048:2560].rearrange("p (k t) -> p k t", k=4), ACT.Copy).then_inc(cp0, 1)

                exponentials(0)
                for n in range(N):
                    if n + 1 < N:
                        exponentials(n + 1)
                    turned(n)

        parts_scope.close()
        area_scope.close()
        parts("attnout", NQ, TX)
        with nc.Block() as block:
            @block.sync
            def _(sp):
                sp.dma_start(X.rearrange("p k t -> p (k t)"), x_dram).then_inc(loads, 16)
        split_tiles([G[:, h, :] for h in range(NQ)], TX, PSTART["attnout"] + 2)
        added = sem("added")
        with nc.Block() as block:
            @block.sync
            def _(sp):
                R.supply(sp, RINGT, weights, START["conv1"] + SLOTS)

            @block.scalar
            def _(a):
                round_block(a, PSTART["conv1"])

            @block.gpsimd
            def _(g):
                part_block(g, PSTART["conv1"])

            @block.tensor
            def _(pe):
                for m in range(DT):
                    if m >= 2:
                        pe.wait_ge(added, m - 1)
                    for half in range(2):
                        tile_product(pe, PS[:, (m % 2) * 512:(m % 2) * 512 + 512], TX, start=half == 0, stop=half == 1,
                                     area=tuple(PARTS["H"][:, e, DT * half:DT * half + DT] for e in range(2)))

            @block.vector
            def _(v):
                v.wait_ge(loads, 144)
                for m in range(DT):
                    v.wait_ge(blocks_done, PSTART["attnout"] + 2 * m + 2)
                    stt(X[:, m, 0:TX], PS[:, (m % 2) * 512:(m % 2) * 512 + 512], MODL[:, 2, 16 + m, 0:1], X[:, m, 0:TX],
                        ALU.mult, ALU.add).then_inc(added, 1)

        kept("none", 0)
        memory("conv1", True)
        conv_layer(3, 1, TX, None)

        take = carve()
        sq = take(2, TT)
        RST = take(TT)
        OUT = take(DT, TX)
        norm_stats([X[:, k, 0:TX] for k in range(DT)], TX, "ones", 1.0 / D, EPS, RST[:, 0:TX],
                   [sq[:, 0, 0:TX], sq[:, 1, 0:TX]], PS)
        out_ready, out_stored = sem("out_ready"), sem("out_stored")
        with nc.Block() as block:
            @block.vector
            def _(v):
                for k in range(DT):
                    stt(OUT[:, k, :], X[:, k, 0:TX], V("final_g_2", k), RST[:, 0:TX]).then_inc(out_ready, 1)

            @block.sync
            def _(sp):
                for k in range(DT):
                    sp.wait_ge(out_ready, k + 1)
                    sp.dma_start(outT[k * P:k * P + P, :], OUT[:, k, :]).then_inc(out_stored, 16)
                sp.wait_ge(out_stored, 16 * DT)


def pack(inputs):
    a = {k: np.asarray(v) for k, v in inputs.items()}
    zeros = np.zeros((64, 64), np.float32)

    def pairs(w):
        return [np.block([[w[2 * m], zeros], [zeros, w[2 * m + 1]]]) for m in range(4)]

    def block(name, layer, m):
        if name == "rg":
            return np.concatenate(pairs(a["rg_wa"][0]) + pairs(a["rg_wx"][0]), 1)
        if name in ("lora_w1", "lora_a1"):
            w = a[f"rwkv_{name[5:]}_2"][0]
            w = np.concatenate([w[0], w[1]], 1)
            return w.reshape(DT, P, P).transpose(1, 0, 2).reshape(P, D)
        if name in ("lora_w2", "lora_a2"):
            return a[f"rwkv_{name[5:]}_2"][0].reshape(P, D)
        if name == "w_ple_proj":
            w = a[name][0].reshape(2, P, 2, 4, P)[:, :, m]
            return w.transpose(1, 2, 0, 3).reshape(P, D)
        if name == "attn_w_out_2":
            w = a[name][0][layer * D:(layer + 1) * D]
        else:
            w = a[name][layer]
        return w[:, m * P:(m + 1) * P].reshape(DT, P, P).transpose(1, 0, 2).reshape(P, D)

    weights = np.stack([block(*b) for b in PLAN])
    vectors = np.concatenate([a[n].reshape(-1, P).T for n in VT], 1)
    out = {"xT": a["x"][0].T, "pT": a["p"][0, 0].T, "ctxT": a["ctx_2"][0].T, "vectors": vectors,
           "consts": constants(), "rope": rope_tables(), "weights": weights}
    return {k: np.ascontiguousarray(v) for k, v in out.items()}


def kernel(**inputs):
    import concourse.bacc as bacc
    from concourse.bass_utils import run_bass_kernel_spmd

    nc = bacc.Bacc("TRN2", target_bir_lowering=False, num_devices=1)
    arrays = pack(inputs)
    args = [nc.dram_tensor(f"in_{n}", a.shape, mybir.dt.from_np(a.dtype), kind="ExternalInput").ap() for n, a in arrays.items()]
    out = nc.dram_tensor("out_T", (D, TX), F32, kind="ExternalOutput").ap()
    two_blocks(nc, *args, out)
    r = run_bass_kernel_spmd(nc, [{f"in_{n}": a for n, a in arrays.items()}], core_ids=[0])
    return np.ascontiguousarray(np.asarray(r.results[0]["out_T"]).T)[None]
```
